# Optimizing a Trainium2 kernel written in Bass

```python
import jax, jax.numpy as jnp
from jax import lax
import numpy as np

D_MODEL = 1024
BATCH = 1
SEQ = 1024
DEPTH = 2
DEC_BATCH = 8
DEC_SEQ = 4
PAST_LEN = 4096
PAGE_SIZE = 128

EPS = 1e-6
POOL_GROUPS = 4
POOL_GC = 64
POOL_W = POOL_GROUPS * POOL_GC
POOL_WINDOWS = (2, 4, 8, 16)
POOL_BUF = 15
MLA_H = 8
Q_LORA = 256
KV_LORA = 128
NOPE = 64
ROPE_DIM = 32
V_DIM = 64
MLA_W = MLA_H * V_DIM
ROPE_BASE = 10000.0
MLA_SCALE = (NOPE + ROPE_DIM) ** -0.5
Q_BLOCK = 128
GLA_H = 4
GLA_DK = 32
GLA_DV = 64
GLA_W = GLA_H * GLA_DV
GATE_RANK = 16
GATE_TAU = 16.0
GLA_CHUNK = 64
IN_WIDTHS = (POOL_W, Q_LORA, KV_LORA, ROPE_DIM, GLA_H * GLA_DK, GLA_H * GLA_DK, GLA_W, GATE_RANK, GLA_W)
IN_SPLITS = tuple(int(s) for s in np.cumsum(IN_WIDTHS)[:-1])
P_IN = sum(IN_WIDTHS)
MIX_W = POOL_W + MLA_W + GLA_W
N_MEM = 256
X_H = 4
X_HD = 128
X_W = X_H * X_HD
N_GROUPS = 4
EXP_PER_GROUP = 8
N_EXPERTS = N_GROUPS * EXP_PER_GROUP
TOP_K = 2
D_EXPERT = 256
MOE_BLOCK = 128

kernel_name = 'hybrid_pool_mla_gla_hiermoe_step'

def rmsnorm(x, g):
    xf = x.astype(jnp.float32)
    y = xf * lax.rsqrt(jnp.mean(xf * xf, axis=-1, keepdims=True) + EPS)
    return (y * g.astype(jnp.float32)).astype(x.dtype)

def rope(x, pos):
    half = ROPE_DIM // 2
    inv = ROPE_BASE ** (-jnp.arange(half, dtype=jnp.float32) * 2.0 / ROPE_DIM)
    ang = pos.astype(jnp.float32)[:, None] * inv[None, :]
    shape = (1, ang.shape[0]) + (1,) * (x.ndim - 3) + (half,)
    c = jnp.cos(ang).reshape(shape)
    s = jnp.sin(ang).reshape(shape)
    xf = x.astype(jnp.float32)
    x1, x2 = xf[..., :half], xf[..., half:]
    return jnp.concatenate([x1 * c - x2 * s, x1 * s + x2 * c], axis=-1).astype(x.dtype)

def pool_mixer(u, u_prev, pos0, w_pool, pool_scale):
    B, T, _ = u.shape
    ue = jnp.concatenate([u_prev.astype(u.dtype), u], axis=1).astype(jnp.float32)
    cs = jnp.concatenate([jnp.zeros((B, 1, POOL_W), jnp.float32), jnp.cumsum(ue, axis=1)], axis=1)
    end = cs[:, POOL_BUF + 1:POOL_BUF + 1 + T]
    cnt_pos = pos0 + jnp.arange(T) + 1
    parts = []
    for g, w in enumerate(POOL_WINDOWS):
        ch = slice(g * POOL_GC, (g + 1) * POOL_GC)
        start = cs[:, POOL_BUF + 1 - w:POOL_BUF + 1 - w + T, ch]
        cnt = jnp.minimum(cnt_pos, w).astype(jnp.float32)
        parts.append((end[..., ch] - start) / cnt[None, :, None])
    pooled = jnp.concatenate(parts, axis=-1) - u.astype(jnp.float32)
    mixed = jnp.einsum('btgc,gcd->btgd', pooled.reshape(B, T, POOL_GROUPS, POOL_GC), w_pool.astype(jnp.float32))
    y = (mixed.reshape(B, T, POOL_W) * pool_scale.astype(jnp.float32)).astype(u.dtype)
    return y, ue[:, -POOL_BUF:].astype(u.dtype)

def mla_attend(q_lat, q_pe, kc, kr, q_pos, k_pos):
    B, T, H, C = q_lat.shape
    qb = Q_BLOCK if T % Q_BLOCK == 0 else T
    n = T // qb

    def block(args):
        ql, qp, pq = args
        s = (jnp.einsum('bthc,blc->bhtl', ql, kc) + jnp.einsum('bthr,blr->bhtl', qp, kr)).astype(jnp.float32) * MLA_SCALE
        s = jnp.where(k_pos[None, None, None, :] <= pq[None, None, :, None], s, -jnp.inf)
        p = jax.nn.softmax(s, axis=-1).astype(kc.dtype)
        return jnp.einsum('bhtl,blc->bthc', p, kc)

    def split(a):
        return a.reshape((B, n, qb) + a.shape[2:]).swapaxes(0, 1)

    out = lax.map(block, (split(q_lat), split(q_pe), q_pos.reshape(n, qb)))
    return out.swapaxes(0, 1).reshape(B, T, H, C)

def gla(q, k, v, log_a, s0):
    B, T, H, DK = q.shape
    DV = v.shape[-1]
    C = GLA_CHUNK if T % GLA_CHUNK == 0 else T
    n = T // C

    def chunks(a):
        return a.astype(jnp.float32).reshape(B, n, C, H, a.shape[-1]).transpose(1, 0, 3, 2, 4)

    qc = chunks(q) * (DK ** -0.5)
    kc, vc, gc = chunks(k), chunks(v), chunks(log_a)
    causal = jnp.tril(jnp.ones((C, C), dtype=bool))[None, None, :, :, None]

    def step(S, inp):
        qb, kb, vb, gb = inp
        b = jnp.cumsum(gb, axis=2)
        o_inter = jnp.einsum('bhtk,bhkv->bhtv', qb * jnp.exp(b), S)
        decay = jnp.exp(jnp.where(causal, b[:, :, :, None, :] - b[:, :, None, :, :], -jnp.inf))
        att = jnp.einsum('bhtsk,bhsk->bhts', qb[:, :, :, None, :] * decay, kb)
        o_intra = jnp.einsum('bhts,bhsv->bhtv', att, vb)
        b_last = b[:, :, -1:, :]
        S = jnp.exp(b_last[:, :, 0, :])[..., None] * S + jnp.einsum('bhsk,bhsv->bhkv', kb * jnp.exp(b_last - b), vb)
        return S, o_inter + o_intra

    S, o = lax.scan(step, s0.astype(jnp.float32), (qc, kc, vc, gc))
    return o.transpose(1, 0, 3, 2, 4).reshape(B, T, H, DV), S

def token_mixer(h, pos0, pool_prev, gla_s0, ckv_past, kpe_past, lw):
    B, T, _ = h.shape
    pos = pos0 + jnp.arange(T, dtype=jnp.int32)
    u, cq, ckv, kpe, gq, gk, gv, ga, go = jnp.split(h @ lw['w_in'], IN_SPLITS, axis=-1)
    ya, pool_new = pool_mixer(u, pool_prev, pos0, lw['w_pool'], lw['pool_scale'])
    q = (rmsnorm(cq, lw['g_qn']) @ lw['w_uq']).reshape(B, T, MLA_H, NOPE + ROPE_DIM)
    q_lat = jnp.einsum('bthn,chn->bthc', q[..., :NOPE], lw['w_uk'])
    q_pe = rope(q[..., NOPE:], pos)
    ckv = rmsnorm(ckv, lw['g_kvn'])
    kpe = rope(kpe, pos)
    if ckv_past is None:
        keys_c, keys_r, k_pos = ckv, kpe, pos
    else:
        keys_c = jnp.concatenate([ckv_past, ckv.astype(ckv_past.dtype)], axis=1)
        keys_r = jnp.concatenate([kpe_past, kpe.astype(kpe_past.dtype)], axis=1)
        k_pos = jnp.concatenate([jnp.arange(ckv_past.shape[1], dtype=jnp.int32), pos])
    o_lat = mla_attend(q_lat, q_pe, keys_c, keys_r, pos, k_pos)
    yb = jnp.einsum('bthc,chv->bthv', o_lat, lw['w_uv']).reshape(B, T, MLA_W).astype(h.dtype)
    log_a = jax.nn.log_sigmoid((ga @ lw['w_gk2'] + lw['b_gk']).astype(jnp.float32)) / GATE_TAU
    o, s_new = gla(gq.reshape(B, T, GLA_H, GLA_DK), gk.reshape(B, T, GLA_H, GLA_DK),
                   gv.reshape(B, T, GLA_H, GLA_DV), log_a.reshape(B, T, GLA_H, GLA_DK), gla_s0)
    gate = jax.nn.silu(go.astype(jnp.float32)).reshape(B, T, GLA_H, GLA_DV)
    yc = (rmsnorm(o, lw['g_gla']) * gate).reshape(B, T, GLA_W).astype(h.dtype)
    y = jnp.concatenate([ya, yb, yc], axis=-1) @ lw['w_out']
    return y, pool_new, ckv, kpe, s_new.astype(h.dtype)

def cross_attn(h, mk, mv, w_xq, w_xo):
    B, T, _ = h.shape
    q = (h @ w_xq).reshape(B, T, X_H, X_HD)
    s = jnp.einsum('bthd,bmhd->bhtm', q, mk).astype(jnp.float32) * (X_HD ** -0.5)
    p = jax.nn.softmax(s, axis=-1).astype(mv.dtype)
    o = jnp.einsum('bhtm,bmhd->bthd', p, mv).reshape(B, T, X_W)
    return (o @ w_xo).astype(h.dtype)

def hier_moe(h, w_rg, b_rg, w_re, b_re, w_eg, w_eu, w_ed):
    B, T, D = h.shape
    n = B * T
    x2 = h.reshape(n, D)
    g_logit = (x2 @ w_rg).astype(jnp.float32) + b_rg.astype(jnp.float32)
    g_sel = jnp.argmax(g_logit, axis=-1)
    g_w = jnp.take_along_axis(jax.nn.softmax(g_logit, axis=-1), g_sel[:, None], axis=1)[:, 0]
    e_logit = ((x2 @ w_re).astype(jnp.float32) + b_re.astype(jnp.float32)).reshape(n, N_GROUPS, EXP_PER_GROUP)
    e_logit = jnp.take_along_axis(e_logit, g_sel[:, None, None], axis=1)[:, 0]
    top_p, top_i = lax.top_k(jax.nn.softmax(e_logit, axis=-1), TOP_K)
    gates = g_w[:, None] * top_p / jnp.sum(top_p, axis=-1, keepdims=True)
    expert = (g_sel[:, None] * EXP_PER_GROUP + top_i).reshape(-1).astype(jnp.int32)
    s = n * TOP_K
    order = jnp.argsort(expert)
    e_sorted = expert[order]
    counts = jnp.bincount(expert, length=N_EXPERTS)
    starts = jnp.cumsum(counts) - counts
    pcounts = (counts + MOE_BLOCK - 1) // MOE_BLOCK * MOE_BLOCK
    pends = jnp.cumsum(pcounts)
    pstarts = pends - pcounts
    dest_sorted = (pstarts[e_sorted] + jnp.arange(s) - starts[e_sorted]).astype(jnp.int32)
    dest = jnp.zeros((s,), jnp.int32).at[order].set(dest_sorted)
    n_blocks = -(-s // MOE_BLOCK) + N_EXPERTS
    rows = jnp.zeros((n_blocks * MOE_BLOCK, D), h.dtype).at[dest].set(x2[jnp.arange(s) // TOP_K])
    block_e = jnp.minimum(jnp.searchsorted(pends, jnp.arange(n_blocks) * MOE_BLOCK, side='right'), N_EXPERTS - 1)

    def expert_block(args):
        xb, e = args
        hid = jax.nn.silu(xb @ w_eg[e]) * (xb @ w_eu[e])
        return hid @ w_ed[e]

    out = lax.map(expert_block, (rows.reshape(n_blocks, MOE_BLOCK, D), block_e)).reshape(-1, D)
    y_slot = out[dest].reshape(n, TOP_K, D).astype(jnp.float32)
    y = jnp.einsum('nkd,nk->nd', y_slot, gates)
    return y.astype(h.dtype).reshape(B, T, D)

def layer(x, pos0, pool_prev, gla_s0, ckv_past, kpe_past, mem_k, mem_v, lw):
    y, pool_new, ckv_new, kpe_new, s_new = token_mixer(rmsnorm(x, lw['g_mix']), pos0, pool_prev, gla_s0, ckv_past, kpe_past, lw)
    x = x + y
    x = x + cross_attn(rmsnorm(x, lw['g_x']), mem_k, mem_v, lw['w_xq'], lw['w_xo'])
    x = x + hier_moe(rmsnorm(x, lw['g_ffn']), lw['w_rg'], lw['b_rg'], lw['w_re'], lw['b_re'], lw['w_eg'], lw['w_eu'], lw['w_ed'])
    return x, pool_new, ckv_new, kpe_new, s_new

def setup_inputs(seed: int = 0) -> dict:
    key = jax.random.key(seed)
    ks = iter(jax.random.split(key, 48))

    def nrm(shape, scale=1.0):
        return jax.random.normal(next(ks), shape, jnp.float32) * scale

    def gain(shape):
        return 1.0 + 0.02 * jax.random.normal(next(ks), shape, jnp.float32)

    n_pages = PAST_LEN // PAGE_SIZE
    n_used = DEC_BATCH * n_pages
    n_phys = n_used + n_used // 4
    L = DEPTH
    return {
        'x_prompt': nrm((BATCH, SEQ, D_MODEL)),
        'x_sample': nrm((DEC_BATCH, DEC_SEQ, D_MODEL)),
        'mem_prompt': nrm((BATCH, N_MEM, D_MODEL)),
        'cache_ckv': nrm((L, n_phys, PAGE_SIZE, KV_LORA)),
        'cache_kpe': nrm((L, n_phys, PAGE_SIZE, ROPE_DIM)),
        'page_table': jax.random.permutation(next(ks), n_phys)[:n_used].reshape(DEC_BATCH, n_pages).astype(jnp.int32),
        'state_pool': nrm((L, DEC_BATCH, POOL_BUF, POOL_W), 0.5),
        'state_gla': nrm((L, DEC_BATCH, GLA_H, GLA_DK, GLA_DV), 0.5),
        'cache_mem_k': nrm((L, DEC_BATCH, N_MEM, X_H, X_HD)),
        'cache_mem_v': nrm((L, DEC_BATCH, N_MEM, X_H, X_HD)),
        'g_mix': gain((L, D_MODEL)),
        'w_in': nrm((L, D_MODEL, P_IN), D_MODEL ** -0.5),
        'w_pool': nrm((L, POOL_GROUPS, POOL_GC, POOL_GC), POOL_GC ** -0.5),
        'pool_scale': gain((L, POOL_W)),
        'g_qn': gain((L, Q_LORA)),
        'w_uq': nrm((L, Q_LORA, MLA_H * (NOPE + ROPE_DIM)), Q_LORA ** -0.5),
        'g_kvn': gain((L, KV_LORA)),
        'w_uk': nrm((L, KV_LORA, MLA_H, NOPE), KV_LORA ** -0.5),
        'w_uv': nrm((L, KV_LORA, MLA_H, V_DIM), KV_LORA ** -0.5),
        'w_gk2': nrm((L, GATE_RANK, GLA_H * GLA_DK), GATE_RANK ** -0.5),
        'b_gk': nrm((L, GLA_H * GLA_DK), 0.1),
        'g_gla': gain((L, GLA_DV)),
        'w_out': nrm((L, MIX_W, D_MODEL), MIX_W ** -0.5),
        'g_x': gain((L, D_MODEL)),
        'g_mem': gain((L, D_MODEL)),
        'w_xq': nrm((L, D_MODEL, X_W), D_MODEL ** -0.5),
        'w_xk': nrm((L, D_MODEL, X_W), D_MODEL ** -0.5),
        'w_xv': nrm((L, D_MODEL, X_W), D_MODEL ** -0.5),
        'w_xo': nrm((L, X_W, D_MODEL), X_W ** -0.5),
        'g_ffn': gain((L, D_MODEL)),
        'w_rg': nrm((L, D_MODEL, N_GROUPS), D_MODEL ** -0.5),
        'b_rg': nrm((L, N_GROUPS), 0.01),
        'w_re': nrm((L, D_MODEL, N_EXPERTS), D_MODEL ** -0.5),
        'b_re': nrm((L, N_EXPERTS), 0.01),
        'w_eg': nrm((L, N_EXPERTS, D_MODEL, D_EXPERT), D_MODEL ** -0.5),
        'w_eu': nrm((L, N_EXPERTS, D_MODEL, D_EXPERT), D_MODEL ** -0.5),
        'w_ed': nrm((L, N_EXPERTS, D_EXPERT, D_MODEL), D_EXPERT ** -0.5),
        'g_final': gain((D_MODEL,)),
    }

def reference(x_prompt, x_sample, mem_prompt, cache_ckv, cache_kpe, page_table, state_pool, state_gla,
              cache_mem_k, cache_mem_v, g_mix, w_in, w_pool, pool_scale, g_qn, w_uq, g_kvn, w_uk, w_uv,
              w_gk2, b_gk, g_gla, w_out, g_x, g_mem, w_xq, w_xk, w_xv, w_xo, g_ffn, w_rg, b_rg, w_re, b_re,
              w_eg, w_eu, w_ed, g_final):
    B = x_prompt.shape[0]
    DB = x_sample.shape[0]
    past_len = page_table.shape[1] * cache_ckv.shape[2]
    xp, xs = x_prompt, x_sample
    ckv_p, kpe_p, pool_p, gla_p, mk_p, mv_p = [], [], [], [], [], []
    ckv_s, kpe_s, pool_s, gla_s = [], [], [], []
    for l in range(DEPTH):
        lw = {'g_mix': g_mix[l], 'w_in': w_in[l], 'w_pool': w_pool[l], 'pool_scale': pool_scale[l],
              'g_qn': g_qn[l], 'w_uq': w_uq[l], 'g_kvn': g_kvn[l], 'w_uk': w_uk[l], 'w_uv': w_uv[l],
              'w_gk2': w_gk2[l], 'b_gk': b_gk[l], 'g_gla': g_gla[l], 'w_out': w_out[l],
              'g_x': g_x[l], 'w_xq': w_xq[l], 'w_xo': w_xo[l], 'g_ffn': g_ffn[l],
              'w_rg': w_rg[l], 'b_rg': b_rg[l], 'w_re': w_re[l], 'b_re': b_re[l],
              'w_eg': w_eg[l], 'w_eu': w_eu[l], 'w_ed': w_ed[l]}
        mem_n = rmsnorm(mem_prompt, g_mem[l])
        mk = (mem_n @ w_xk[l]).reshape(B, N_MEM, X_H, X_HD)
        mv = (mem_n @ w_xv[l]).reshape(B, N_MEM, X_H, X_HD)
        pool0 = jnp.zeros((B, POOL_BUF, POOL_W), xp.dtype)
        gla0 = jnp.zeros((B, GLA_H, GLA_DK, GLA_DV), jnp.float32)
        xp, pn, cn, kn, sn = layer(xp, 0, pool0, gla0, None, None, mk, mv, lw)
        ckv_p.append(cn); kpe_p.append(kn); pool_p.append(pn); gla_p.append(sn); mk_p.append(mk); mv_p.append(mv)
        ckv_past = cache_ckv[l][page_table].reshape(DB, past_len, KV_LORA)
        kpe_past = cache_kpe[l][page_table].reshape(DB, past_len, ROPE_DIM)
        xs, pn, cn, kn, sn = layer(xs, past_len, state_pool[l], state_gla[l], ckv_past, kpe_past,
                                   cache_mem_k[l], cache_mem_v[l], lw)
        ckv_s.append(cn); kpe_s.append(kn); pool_s.append(pn); gla_s.append(sn)
    y_prompt = rmsnorm(xp, g_final)
    y_sample = rmsnorm(xs, g_final)
    return (y_prompt, y_sample,
            jnp.stack(ckv_p), jnp.stack(kpe_p), jnp.stack(pool_p), jnp.stack(gla_p), jnp.stack(mk_p), jnp.stack(mv_p),
            jnp.stack(ckv_s), jnp.stack(kpe_s), jnp.stack(pool_s), jnp.stack(gla_s))


_drawn_inputs = setup_inputs


def setup_inputs(seed=0):
    import zlib

    import numpy as np

    out = dict(_drawn_inputs(seed))
    spreads = {}
    factors = {'cache_kpe': 4.471, 'g_qn': 5.203, 'g_x': 4.65, 'g_mem': 2.834, 'g_final': 2.711}
    for name, (base, spread) in spreads.items():
        noise = np.random.default_rng([zlib.crc32(name.encode()), seed]).standard_normal(out[name].shape)
        drawn = base * np.exp(spread * noise) if base else spread * noise
        out[name] = __import__('jax').numpy.asarray(drawn.astype(out[name].dtype))
    for name, factor in factors.items():
        out[name] = (out[name] * factor).astype(out[name].dtype)
    return out
```

```python
from contextlib import ExitStack

import numpy as np

import concourse.bass as bass
from concourse import mybir

F32 = mybir.dt.float32
I32 = mybir.dt.int32
U8 = mybir.dt.uint8
ALU = mybir.AluOpType
ACT = mybir.ActivationFunctionType
AX = mybir.AxisListType.X

P = 128
DEPTH, D, SEQ, DB, DT = 2, 1024, 1024, 8, 4
KT = D // P
ND = DB * DT
TOK = SEQ + ND
NCH = 3
CH = TOK // NCH
NT = SEQ // P
EPS = 1e-6
H, NOPE, ROPE, VD = 8, 64, 32, 64
QK = NOPE + ROPE
MLA_SCALE = float(QK) ** -0.5
GH, GK, GV = 4, 32, 64
GW = GH * GV
LEVELS = (64, 32, 16, 8, 4, 2, 1)
DLEVELS = (2, 1)
POOL_BUF = 15
WINDOWS = (2, 4, 8, 16)
PAGES, PAGE = 32, 128
PAST = PAGES * PAGE
KROW = 32
BLK = PAST // P
XH, XHD, NMEM = 4, 128, 256
X_SCALE = float(XHD) ** -0.5
NG, EPG, NE, DE = 4, 8, 32, 256
CAP = 128
OVER = 16
NBLK = NE + OVER
WE = KT * 2 * DE + DE // P * D
NR = NG + NE
NEG = -1e30
SCRATCH = 6640
DSPLIT = 3
NSLOT, NGR = 4, BLK // 4
NPHYS = 320
NXQ = (NT + 1) * P
LOG_SCALE = float(np.log(GK ** -0.5))

IN_MT, OUT_MT, XK_MT, XQ_MT, XO_MT = 8, 8, 4, 4, 8
RING = 4
RING_USES = IN_MT + OUT_MT + XK_MT + XQ_MT + XO_MT // 2

_c = {}
_at = 0
for _n, _w in (("ident", 128), ("ones", 128), ("causal", 128), ("below", 128), ("headmask", GH), ("bdmask", GW),
               ("newmask", DB * ND), ("rowbatch", DB), ("colbatch", DB * ND), ("pool_inv", 2), ("pool_fix", 32),
               ("iota32", 32), ("steps128", 8), ("pmod", 1), ("over", OVER)):
    _c[_n] = (_at, _w)
    _at += _w
NCONST = _at

_v = {}
_at = 0
for _n, _w in (("g_mix", 8), ("g_x", 8), ("g_ffn", 8), ("g_mem", 8), ("g_qn", 2), ("g_kvn", 1), ("b_gk", 1),
               ("pool_scale", 2), ("g_gla", 1), ("b_r", 1), ("g_final", 8)):
    _v[_n] = (_at, _w)
    _at += _w
NVEC = _at


def constants():
    c = np.zeros((P, NCONST), np.float32)

    def put(name, a):
        at, w = _c[name]
        c[:, at:at + w] = np.asarray(a, np.float32).reshape(-1, w) if np.ndim(a) == 2 else a

    i = np.arange(P)
    put("ident", np.eye(P))
    put("ones", 1.0)
    put("causal", np.where(i[None, :] <= i[:, None], 0.0, NEG))
    put("below", (i[:, None] < i[None, :]).astype(np.float32))
    put("headmask", (i[:, None] // GK == np.arange(GH)[None, :]) * np.float32(GK ** -0.5))
    put("bdmask", (i[:, None] // GK == np.arange(GW)[None, :] // GV).astype(np.float32))
    key = np.arange(P)[:, None, None]
    b = np.arange(DB)[None, :, None]
    t = (np.arange(ND) % DT)[None, None, :]
    ok = (key // DT == b) & (key % DT <= t) & (key < ND)
    put("newmask", np.where(ok, 0.0, NEG).reshape(P, -1))
    put("rowbatch", (i[:, None] // DT == np.arange(DB)[None, :]).astype(np.float32))
    col = (np.arange(ND)[None, :] // DT == np.arange(DB)[:, None]).astype(np.float32)
    put("colbatch", np.broadcast_to(col.reshape(1, -1), (P, DB * ND)))
    w = np.array([[WINDOWS[2 * k + p // 64] for k in range(2)] for p in range(P)], np.float32)
    put("pool_inv", 1.0 / w)
    n = np.arange(1, 17, dtype=np.float32)[None, None, :]
    put("pool_fix", (w[:, :, None] / np.minimum(n, w[:, :, None])).reshape(P, -1))
    put("iota32", np.broadcast_to(np.arange(NE)[None, :] - NE, (P, NE)))
    put("steps128", np.broadcast_to(128.0 * np.arange(1, 9)[None, :], (P, 8)))
    put("pmod", (i % (P // PAGES))[:, None])
    put("over", np.broadcast_to(np.arange(OVER)[None, :], (P, OVER)))
    pos = np.concatenate([np.arange(SEQ), PAST + np.arange(ND) % DT]).astype(np.float32)
    half = ROPE // 2
    inv = np.float32(10000.0) ** (-np.arange(half, dtype=np.float32) * np.float32(2.0) / np.float32(ROPE))
    ang = (pos[None, :] * inv[:, None].astype(np.float32)).astype(np.float32)
    cos, sin = np.cos(ang), np.sin(ang)
    rope = np.stack([np.concatenate([cos, cos]), np.concatenate([-sin, sin])], 1).astype(np.float32)
    s, t = np.arange(P)[:, None], np.arange(P)[None, :]
    masks = [((s // (2 * z) == t // (2 * z)) & (s % (2 * z) < z) & (t % (2 * z) >= z)) for z in LEVELS]
    return c, rope, np.stack(masks, 1).astype(np.float32)


def build(nc, ins, outs):
    with ExitStack() as ctx:
        def sb(name, shape, dt=F32):
            return ctx.enter_context(nc.sbuf_tensor(name, shape, dt))

        sems = []

        def sem(name):
            s = ctx.enter_context(nc.semaphore(name))
            sems.append(s)
            return s

        x = sb("x", [P, KT, TOK])
        ring = sb("ring", [P, RING, KT, P])
        consts = sb("consts", [P, NCONST])
        rope = sb("rope", [P, 2, TOK])
        lmask = sb("lmask", [P, len(LEVELS), P], U8)
        vec = sb("vec", [P, NVEC])
        W = KT * TOK
        pages, page_i, page_f = sb("pages", [P, DB], I32), sb("page_i", [P, DB], I32), sb("page_f", [P, DB])
        nmax = sb("nmax", [P, 2, 2])
        gates, dest = sb("gates", [P, 2, NT + 1]), sb("dest", [P, 2, NT + 1], I32)
        over_i = sb("over_i", [P, 1 + OVER], I32)
        slots = nc.dram_tensor("slots", [NBLK * CAP, D], F32).ap()
        arena = sb("arena", [P, 3 * W + (NT + 1) * 512 + SCRATCH])
        ps = ctx.enter_context(nc.psum_tensor("ps", [P, 8, 512], F32))

        def view(at, *shape):
            n = int(np.prod(shape))
            v = arena[:, at:at + n]
            names = [f"a{k}" for k in range(len(shape))]
            if len(shape) == 1:
                return v
            return v.rearrange(f"p ({' '.join(names)}) -> p {' '.join(names)}",
                               **{n_: s for n_, s in zip(names[1:], shape[1:])})

        MIX, XN, PR, VG = 0, W, 2 * W, 3 * W
        SC = 3 * W + (NT + 1) * 512

        def con(name, rows=P):
            at, w = _c[name]
            return consts[0:rows, at:at + w]

        def gain(name, k=0, rows=P):
            at, _ = _v[name]
            return vec[0:rows, at + k:at + k + 1]

        ident, ones = con("ident"), con("ones")
        mix = view(MIX, KT, TOK)
        rstd = view(MIX + 6 * TOK, 2, TOK)
        recip = rope[0:64, 0, 0:512]
        xn = view(XN, KT, TOK)
        lmask_f = view(XN, len(LEVELS), P)
        sq = view(PR, KT, TOK)
        pr = view(PR, KT, TOK)
        vg = view(VG, NT + 1, 512)
        wvg = view(SC, KT, 512)
        sq2 = view(XN, 3, TOK)
        psum_a, psum_b = view(XN + 3 * TOK, 2, TOK), view(XN + 5 * TOK, 2, TOK)
        dbuf = view(XN + 7 * TOK, 2, DB, POOL_BUF + DT)
        dsum = view(XN + 7 * TOK + 304, 2, 2, DB, POOL_BUF + DT)
        wpool = view(SC, 2, P)
        wgk = view(SC + 256, P)
        q_h = view(XN, 2, TOK)
        k_h = view(XN + 2 * TOK, 2, TOK)
        v_h = view(XN + 4 * TOK, 2, NT, P)
        prob = view(XN + 4 * TOK + 2048, 2, SEQ)
        q_dec = view(SC, DB, 224)
        qpe_dec = view(SC + 1792, DB, 4, ND)
        qpe_new = view(SC + 2816, DB, ND)
        S2 = SC + 3072
        qswap = view(S2, TOK)
        pt = view(S2 + TOK, 2, 512)
        w_h = view(S2 + TOK + 1024, 2, 384)
        kswap = view(S2, TOK)
        vv = [view(PR, 4, 512), view(MIX + 6 * TOK, 4, 512)]
        wuv = view(S2 + TOK + 1024 + 768, 512)
        keep = S2 + TOK + 1024 + 768 + 512
        ckv_new, kr_new, ckv_tok = view(keep, ND), view(keep + 32, ND), view(keep + 64, P)
        u_out = view(MIX + 2 * TOK + (NT + 1) * GW, 2, GW)
        kr = view(MIX + 5 * TOK, TOK)
        silu = view(MIX + 2 * TOK, NT + 1, GW)
        la = pr[:, 5, :]
        la_t = view(XN, TOK)

        NL = len(LEVELS) + 1
        g_q = view(XN, 2, NL - 1, GH, P)
        g_k = [view(XN + 2 * (NL - 1) * GH * P, NL, P), view(PR, NL, P)]
        state = view(XN + 8192, GW)
        g_q0 = view(PR + 1024, 2, GH, P)
        g_att = view(PR + 2 * TOK, 2, GH, P)
        g_e = view(PR + 2 * TOK + 1024, NL, P)
        g_b = view(S2, 2, P)
        g_eb, g_ek = view(S2 + 256, P), view(S2 + 384, P)
        g_qe, g_kt, g_ktt = view(S2 + 512, 2, P), view(S2 + 768, 2, P), view(S2 + 1024, 2, P)
        g_o, g_sq, g_tmp = view(S2 + 1280, 2, GW), view(S2 + 1792, GW), view(S2 + 2048, GW)
        g_last, g_ms = view(S2 + 2304, 2, DB), view(S2 + 2320, 2, GH)
        d_state, d_qe, d_kt = view(XN + 3584, DB, GW), view(XN + 5632, DB, ND), view(XN + 5888, DB, P)

        ck = [view(XN + j * 5120, BLK, P) for j in range(NSLOT)]
        kr_c = [view(XN + j * 5120 + 4096, BLK, ROPE) for j in range(NSLOT)]
        ct, k4 = view(S2, 2, 512), view(S2 + 1024, 2, P)
        pd = view(S2 + 1280, BLK, ND)
        mx, diag, mb, sm, p_new = (view(S2 + 2304 + 32 * k, ND) for k in range(5))
        small, d_o, o_lat = nmax[:, 0, :], view(S2 + 2464, P), view(S2 + 2592, H, DB, DT)
        mem, mem_n, mem_sq = view(VG, KT, NMEM), view(VG + 2048, KT, NMEM), view(SC + 4096, KT, NMEM)
        wxv = view(SC, KT, 512)
        xq, mk = view(MIX, XH, NXQ), view(MIX + XH * NXQ, XH, NMEM)
        mem_r, mv = view(MIX + 5632, NMEM), view(MIX + 7 * TOK, 2, 512)
        qt, xon = view(XN, 2, XH, P), view(XN + 1024, 2, XH, XHD)
        kd, vd = view(XN + 2048, 2, XH, NMEM), view(XN + 4096, 2, 2, 512)
        d_qm = view(XN + 6144, XH, DB, ND)
        co = view(PR, XH, TOK)
        px, pxt = view(PR + 4 * TOK, 2, XH, NMEM), view(PR + 4 * TOK + 2048, 2, 2, 512)
        d_pt = view(VG, 2 * XH, DB, ND)
        xm = view(SC, 2, 16)

        w_r = view(SC, KT, NR)
        lgt = view(SC + 288, NXQ)
        R = SC + 288 + NXQ
        lg = view(R, NT + 1, NR)
        e_all, oh1, oh2, both, r_tmp, rank = (view(R + 324 + 288 * k, NT + 1, NE) for k in range(6))
        cum = view(R + 2052, NT + 2, NE)
        r_exp, g_oh = view(R + 2372, NT + 1, NG + 1), view(R + 2420, NT + 1, NG)
        gm, r_min, m1, m2, g_w = (view(R + 2456 + 9 * k, NT + 1) for k in range(5))
        nov, oend, base, jump = (view(R + 2504 + 32 * k, NE) for k in range(4))
        steps8, over_f = view(R + 2632, NE, 8), view(R + 2632, OVER, NE)
        r_f, over_c = view(R + 3144, 2, NT + 1), view(R + 3162, 1 + OVER)
        xr = view(VG, 4, D)
        w_e = [view(j * WE, WE) for j in range(4)]
        xb, xb_t, y_sb = view(VG, 2, D), view(VG + 2 * D, 2, KT, P), view(VG + 4 * D, 2, D)
        h_e, h_b, h_t = view(VG + 6 * D, DE), view(VG + 6 * D + DE, DE), view(VG + 6 * D + 2 * DE, 2, 2, P)
        zeros = view(S2 + TOK + 1024, 512)
        yg, comb = view(MIX, 4, 2, D), view(XN, 2, D)
        assert R + 3200 <= SC + SCRATCH and 4 * WE <= VG

        slots_clear = ctx.enter_context(nc.semaphore("slots_clear"))
        next_layer = ctx.enter_context(nc.semaphore("next_layer"))
        setup = ctx.enter_context(nc.semaphore("setup"))
        y_stored = ctx.enter_context(nc.semaphore("y_stored"))
        layer_done = sem("layer_done")
        stage_done = sem("stage_done")
        std_ready, lat_std, turn = sem("std_ready"), sem("lat_std"), sem("turn")
        ring_full = [sem(f"ring_full{j}") for j in range(RING)]
        vec_full = sem("vec_full")
        sq_ready, ssq_ready, norm_ready = sem("sq_ready"), sem("ssq_ready"), sem("norm_ready")
        lin_done, lin_evac = sem("lin_done"), sem("lin_evac")
        act_step, dve_step, pool_step = sem("act_step"), sem("dve_step"), sem("pool_step")
        wvg_full, vg_done, vg_evac = sem("wvg_full"), sem("vg_done"), sem("vg_evac")
        lat_sq, lat_ssq, lat_norm = sem("lat_sq"), sem("lat_ssq"), sem("lat_norm")
        pre_full, kswap_full, kr_ready = sem("pre_full"), sem("kswap_full"), sem("kr_ready")
        z_done, z_evac, gate_e = sem("z_done"), sem("z_evac"), sem("gate_e")
        zeroed = sem("zeroed")
        pooled, pool_mm = sem("pooled"), sem("pool_mm")
        vv_done, vv_evac, wuv_full = sem("vv_done"), sem("vv_evac"), sem("wuv_full")
        utr_done, utr_evac, states_stored = sem("utr_done"), sem("utr_evac"), sem("states_stored")
        w_full = [sem(f"w_full{j}") for j in range(2)]
        s_done, nmax_ready, p_ready = sem("s_done"), sem("nmax_ready"), sem("p_ready")
        tp_done = sem("tp_done")
        tp_free = [sem(f"tp_free{j}") for j in range(2)]
        qswap_full, q_rope, v_ready = sem("qswap_full"), sem("q_rope"), sem("v_ready")
        y_done, y_free = sem("y_done"), sem("y_free")

        g_sub, g_exp, g_pool, g_dve = sem("g_sub"), sem("g_exp"), sem("g_pool"), sem("g_dve")
        at_done, at_free, g_spread = sem("at_done"), sem("at_free"), sem("g_spread")
        kt_done, kt_evac, st_done, st_ready = sem("kt_done"), sem("kt_evac"), sem("st_done"), sem("st_ready")
        o_done, o_evac, o_sum, o_root, o_norm = sem("o_done"), sem("o_evac"), sem("o_sum"), sem("o_root"), sem("o_norm")
        ot_done, ot_evac, ds_full = sem("ot_done"), sem("ot_evac"), sem("ds_full")
        ds_clear, dkt_ready = sem("ds_clear"), sem("dkt_ready")
        tok_done, tok_evac = sem("tok_done"), sem("tok_evac")
        ct_done, ct_evac, k4_done, k4_evac = sem("ct_done"), sem("ct_evac"), sem("k4_done"), sem("k4_evac")
        sc_done, shifted, pd_ready = sem("sc_done"), sem("shifted"), sem("pd_ready")
        tail_pe, tail_dve = sem("tail_pe"), sem("tail_dve")
        ck_full = [sem(f"ck_full{j}") for j in range(NSLOT)]
        mem_full, wxv_full, msq_ready, mssq_ready = sem("mem_full"), sem("wxv_full"), sem("msq_ready"), sem("mssq_ready")
        mstd_ready, mnorm_ready, mv_done, mv_evac = sem("mstd_ready"), sem("mnorm_ready"), sem("mv_done"), sem("mv_evac")
        qt_ready = sem("qt_ready")
        xs_done, xm_ready, xp_ready = sem("xs_done"), sem("xm_ready"), sem("xp_ready")
        xt_done, xt_evac, xv_done = sem("xt_done"), sem("xt_evac"), sem("xv_done")
        xon_ready, xot_done, xot_evac = sem("xon_ready"), sem("xot_done"), sem("xot_evac")
        dt_done, dpt_ready = sem("dt_done"), sem("dpt_ready")
        kd_full, vd_full = [sem(f"kd_full{j}") for j in range(2)], [sem(f"vd_full{j}") for j in range(2)]
        kd_used, vd_used = sem("kd_used"), sem("vd_used")
        wr_full, lg_done, lg_evac, lt_done = sem("wr_full"), sem("lg_done"), sem("lg_evac"), sem("lt_done")
        rx_in, rx_out = sem("rx_in"), sem("rx_out")
        both_ready, ranked, routed = sem("both_ready"), sem("ranked"), sem("routed")
        xr_done, xr_evac, rows_ready = sem("xr_done"), sem("xr_evac"), sem("rows_ready")
        row_moved = [sem(f"row_moved{j}") for j in range(4)]
        we_full, xb_full, y_sent = [sem(f"we_full{j}") for j in range(4)], [sem(f"xb_full{j}") for j in range(2)], [sem(f"y_sent{j}") for j in range(2)]
        tx_done, tx_evac, gu_done, ge_ready, h_ready = sem("tx_done"), sem("tx_evac"), sem("gu_done"), sem("ge_ready"), sem("h_ready")
        ht_done, ht_evac, dn_done, dn_evac = sem("ht_done"), sem("ht_evac"), sem("dn_done"), sem("dn_evac")
        c_half, c_ready = sem("c_half"), sem("c_ready")
        c_done, c_added = sem("c_done"), sem("c_added")
        assert keep + 192 <= SC + SCRATCH

        class Steps:

            def __init__(self, eng, s):
                self.eng, self.sem, self.n = eng, s, 0

            def mark(self, ins):
                self.n += 1
                return ins.then_inc(self.sem, 1)

            def sync(self):
                self.eng.wait_ge(self.sem, self.n)

            def __call__(self, ins):
                self.mark(ins)
                self.sync()

            def restart(self):
                self.eng.sem_clear(self.sem)
                self.n = 0

        def stage_end(eng, n):
            eng.drain().then_inc(stage_done, 1)
            eng.wait_ge(stage_done, 4 * n)

        def end_layer(eng, l, clears=False):
            eng.drain().then_inc(layer_done, 1)
            if clears:
                eng.wait_ge(layer_done, 5)
                nums = sorted(s.num for s in sems)
                eng.dma_reset(range(nums[0], nums[-1] + 1))
                eng.sem_clear(range(nums[0], nums[-1] + 1))
                eng.drain().then_inc(next_layer, 1)
            eng.wait_ge(next_layer, l + 1)

        chunks = [(c, slice(c * CH, (c + 1) * CH)) for c in range(NCH)]

        block = ctx.enter_context(nc.Block())

        @block.sync
        def _(sp):
            sp.dma_start(consts[:, :], ins["consts"]).then_inc(setup, 16)
            sp.dma_start(rope[64:96, :, :], ins["rope"]).then_inc(setup, 16)
            sp.dma_start(lmask_f, ins["lmask"]).then_inc(setup, 16)
            sp.dma_start(x[:, :, :], ins["x"]).then_inc(setup, 16)
            sp.dma_start(pages[:, :], ins["pages"]).then_inc(setup, 16)
            with sp.Fori(0, DEPTH) as l:
                def ring_load(u, j):
                    sp.dma_start(ring[:, j, :, :], ins["ring"][bass.ds(l, 1), bass.ds(u, 1)]
                                 .rearrange("a b p k m -> p (a b k) m")).then_inc(ring_full[j], 16)

                sp.dma_start(vec[:, :], ins["vec"][bass.ds(l, 1)].rearrange("a p n -> p (a n)")).then_inc(vec_full, 16)
                for j in range(RING):
                    ring_load(j, j)
                sp.dma_start(wvg, ins["wvg"][bass.ds(l, 1)].rearrange("a p k m -> p (a k) m")).then_inc(wvg_full, 16)
                for j in range(RING):
                    sp.wait_ge(lin_done, j + 1)
                    ring_load(RING + j, j)
                for j in range(RING):
                    sp.wait_ge(lin_done, RING + j + 1)
                    ring_load(2 * RING + j, j)
                sp.wait_ge(vg_done, NT + 1)
                sp.dma_start(wpool, ins["wpool"][bass.ds(l, 1)].rearrange("a p k m -> p (a k) m")).then_inc(pre_full, 16)
                sp.dma_start(wgk[0:16, :], ins["wgk"][bass.ds(l, 1)].rearrange("a p n -> p (a n)")).then_inc(pre_full, 16)
                sp.dma_start(dbuf[:, :, :, 0:POOL_BUF], ins["pool_prev"][bass.ds(l, 1)]
                             .rearrange("a p k b t -> p (a k) b t")).then_inc(pre_full, 16)
                sp.dma_start(wuv, ins["wuv"][bass.ds(l, 1)].rearrange("a p n -> p (a n)")).then_inc(wuv_full, 16)
                half = ROPE // 2
                sp.dma_start(kswap[64:64 + half, :], pr[64 + half:96, 5, :]).then_inc(kswap_full, 16)
                sp.dma_start(kswap[64 + half:96, :], pr[64:64 + half, 5, :]).then_inc(kswap_full, 16)
                sp.wait_ge(stage_done, 4)
                sp.wait_ge(slots_clear, 16)
                for p in range(2):
                    sp.dma_start(w_h[:, p, :], ins["w_h"][bass.ds(l, 1), p].rearrange("a p n -> p (a n)")).then_inc(w_full[p], 16)
                for i, _ in [(0, 0)]:
                    sp.wait_ge(tp_free[0], 2)
                    sp.wait_ge(tp_free[1], 1)
                    sp.dma_start(qswap[64:64 + half, :], q_h[64 + half:96, 0, :]).then_inc(qswap_full, 16)
                    sp.dma_start(qswap[64 + half:96, :], q_h[64:64 + half, 0, :]).then_inc(qswap_full, 16)
                with sp.Fori(0, H // 2) as i:
                    for p in range(2):
                        sp.wait_ge(tp_free[1], 18 * i + 9 * p + 6)
                        sp.wait_ge(q_rope, 2 * i + p + 1)
                        sp.dma_start(qswap[64:64 + half, :], q_h[64 + half:96, 1 - p, :]).then_inc(qswap_full, 16)
                        sp.dma_start(qswap[64 + half:96, :], q_h[64:64 + half, 1 - p, :]).then_inc(qswap_full, 16)
                        sp.wait_ge(tp_done, 36 * i + 18 * p + 6)
                        sp.sem_inc(turn, 1)
                        sp.dma_start(w_h[:, p, :], ins["w_h"][bass.ds(l, 1), bass.ds(2 * i + p + 2, 1)]
                                     .rearrange("a b p n -> p (a b n)")).then_inc(w_full[p], 16)
                sp.wait_ge(w_full[0], 16 * (H // 2 + 1))
                sp.wait_ge(w_full[1], 16 * (H // 2 + 1))
                sp.wait_ge(stage_done, 8)
                sp.wait_ge(ds_clear, 1)
                for h in range(GH):
                    sp.dma_start(d_state[GK * h:GK * (h + 1), :, GV * h:GV * (h + 1)],
                                 ins["state_gla"][bass.ds(l, 1), :, h].rearrange("a b k v -> (a k) b v")).then_inc(ds_full, 16)
                sp.wait_ge(stage_done, 12)

                sp.wait_ge(stage_done, 16)
                sp.dma_start(mem, ins["mem"]).then_inc(mem_full, 16)
                sp.dma_start(wxv, ins["wxv"][bass.ds(l, 1)].rearrange("a p k m -> p (a k) m")).then_inc(wxv_full, 16)
                for u in range(12, RING_USES):
                    sp.wait_ge(lin_done, u - RING + 1)
                    ring_load(u, u % RING)
                    if u == 23:
                        sp.wait_ge(stage_done, 24)
                        for b in range(DB):
                            if b >= 2:
                                sp.wait_ge(kd_used, b - 1)
                            sp.dma_start(kd[:, b % 2], ins["mem_k"][bass.ds(l, 1), b].rearrange("a p h m -> p (a h) m")).then_inc(kd_full[b % 2], 16)
                            if b < 2:
                                sp.dma_start(vd[:, b], ins["mem_v"][bass.ds(l, 1), b].rearrange("a (f m) h c -> m (a f) (h c)", f=2)).then_inc(vd_full[b], 16)
                        for b in range(2, DB):
                            sp.wait_ge(vd_used, b - 1)
                            sp.dma_start(vd[:, b % 2], ins["mem_v"][bass.ds(l, 1), b].rearrange("a (f m) h c -> m (a f) (h c)", f=2)).then_inc(vd_full[b % 2], 16)
                sp.wait_ge(stage_done, 32)
                def load_w(j, e):
                    sp.dma_start(w_e[j], ins["w_e"][bass.ds(l, 1), bass.ds(e, 1)].rearrange("a b p n -> p (a b n)")).then_inc(we_full[j], 16)

                def load_x(p, n):
                    sp.dma_start(xb[:, p, :], slots[bass.ds(CAP * n, CAP), :]).then_inc(xb_full[p], 16)

                sp.dma_start(w_r, ins["w_r"][bass.ds(l, 1)].rearrange("a p k n -> p (a k) n")).then_inc(wr_full, 16)
                load_w(0, 0)
                sp.wait_ge(ssq_ready, 3 * NCH)
                load_w(3, 3)
                sp.wait_ge(xr_done, NT + 1)
                load_w(1, 1)
                load_w(2, 2)
                sp.wait_ge(rows_ready, 1)
                load_x(0, 0)
                load_x(1, 1)
                with sp.Fori(0, NE // 4 - 1) as i:
                    for j in range(4):
                        n = 4 * i + j
                        sp.wait_ge(tx_done, n + 1)
                        sp.sem_inc(turn, 1)
                        load_x(j % 2, n + 2)
                        sp.wait_ge(dn_done, n + 1)
                        sp.sem_inc(turn, 1)
                        load_w(j, n + 4)
                for n in (NE - 4, NE - 3):
                    sp.wait_ge(tx_done, n + 1)
                    load_x(n % 2, n + 2)
                n_over = sp.value_load(over_i[0:1, 0:1], min_val=0, max_val=OVER)
                with sp.Fori(0, OVER // 4) as i:
                    for j in range(4):
                        o = 4 * i + j
                        with sp.If(n_over > o):
                            sp.wait_ge(dn_done, NE + o)
                            sp.sem_inc(turn, 1)
                            load_x(j % 2, NE + o)
                            e = sp.value_load(over_i[0:1, bass.ds(o + 1, 1)], min_val=0, max_val=NE - 1)
                            load_w(j, e)
                sp.wait_ge(stage_done, 44)
                end_layer(sp, l)
                sp.sem_inc(turn, 1)
            sp.wait_ge(norm_ready, NCH)
            sp.dma_start(outs["y"], xn).then_inc(y_stored, 16)
            sp.wait_ge(y_stored, 16)

        @block.tensor
        def _(pe):
            pe.wait_ge(setup, 80)
            with pe.Fori(0, DEPTH) as l:
                def sum_squares(src, n, tiles, count, base, ready, done, width=CH):
                    for c in range(count):
                        pe.wait_ge(ready, n + c + 1)
                        for k in range(tiles):
                            mm = pe.matmul(ps[:, base + c, 0:width], ones, src(k, c), start=k == 0, stop=k == tiles - 1)
                        mm.then_inc(done, 1)

                def linear(groups, first, use, src, units=8, per=1):
                    def body(i):
                        for j in range(RING * per):
                            slot = j // per
                            n = first + RING * per * i + j
                            if j % per == 0:
                                pe.wait_ge(ring_full[slot], (use + i + 1) * 16)
                            pe.wait_ge(lin_evac, n + 1)
                            for c, tok in chunks:
                                for k in range(units):
                                    mm = pe.matmul(ps[:, (j % 2) * NCH + c, 0:CH], ring[:, slot, (j % per) * units + k, :],
                                                   src[:, k, tok], start=k == 0, stop=k == units - 1)
                            mm.then_inc(lin_done, 1)
                    if groups == 1:
                        body(0)
                    else:
                        with pe.Fori(0, groups) as i:
                            body(i)

                sum_squares(lambda k, c: sq[:, k, chunks[c][1]], 0, KT, NCH, 0, sq_ready, ssq_ready)
                pe.wait_ge(norm_ready, NCH)
                pe.wait_ge(ssq_ready, NCH)
                linear(2, 0, 0, xn)
                pe.wait_ge(wvg_full, 16)
                for t in range(NT + 1):
                    m = P if t < NT else ND
                    if t >= 2:
                        pe.wait_ge(vg_evac, t - 1)
                    for k in range(KT):
                        mm = pe.matmul(ps[0:m, 6 + t % 2, :], xn[:, k, t * P:t * P + m], wvg[:, k, :],
                                       start=k == 0, stop=k == KT - 1)
                    mm.then_inc(vg_done, 1)
                pe.wait_ge(lin_evac, IN_MT + 2)
                pe.wait_ge(vg_evac, NT + 1)
                for k in range(2):
                    pe.transpose(ps[0:POOL_BUF, 6, k * P:(k + 1) * P], pr[:, k, SEQ - POOL_BUF:SEQ], ident)
                for k in range(2):
                    mm = pe.transpose(ps[0:ND, 7, k * P:(k + 1) * P], pr[:, k, SEQ:TOK], ident)
                mm.then_inc(utr_done, 1)
                pe.wait_ge(lat_sq, 1)
                for c, tok in chunks:
                    for k in range(2):
                        pe.matmul(ps[:, c, 0:CH], ones, sq2[:, k, tok], start=k == 0, stop=k == 1)
                for c, tok in chunks:
                    mm = pe.matmul(ps[:, NCH + c, 0:CH], ones, sq2[:, 2, tok], start=True, stop=True)
                mm.then_inc(lat_ssq, 1)
                pe.wait_ge(pre_full, 48)
                pe.wait_ge(lat_norm, 1)
                for c, tok in chunks:
                    mm = pe.matmul(ps[:, c, 0:CH], wgk[0:16, :], pr[0:16, 5, tok], start=True, stop=True)
                mm.then_inc(z_done, 1)
                pe.wait_ge(z_evac, 1)
                pe.wait_ge(lat_norm, 2)
                pe.wait_ge(pooled, 1)
                for k in range(2):
                    for c, tok in chunks:
                        mm = pe.matmul(ps[:, k * NCH + c, 0:CH], wpool[:, k, :], psum_a[:, k, tok], start=True, stop=True)
                mm.then_inc(pool_mm, 1)
                pe.wait_ge(wuv_full, 16)
                pe.wait_ge(pool_mm, 1)
                pe.wait_ge(utr_evac, 1)
                for t in range(NT):
                    if t >= 2:
                        pe.wait_ge(vv_evac, t - 1)
                    pe.matmul(ps[:, 6 + t % 2, :], pr[:, 4, t * P:(t + 1) * P], wuv, start=True, stop=True).then_inc(vv_done, 1)

                stage_end(pe, 1)

                def proj(p, piece, n):
                    bank = 4 + piece % 2
                    if piece in (0, 1, 2):
                        tok = (slice(0, 512), slice(512, 1024), slice(SEQ, TOK))[piece]
                        w = tok.stop - tok.start
                        for k in range(2):
                            mm = pe.matmul(ps[0:QK, bank, 0:w], w_h[:, p, k * QK:(k + 1) * QK], pr[:, 2 + k, tok],
                                           start=k == 0, stop=k == 1)
                    elif piece in (3, 4):
                        tok = (slice(0, 512), slice(512, 1024))[piece - 3]
                        mm = pe.matmul(ps[0:NOPE, bank, :], w_h[:, p, 192:256], pr[:, 4, tok], start=True, stop=True)
                    else:
                        mm = pe.matmul(ps[:, bank, 0:ND], w_h[0:NOPE, p, 256:384], q_h[0:NOPE, p, SEQ:TOK],
                                       start=True, stop=True)
                    mm.then_inc(tp_done, 1)
                    return mm

                def scores(p, qb, s, n_s):
                    w = (qb + 1) * P
                    lhs = q_h[0:QK, p, qb * P:(qb + 1) * P]
                    for at in range(0, w, 512):
                        e = min(at + 512, w)
                        last = e == w
                        mm = pe.matmul(ps[:, 2 * s + at // 512, 0:e - at], lhs, k_h[0:QK, p, at:e], start=True, stop=not last)
                    at = (qb * P) % 512
                    pe.matmul(ps[:, 2 * s + qb // 4, at:at + P], ident, con("causal"), start=False, stop=True).then_inc(s_done, 1)

                for k in range(6):
                    if k == 0:
                        pe.wait_ge(w_full[0], 16)
                    if k >= 2:
                        pe.wait_ge(tp_free[k % 2], k // 2)
                    if k == 5:
                        pe.wait_ge(tp_free[0], 2)
                    proj(0, k, 0)
                pe.wait_ge(tp_free[0], 3)
                pe.wait_ge(tp_free[1], 3)
                pe.wait_ge(q_rope, 1)
                scores(0, 0, 0, 0)
                scores(0, 1, 1, 1)
                with pe.Fori(0, H // 2) as i:
                    for p in range(2):
                        n9 = 18 * i + 9 * p + 3
                        item = 16 * i + 8 * p
                        m = 0

                        def transposes(qb):
                            nonlocal m
                            pe.wait_ge(p_ready, item + qb + 1)
                            used = []
                            for at in range(0, qb + 1, 4):
                                pe.wait_ge(tp_free[m % 2], n9 + m // 2)
                                for kb in range(at, min(at + 4, qb + 1)):
                                    mm = pe.transpose(ps[:, 4 + m % 2, (kb - at) * P:(kb - at + 1) * P],
                                                      prob[:, qb % 2, kb * P:(kb + 1) * P], ident)
                                mm.then_inc(tp_done, 1)
                                used.append(m)
                                m += 1
                            return used

                        def values(qb, used):
                            for g, s in enumerate(used):
                                pe.wait_ge(tp_free[s % 2], n9 + s // 2 + 1)
                                for kb in range(4 * g, min(4 * g + 4, qb + 1)):
                                    if qb % 4 == 0 and kb == 0:
                                        pe.wait_ge(y_free, 4 * i + 2 * p + qb // 4 + 1)
                                    mm = pe.matmul(ps[:, 6 + qb // 4, (qb % 4) * P:(qb % 4 + 1) * P], v_h[:, p, kb, :],
                                                   pt[:, s % 2, (kb - 4 * g) * P:(kb - 4 * g + 1) * P],
                                                   start=kb == 0, stop=kb == qb)
                            if qb % 4 == 3:
                                mm.then_inc(y_done, 1)

                        def piece(k):
                            nonlocal m
                            if k == 0:
                                pe.wait_ge(w_full[1 - p], 16 * (i + 1) if p == 0 else 16 * (i + 2))
                            pe.wait_ge(tp_free[m % 2], n9 + m // 2)
                            proj2(1 - p, k, m % 2)
                            m += 1

                        def proj2(q, k, b):
                            bank = 4 + b
                            if k < 3:
                                tok = (slice(0, 512), slice(512, 1024), slice(SEQ, TOK))[k]
                                for kk in range(2):
                                    mm = pe.matmul(ps[0:QK, bank, 0:tok.stop - tok.start], w_h[:, q, kk * QK:(kk + 1) * QK],
                                                   pr[:, 2 + kk, tok], start=kk == 0, stop=kk == 1)
                            elif k < 5:
                                tok = (slice(0, 512), slice(512, 1024))[k - 3]
                                mm = pe.matmul(ps[0:NOPE, bank, :], w_h[:, q, 192:256], pr[:, 4, tok], start=True, stop=True)
                            else:
                                mm = pe.matmul(ps[:, bank, 0:ND], w_h[0:NOPE, q, 256:384], q_h[0:NOPE, q, SEQ:TOK],
                                               start=True, stop=True)
                            mm.then_inc(tp_done, 1)

                        pe.wait_ge(v_ready, 2 * i + p + 1)
                        for qb in range(NT):
                            used = transposes(qb)
                            nxt = qb + 2
                            if nxt == NT:
                                pe.wait_ge(q_rope, 2 * i + p + 2)
                                pe.wait_ge(tp_free[0], n9 + 6)
                                pe.wait_ge(tp_free[1], n9 + 7)
                            scores(p if nxt < NT else 1 - p, nxt % NT, nxt % 2, 0)
                            if qb < 6:
                                piece(qb)
                            values(qb, used)
                stage_end(pe, 2)

                def levels(i, p, first, w, idx):
                    for j, lv in enumerate(idx):
                        pe.wait_ge(at_free, first + j + 1)
                        q = g_q0[:, p, :, 0:w] if lv == NL - 1 else g_q[:, p, lv, :, 0:w]
                        pe.matmul(ps[0:w, j % 4, 0:GH * w].rearrange("p (h t) -> p h t", h=GH), g_k[p][:, lv, 0:w], q,
                                  start=True, stop=True).then_inc(at_done, 1)

                order = [NL - 1] + list(range(NL - 1))

                def tile(i, p):
                    n = 2 * i + p
                    pe.wait_ge(g_dve, n + 1)
                    pe.wait_ge(g_pool, n + 1)
                    levels(i, p, 16 * i + 8 * p, P, order)
                    pe.wait_ge(o_norm, n + 1)
                    pe.wait_ge(ot_evac, n + 1)
                    for k in range(2):
                        mm = pe.transpose(ps[:, 6, k * P:(k + 1) * P], g_o[:, 1 - p, k * P:(k + 1) * P], ident)
                    mm.then_inc(ot_done, 1)
                    pe.wait_ge(st_ready, n + 1)
                    pe.transpose(ps[:, 7, 0:P], g_kt[:, p, :], ident).then_inc(kt_done, 1)
                    pe.wait_ge(o_evac, n + 1)
                    pe.wait_ge(at_free, 16 * i + 8 * p + 12)
                    pe.matmul(ps[:, 4 + p, 0:GW], g_qe[:, p, :], state, start=True, stop=False, skip_group_check=True)
                    for h in range(GH):
                        mm = pe.matmul(ps[:, 4 + p, h * GV:(h + 1) * GV], g_att[:, p, h, :],
                                       vg[:, bass.ds(n, 1), h * GV:(h + 1) * GV].rearrange("p a v -> p (a v)"),
                                       start=False, stop=h == GH - 1, skip_group_check=True)
                    mm.then_inc(o_done, 1)
                    pe.wait_ge(kt_evac, n + 1)
                    pe.matmul(ps[:, 7, 0:GW], g_ktt[:, p, :],
                              vg[:, bass.ds(n, 1), 0:GW].rearrange("p a v -> p (a v)"), start=True, stop=True).then_inc(st_done, 1)

                with pe.Fori(0, NT // 2) as i:
                    for p in range(2):
                        tile(i, p)
                pe.wait_ge(g_dve, NT + 2)
                levels(0, 0, NL * NT, ND, [NL - 1, NL - 3, NL - 2])
                pe.wait_ge(o_norm, NT + 1)
                pe.wait_ge(ot_evac, NT + 1)
                for k in range(2):
                    mm = pe.transpose(ps[:, 6, k * P:(k + 1) * P], g_o[:, 1, k * P:(k + 1) * P], ident)
                mm.then_inc(ot_done, 1)
                pe.wait_ge(st_ready, NT + 1)
                pe.transpose(ps[0:ND, 7, 0:P], g_kt[:, 0, 0:ND], ident).then_inc(kt_done, 1)
                pe.wait_ge(ds_full, 16 * GH)
                pe.wait_ge(o_evac, NT + 2)
                pe.wait_ge(at_free, NL * NT + 3 + 4)
                for b in range(DB):
                    pe.matmul(ps[0:ND, 4, 0:GW], d_qe[:, b, :], d_state[:, b, :], start=b == 0, stop=False, skip_group_check=True)
                for h in range(GH):
                    mm = pe.matmul(ps[0:ND, 4, h * GV:(h + 1) * GV], g_att[0:ND, 0, h, 0:ND], vg[0:ND, NT, h * GV:(h + 1) * GV],
                                   start=False, stop=h == GH - 1, skip_group_check=True)
                mm.then_inc(o_done, 1)
                pe.wait_ge(dkt_ready, 1)
                for b in range(DB):
                    if b >= 2:
                        pe.wait_ge(st_ready, NT + 1 + b - 1)
                    pe.matmul(ps[:, 7 - 2 * (b % 2), 0:GW], d_kt[0:ND, b, :], vg[0:ND, NT, 0:GW],
                              start=True, stop=True).then_inc(st_done, 1)
                pe.wait_ge(o_norm, NT + 2)
                pe.wait_ge(ot_evac, NT + 2)
                for k in range(2):
                    mm = pe.transpose(ps[:, 6, k * ND:(k + 1) * ND], g_o[0:ND, 0, k * P:(k + 1) * P], ident[0:ND, 0:ND])
                mm.then_inc(ot_done, 1)
                stage_end(pe, 3)

                pe.transpose(ps[0:ND, 3, 0:P], ckv_new, ident).then_inc(tok_done, 1)
                pe.wait_ge(tok_evac, 1)

                def turn_over(n, g):
                    s = n % NSLOT
                    if g == 0:
                        pe.wait_ge(ck_full[s], 32 * (n // NSLOT + 1))
                    pe.wait_ge(ct_evac, NGR * n + g + 1)
                    for j in range(4):
                        mm = pe.transpose(ps[:, g % 2, j * P:(j + 1) * P], ck[s][:, 4 * g + j, :], ident)
                    mm.then_inc(ct_done, 1)
                    pe.wait_ge(k4_evac, NGR * n + g + 1)
                    pe.transpose(ps[:, 2, 0:P], kr_c[s][:, 4 * g:4 * g + 4, :].rearrange("p j r -> p (j r)"), ident).then_inc(k4_done, 1)

                def block_scores(n, g):
                    out = ps[:, 4 + 2 * (n % 2) + g // 4, (g % 4) * P:(g % 4 + 1) * P]
                    pe.wait_ge(ct_evac, NGR * n + g + 3)
                    pe.wait_ge(k4_evac, NGR * n + g + 2)
                    pe.matmul(out, k4[:, g % 2, :], qpe_dec[:, n, :, :].rearrange("p j q -> p (j q)"), start=True, stop=False)
                    for j in range(4):
                        mm = pe.matmul(out, ct[:, g % 2, j * P:(j + 1) * P], q_dec[:, n, 96 - ND * j:224 - ND * j],
                                       start=False, stop=j == 3)
                    mm.then_inc(sc_done, 1)

                def new_scores(n):
                    pe.wait_ge(tail_dve, 5 * n)
                    pe.matmul(ps[0:ND, 3, 0:ND], ckv_new, q_dec[:, n, 96:128], start=True, stop=False)
                    pe.matmul(ps[0:ND, 3, 0:ND], kr_new[64:96, :], qpe_new[64:96, n, :], start=False, stop=True).then_inc(tail_pe, 1)

                def max_rows(n):
                    pe.wait_ge(tail_dve, 5 * n + 1)
                    pe.transpose(ps[0:ND, 3, 0:P], mx, ident).then_inc(tail_pe, 1)

                def max_everywhere(n):
                    pe.wait_ge(tail_dve, 5 * n + 2)
                    pe.matmul(ps[:, 3, 0:ND], ones[0:ND, :], diag[0:ND, :], start=True, stop=True).then_inc(tail_pe, 1)

                def latents(n):
                    pe.wait_ge(tail_dve, 5 * n + 3)
                    for j in range(BLK):
                        pe.matmul(ps[0:ND, 3, 0:P], pd[:, j, :], ck[n % NSLOT][:, j, :], start=j == 0, stop=False)
                    pe.matmul(ps[0:ND, 3, 0:P], p_new[0:ND, :], ckv_tok[0:ND, :], start=False, stop=True)
                    pe.matmul(ps[0:ND, 3, P:P + 1], sm, ones[:, 0:1], start=True, stop=True).then_inc(tail_pe, 1)

                def latents_back(n):
                    pe.wait_ge(tail_dve, 5 * n + 4)
                    pe.transpose(ps[:, 3, 0:ND], d_o[0:ND, :], ident[0:ND, 0:ND]).then_inc(tail_pe, 1)

                for n in range(DB):
                    turn_over(n, 0)
                    for g in range(NGR):
                        if g + 1 < NGR:
                            turn_over(n, g + 1)
                        block_scores(n, g)
                        if n >= 1:
                            if g == 0:
                                max_rows(n - 1)
                            if g == 1:
                                max_everywhere(n - 1)
                            if g == 3:
                                latents(n - 1)
                            if g == 5:
                                latents_back(n - 1)
                    new_scores(n)
                for f in (max_rows, max_everywhere, latents, latents_back):
                    f(DB - 1)
                pe.wait_ge(tail_dve, 5 * DB)
                for h in range(H):
                    mm = pe.matmul(ps[64 * (h % 2):64 * (h % 2) + 64, 0, (h // 2) * ND:(h // 2 + 1) * ND],
                                   wuv[:, h * VD:(h + 1) * VD], o_lat[:, h].rearrange("p b t -> p (b t)"),
                                   start=True, stop=True, skip_group_check=True)
                mm.then_inc(tail_pe, 1)
                stage_end(pe, 4)
                linear(2, IN_MT, 2, mix)
                stage_end(pe, 5)
                pe.wait_ge(msq_ready, 1)
                for k in range(KT):
                    mm = pe.matmul(ps[:, 3, 0:NMEM], ones, mem_sq[:, k, :], start=k == 0, stop=k == KT - 1)
                mm.then_inc(mssq_ready, 1)
                sum_squares(lambda k, c: sq[:, k, chunks[c][1]], NCH, KT, NCH, 0, sq_ready, ssq_ready)
                pe.wait_ge(mnorm_ready, 1)
                pe.wait_ge(wxv_full, 16)
                for t in range(2):
                    for k in range(KT):
                        mm = pe.matmul(ps[:, 6 + t, :], mem_n[:, k, t * P:(t + 1) * P], wxv[:, k, :], start=k == 0, stop=k == KT - 1)
                    mm.then_inc(mv_done, 1)
                pe.wait_ge(std_ready, 2 * NCH)
                for j in range(XK_MT):
                    pe.wait_ge(ring_full[j], 16 * 5)
                    pe.wait_ge(lin_evac, IN_MT + OUT_MT + j + 1)
                    for k in range(KT):
                        mm = pe.matmul(ps[:, (j % 2) * NCH, 0:NMEM], ring[:, j, k, :], mem_n[:, k, :], start=k == 0, stop=k == KT - 1)
                    mm.then_inc(lin_done, 1)
                pe.wait_ge(norm_ready, 2 * NCH)
                linear(1, IN_MT + OUT_MT + XK_MT, 5, xn)
                stage_end(pe, 6)

                def x_back(n, p, w):
                    pe.wait_ge(xon_ready, n + 1)
                    pe.wait_ge(xot_evac, n)
                    for h in range(XH):
                        mm = pe.transpose(ps[:, 7, h * w:(h + 1) * w], xon[0:w, p, h, :], ident[0:w, 0:w])
                    mm.then_inc(xot_done, 1)

                pe.wait_ge(qt_ready, 1)
                for h in range(XH):
                    mm = pe.matmul(ps[:, h // 2, (h % 2) * NMEM:(h % 2 + 1) * NMEM], qt[:, 0, h, :], mk[:, h, :],
                                   start=True, stop=True)
                mm.then_inc(xs_done, 1)
                with pe.Fori(0, NT // 2) as i:
                    for p in range(2):
                        n = 2 * i + p
                        pe.wait_ge(xp_ready, n)
                        pe.wait_ge(qt_ready, n + 2)
                        for h in range(XH):
                            mm = pe.matmul(ps[:, 2 * (1 - p) + h // 2, (h % 2) * NMEM:(h % 2 + 1) * NMEM], qt[:, 1 - p, h, :],
                                           mk[:, h, :], start=True, stop=True)
                        mm.then_inc(xs_done, 1)
                        pe.wait_ge(xp_ready, n + 1)
                        for g in range(2):
                            pe.wait_ge(xt_evac, 2 * n + g)
                            for h in range(XH):
                                mm = pe.transpose(ps[:, 4 + g, h * P:(h + 1) * P], px[:, p, h, g * P:(g + 1) * P], ident)
                            mm.then_inc(xt_done, 1)
                        pe.wait_ge(xt_evac, 2 * n + 2)
                        pe.wait_ge(xon_ready, n)
                        for h in range(XH):
                            for g in range(2):
                                mm = pe.matmul(ps[:, 6, h * P:(h + 1) * P], pxt[:, p, g, h * P:(h + 1) * P], mv[:, g, h * P:(h + 1) * P],
                                               start=g == 0, stop=g == 1)
                        mm.then_inc(xv_done, 1)
                        x_back(n, p, P)
                pe.wait_ge(qt_ready, NT + 2)
                pe.wait_ge(xp_ready, NT + 1)
                for b in range(DB):
                    pe.wait_ge(kd_full[b % 2], 16 * (b // 2 + 1))
                    for h in range(XH):
                        mm = pe.matmul(ps[0:ND, 2 + h // 2, (h % 2) * NMEM:(h % 2 + 1) * NMEM], d_qm[:, h, b, :], kd[:, b % 2, h, :],
                                       start=b == 0 and h % 2 == 0, stop=b == DB - 1, skip_group_check=True)
                    mm.then_inc(kd_used if b < DB - 1 else xs_done, 1)
                pe.wait_ge(xp_ready, NT + 2)
                for g in range(2):
                    for h in range(XH):
                        mm = pe.transpose(ps[:, 4, (g * XH + h) * ND:(g * XH + h + 1) * ND], px[0:ND, 1, h, g * P:(g + 1) * P],
                                          ident[0:ND, 0:ND])
                mm.then_inc(dt_done, 1)
                pe.wait_ge(dpt_ready, 1)
                for b in range(DB):
                    pe.wait_ge(vd_full[b % 2], 16 * (b // 2 + 1))
                    for g in range(2):
                        for h in range(XH):
                            mm = pe.matmul(ps[0:ND, 6, h * P:(h + 1) * P], d_pt[:, g * XH + h, b, :], vd[:, b % 2, g, h * P:(h + 1) * P],
                                           start=b + g + h == 0, stop=b == DB - 1 and g == 1, skip_group_check=True)
                    mm.then_inc(vd_used if b < DB - 1 else xv_done, 1)
                x_back(NT, 1, ND)
                stage_end(pe, 7)
                linear(1, IN_MT + OUT_MT + XK_MT + XQ_MT, 6, co, units=4, per=2)
                stage_end(pe, 8)
                sum_squares(lambda k, c: sq[:, k, chunks[c][1]], 2 * NCH, KT, NCH, 0, sq_ready, ssq_ready)
                pe.wait_ge(norm_ready, 3 * NCH)
                pe.wait_ge(std_ready, 3 * NCH)
                pe.wait_ge(wr_full, 16)
                for c, tok in chunks:
                    for k in range(KT):
                        mm = pe.matmul(ps[0:NR, c, 0:CH], w_r[:, k, :], xn[:, k, tok], start=k == 0, stop=k == KT - 1)
                    mm.then_inc(lg_done, 1)
                pe.wait_ge(lg_evac, NCH + 1)
                for t in range(NT + 1):
                    mm = pe.transpose(ps[:, 3, t * NR:(t + 1) * NR], lgt[0:NR, t * P:(t + 1) * P], ident[0:NR, 0:NR])
                mm.then_inc(lt_done, 1)

                def rows_of(t):
                    m = P if t < NT else ND
                    if t >= 2:
                        pe.wait_ge(xr_evac, t - 1)
                    for k in range(KT):
                        b = (k // 4) + (0 if t % 2 == 0 else 6)
                        mm = pe.transpose(ps[0:m, b, (k % 4) * P:(k % 4 + 1) * P], xn[:, k, t * P:t * P + m], ident)
                    mm.then_inc(xr_done, 1)

                for t in range(4):
                    rows_of(t)
                pe.wait_ge(both_ready, 1)
                pe.matmul(ps[:, 4, 0:(NT + 1) * NE], con("below"), both.rearrange("p t e -> p (t e)"), start=True, stop=True)
                pe.matmul(ps[:, 5, 0:(NT + 1) * NE], ones, both.rearrange("p t e -> p (t e)"), start=True, stop=True).then_inc(ranked, 1)
                for t in range(4, NT + 1):
                    rows_of(t)
                stage_end(pe, 9)

                def turn_x(n, p, full):
                    pe.wait_ge(xb_full[p], full)
                    pe.wait_ge(tx_evac, n)
                    for k in range(KT):
                        mm = pe.transpose(ps[:, k // 4, (k % 4) * P:(k % 4 + 1) * P], xb[:, p, k * P:(k + 1) * P], ident)
                    mm.then_inc(tx_done, 1)

                def gate_up(n, p, j, full):
                    pe.wait_ge(we_full[j], full)
                    pe.wait_ge(tx_evac, n + 1)
                    for k in range(KT):
                        mm = pe.matmul(ps[:, 2, :], xb_t[:, p, k, :], w_e[j][:, k * 512:(k + 1) * 512], start=k == 0, stop=k == KT - 1)
                    mm.then_inc(gu_done, 1)

                def turn_h(n):
                    pe.wait_ge(h_ready, n + 1)
                    pe.wait_ge(ht_evac, n)
                    for k in range(2):
                        mm = pe.transpose(ps[:, 6, k * P:(k + 1) * P], h_b[:, k * P:(k + 1) * P], ident)
                    mm.then_inc(ht_done, 1)

                def down(n, p, j):
                    pe.wait_ge(ht_evac, n + 1)
                    pe.wait_ge(dn_evac, n)
                    for f in range(2):
                        for k in range(2):
                            at = KT * 512 + k * D + f * 512
                            mm = pe.matmul(ps[:, 4 + f, :], h_t[:, p, k, :], w_e[j][:, at:at + 512], start=k == 0, stop=k == 1)
                    mm.then_inc(dn_done, 1)

                def block(n, j, i, j1, i1, more=True):
                    gate_up(n, j % 2, j, 16 * (i + 1))
                    down(n - 1, (j + 1) % 2, (j + 3) % 4)
                    if more:
                        turn_x(n + 1, j1 % 2, 16 * (2 * i1 + j1 // 2 + 1))
                    turn_h(n)

                turn_x(0, 0, 16)
                gate_up(0, 0, 0, 16)
                turn_x(1, 1, 16)
                turn_h(0)
                with pe.Fori(0, NE // 4 - 1) as i:
                    for j in range(1, 5):
                        nxt = j + 1
                        block(4 * i + j, j % 4, i + j // 4, nxt % 4, i + nxt // 4)
                for n in range(NE - 3, NE):
                    block(n, n % 4, n // 4, (n + 1) % 4, (n + 1) // 4, more=n < NE - 1)
                down(NE - 1, 1, 3)
                n_over = pe.value_load(over_i[0:1, 0:1], min_val=0, max_val=OVER)
                with pe.Fori(0, OVER // 4) as i:
                    for j in range(4):
                        with pe.If(n_over > 4 * i + j):
                            n = NE + 4 * i + j
                            turn_x(n, j % 2, 16 * (NE // 2 + 2 * i + j // 2 + 1))
                            gate_up(n, j % 2, j, 16 * (NE // 4 + i + 1))
                            turn_h(n)
                            down(n, j % 2, j)
                stage_end(pe, 10)
                for t in range(NT + 1):
                    m = P if t < NT else ND
                    if t >= 2:
                        pe.wait_ge(c_added, t - 1)
                    pe.wait_ge(c_ready, t + 1)
                    for k in range(KT):
                        mm = pe.transpose(ps[:, 2 * (t % 2) + k // 4, (k % 4) * m:(k % 4 + 1) * m], comb[0:m, t % 2, k * P:(k + 1) * P],
                                          ident[0:m, 0:m])
                    mm.then_inc(c_done, 1)
                stage_end(pe, 11)
                end_layer(pe, l)
            sum_squares(lambda k, c: sq[:, k, chunks[c][1]], 0, KT, NCH, 0, sq_ready, ssq_ready)

        @block.scalar
        def _(act):
            step = Steps(act, act_step)
            act.wait_ge(setup, 80)
            with act.Fori(0, DEPTH) as l:
                def squares(src, dst, width, count, scale, ready):
                    for c in range(count):
                        tok = slice(c * width, (c + 1) * width)
                        act.activation(dst[:, :, tok], src[:, :, tok], ACT.Square, scale=scale).then_inc(ready, 1)

                def roots(src, r, width, count, base, ready, done):
                    for c in range(count):
                        act.wait_ge(ready, base + c + 1)
                        act.activation(r[:, c * width:(c + 1) * width], src[:, c, 0:width], ACT.Sqrt,
                                       bias=EPS).then_inc(done, 1)

                act.sem_inc(lin_evac, 2)
                squares(x, sq, CH, NCH, D ** -0.5, sq_ready)
                roots(ps, rstd[:, 0, :], CH, NCH, 0, ssq_ready, std_ready)
                with act.Fori(0, 2) as i:
                    for j in range(RING):
                        act.wait_ge(lin_done, RING * i + j + 1)
                        act.activation(pr[:, bass.ds(RING * i + j, 1), :].rearrange("p a (c n) -> p (a c) n", c=NCH),
                                       ps[:, (j % 2) * NCH:(j % 2 + 1) * NCH, 0:CH], ACT.Copy).then_inc(lin_evac, 1)
                for t in range(NT + 1):
                    m = P if t < NT else ND
                    act.wait_ge(vg_done, t + 1)
                    act.activation(vg[0:m, t, :], ps[0:m, 6 + t % 2, :], ACT.Copy).then_inc(vg_evac, 1)
                act.wait_ge(lin_evac, IN_MT + 2)
                step.mark(act.activation(sq2[:, 0:2, :], pr[:, 2:4, :], ACT.Square, scale=1.0 / 16))
                act.activation(sq2[:, 2, :], pr[:, 4, :], ACT.Square, scale=float(P) ** -0.5).then_inc(lat_sq, 1)
                act.wait_ge(utr_done, 1)
                step.mark(act.activation(u_out[0:POOL_BUF, 0, :], ps[0:POOL_BUF, 6, 0:GW], ACT.Copy))
                act.activation(u_out[0:ND, 1, :], ps[0:ND, 7, 0:GW], ACT.Copy).then_inc(utr_evac, 1)
                act.wait_ge(utr_evac, 1)
                step.sync()
                act.dma_start(outs["pool_p"][bass.ds(l, 1)].rearrange("a t c -> (a t) c"), u_out[0:POOL_BUF, 0, :]).then_inc(states_stored, 16)
                for b in range(DB):
                    act.dma_start(outs["pool_s"][bass.ds(l, 1), b, POOL_BUF - DT:POOL_BUF, :].rearrange("a t c -> (a t) c"),
                                  u_out[b * DT:(b + 1) * DT, 1, :]).then_inc(states_stored, 16)
                act.dma_start(outs["pool_s"][bass.ds(l, 1), :, 0:POOL_BUF - DT, :].rearrange("a b t c -> (a b) t c"),
                              ins["pool_old"][bass.ds(l, 1), :, DT:POOL_BUF, :].rearrange("a b t c -> (a b) t c")).then_inc(states_stored, 16)
                act.wait_ge(lat_ssq, 1)
                step.mark(act.activation(rstd[:, 0, :].rearrange("p (c n) -> p c n", c=NCH), ps[:, 0:NCH, 0:CH], ACT.Sqrt, bias=EPS))
                act.activation(rstd[:, 1, :].rearrange("p (c n) -> p c n", c=NCH), ps[:, NCH:2 * NCH, 0:CH], ACT.Sqrt,
                               bias=EPS).then_inc(lat_std, 1)
                act.activation(silu[:, 0:NT, :], vg[:, 0:NT, GW:512], ACT.Exp, scale=-1.0).then_inc(gate_e, 1)
                act.activation(silu[0:ND, NT, :], vg[0:ND, NT, GW:512], ACT.Exp, scale=-1.0).then_inc(gate_e, 1)
                act.wait_ge(z_done, 1)
                act.wait_ge(kr_ready, 1)
                act.activation(la.rearrange("p (c n) -> p c n", c=NCH), ps[:, 0:NCH, 0:CH], ACT.Identity,
                               bias=gain("b_gk")).then_inc(z_evac, 1)
                act.wait_ge(z_evac, 1)
                step(act.activation(la_t, la, ACT.Abs))
                step(act.activation(la_t, la_t, ACT.Exp, scale=-1.0))
                act.activation(la_t, la_t, ACT.Ln, bias=1.0).then_inc(z_evac, 1)
                act.wait_ge(pool_mm, 1)
                for k in range(2):
                    ev = act.activation(mix[:, k, :].rearrange("p (c n) -> p c n", c=NCH), ps[:, k * NCH:(k + 1) * NCH, 0:CH],
                                        ACT.Copy, scale=gain("pool_scale", k))
                step.mark(ev)
                for t in range(NT):
                    act.wait_ge(vv_done, t + 1)
                    act.activation(vv[t // 4][:, t % 4, :], ps[:, 6 + t % 2, :], ACT.Copy).then_inc(vv_evac, 1)
                act.wait_ge(kr_ready, 1)
                act.wait_ge(lat_norm, 2)
                act.dma_start(outs["ckv"][bass.ds(l, 1)].rearrange("a p n -> p (a n)"), pr[:, 4, :]).then_inc(states_stored, 16)
                act.dma_start(outs["kpe"][bass.ds(l, 1)].rearrange("a p n -> p (a n)"), kr[64:96, :]).then_inc(states_stored, 16)
                act.wait_ge(states_stored, 16 * (DB + 4))
                step.restart()
                stage_end(act, 1)

                def evacuate(m, n9, w):
                    act.activation(pt[:, m % 2, 0:w], ps[:, 4 + m % 2, 0:w], ACT.Copy).then_inc(tp_free[m % 2], 1)

                def expo(qb, item):
                    act.wait_ge(nmax_ready, item + 1)
                    act.activation(prob[:, qb % 2, 0:(qb + 1) * P],
                                   ps[:, 2 * (qb % 2):2 * (qb % 2) + 2, :].rearrange("p a n -> p (a n)")[:, 0:(qb + 1) * P],
                                   ACT.Exp, bias=nmax[:, qb % 2, 1:2], scale=MLA_SCALE).then_inc(p_ready, 1)

                expo(0, 0)
                expo(1, 1)
                with act.Fori(0, H // 2) as i:
                    for p in range(2):
                        m = 0
                        item = 16 * i + 8 * p
                        for qb in range(NT):
                            for at in range(0, qb + 1, 4):
                                act.wait_ge(tp_done, 36 * i + 18 * p + 6 + m + 1)
                                evacuate(m, 0, (min(at + 4, qb + 1) - at) * P)
                                m += 1
                            if qb < 6:
                                expo(qb + 2, item + qb + 2)
                                m += 1
                            else:
                                expo(qb - 6, item + qb + 2)
                stage_end(act, 2)

                act.sem_inc(o_evac, 2)
                act.sem_inc(ot_evac, 1)

                def exps(n, p, w, lv):
                    act.wait_ge(g_sub, n)
                    step.mark(act.activation(g_e[:, lv:NL - 1, 0:w], g_e[:, lv:NL - 1, 0:w], ACT.Exp))
                    act.wait_ge(g_pool, n - 1)
                    act.wait_ge(g_dve, n - 1)
                    step.mark(act.activation(g_eb[:, 0:w], g_b[:, p, 0:w], ACT.Exp, bias=LOG_SCALE))
                    if w == P:
                        step.mark(act.activation(g_ek, g_b[:, p, :], ACT.Exp, scale=-1.0, bias=g_b[:, p, P - 1:P]))
                        act.activation(g_last[:, p, 0:1], g_b[:, p, P - 1:P], ACT.Exp).then_inc(g_exp, 1)
                    else:
                        step.mark(act.activation(g_ek[:, 0:w], g_ek[:, 0:w], ACT.Exp))
                        act.activation(g_last[:, 0, :], g_b[:, 0, 0:ND].rearrange("p (b t) -> p b t", b=DB)[:, :, DT - 1], ACT.Exp).then_inc(g_exp, 1)

                def take_kt(n, p, w):
                    act.wait_ge(kt_done, n)
                    act.activation(g_ktt[0:w, p, :], ps[0:w, 7, 0:P], ACT.Copy).then_inc(kt_evac, 1)

                def take_o(n, p, w):
                    act.wait_ge(o_done, n)
                    act.activation(g_o[0:w, p, :], ps[0:w, 4 + p, 0:GW], ACT.Copy).then_inc(o_evac, 1)
                    act.wait_ge(o_sum, n)
                    act.activation(g_ms[0:w, 1, :], g_ms[0:w, 0, :], ACT.Sqrt, bias=EPS, scale=1.0 / GV).then_inc(o_root, 1)

                def take_ot(n, w, cols):
                    act.wait_ge(ot_done, n)
                    act.activation(mix[:, 6:8, cols], ps[:, 6, 0:2 * w].rearrange("p (k t) -> p k t", k=2), ACT.Copy,
                                   scale=gain("g_gla")).then_inc(ot_evac, 1)

                act.wait_ge(g_sub, 1)
                step.mark(act.activation(g_e[:, 0:NL - 1, :], g_e[:, 0:NL - 1, :], ACT.Exp))
                step.mark(act.activation(g_eb, g_b[:, 0, :], ACT.Exp, bias=LOG_SCALE))
                step.mark(act.activation(g_ek, g_b[:, 0, :], ACT.Exp, scale=-1.0, bias=g_b[:, 0, P - 1:P]))
                act.activation(g_last[:, 0, 0:1], g_b[:, 0, P - 1:P], ACT.Exp).then_inc(g_exp, 1)
                step.sync()
                step.restart()
                with act.Fori(0, NT // 2) as i:
                    for p in range(2):
                        n = 2 * i + p
                        exps(n + 2, 1 - p, P, 0)
                        take_ot(n + 1, P, bass.ds(P * ((n + NT - 1) % NT), P))
                        take_kt(n + 1, p, P)
                        take_o(n + 1, p, P)
                        step.sync()
                        step.restart()
                exps(NT + 2, 0, ND, NL - 3)
                take_ot(NT + 1, P, slice(SEQ - P, SEQ))
                take_kt(NT + 1, 0, ND)
                take_o(NT + 1, 0, ND)
                take_ot(NT + 2, ND, slice(SEQ, TOK))
                act.wait_ge(st_ready, NT + DB + 1)
                act.wait_ge(g_dve, NT + 2)
                for h in range(GH):
                    rows, cols = slice(GK * h, GK * (h + 1)), slice(GV * h, GV * (h + 1))
                    act.dma_start(outs["gla_p"][bass.ds(l, 1), h].rearrange("a k v -> (a k) v"), state[rows, cols]).then_inc(states_stored, 16)
                    act.dma_start(outs["gla_s"][bass.ds(l, 1), :, h].rearrange("a b k v -> (a k) b v"), d_state[rows, :, cols]).then_inc(states_stored, 16)
                act.wait_ge(states_stored, 16 * (DB + 4 + 2 * GH))
                step.sync()
                step.restart()
                stage_end(act, 3)

                act.sem_inc(ct_evac, 2)
                for n in range(DB + 1):
                    for g in range(NGR if n < DB else 0):
                        act.wait_ge(ct_done, NGR * n + g + 1)
                        act.activation(ct[:, g % 2, :], ps[:, g % 2, :], ACT.Copy).then_inc(ct_evac, 1)
                        if n >= 1 and g == 3:
                            act.wait_ge(shifted, n)
                            step.mark(act.activation(pd, pd, ACT.Exp, scale=MLA_SCALE))
                            act.activation(p_new[0:ND, :], p_new[0:ND, :], ACT.Exp, scale=MLA_SCALE).then_inc(pd_ready, 1)
                    if n == DB:
                        act.wait_ge(shifted, n)
                        step.mark(act.activation(pd, pd, ACT.Exp, scale=MLA_SCALE))
                        act.activation(p_new[0:ND, :], p_new[0:ND, :], ACT.Exp, scale=MLA_SCALE).then_inc(pd_ready, 1)
                act.wait_ge(tail_pe, 5 * DB + 1)
                act.activation(mix[:, 2:6, SEQ:TOK], ps[:, 0, 0:4 * ND].rearrange("p (k t) -> p k t", k=4), ACT.Copy).then_inc(act_step, 1)
                step.n += 1
                step.sync()
                step.restart()
                stage_end(act, 4)
                stage_end(act, 5)
                act.wait_ge(mem_full, 16)
                act.activation(mem_sq, mem, ACT.Square, scale=D ** -0.5).then_inc(msq_ready, 1)
                squares(x, sq, CH, NCH, D ** -0.5, sq_ready)
                act.wait_ge(mssq_ready, 1)
                act.activation(mem_r, ps[:, 3, 0:NMEM], ACT.Sqrt, bias=EPS).then_inc(mstd_ready, 1)
                roots(ps, rstd[:, 0, :], CH, NCH, NCH, ssq_ready, std_ready)
                for j in range(XK_MT):
                    act.wait_ge(lin_done, IN_MT + OUT_MT + j + 1)
                    act.activation(mk[:, j, :], ps[:, (j % 2) * NCH, 0:NMEM], ACT.Copy).then_inc(lin_evac, 1)
                for t in range(2):
                    act.wait_ge(mv_done, t + 1)
                    act.activation(mv[:, t, :], ps[:, 6 + t, :], ACT.Copy).then_inc(mv_evac, 1)
                act.wait_ge(lin_evac, IN_MT + OUT_MT + XK_MT + 2)
                act.wait_ge(mv_evac, 2)
                act.dma_start(outs["mk"][bass.ds(l, 1)].rearrange("a p h m -> p (a h) m"), mk).then_inc(states_stored, 16)
                act.dma_start(outs["mv"][bass.ds(l, 1)].rearrange("a p h m -> p (a h) m"), mv).then_inc(states_stored, 16)
                stage_end(act, 6)

                def x_exps(n, p, w):
                    act.wait_ge(xm_ready, n)
                    for h in range(XH):
                        last = act.activation(px[0:w, p, h, :], ps[0:w, 2 * p + h // 2, (h % 2) * NMEM:(h % 2 + 1) * NMEM], ACT.Exp,
                                              bias=xm[0:w, p, 4 + h:5 + h], scale=X_SCALE, accum_out=xm[0:w, p, 8 + h:9 + h])
                    last.then_inc(xp_ready, 1)

                x_exps(1, 0, P)
                with act.Fori(0, NT // 2) as i:
                    for p in range(2):
                        n = 2 * i + p
                        for g in range(2):
                            act.wait_ge(xt_done, 2 * n + g + 1)
                            act.activation(pxt[:, p, g, :], ps[:, 4 + g, :], ACT.Copy).then_inc(xt_evac, 1)
                        x_exps(n + 2, 1 - p, P)
                x_exps(NT + 2, 1, ND)
                act.wait_ge(states_stored, 16 * (DB + 6 + 2 * GH))
                stage_end(act, 7)
                stage_end(act, 8)
                squares(x, sq, CH, NCH, D ** -0.5, sq_ready)
                roots(ps, rstd[:, 0, :], CH, NCH, 2 * NCH, ssq_ready, std_ready)
                for c, tok in chunks:
                    act.wait_ge(lg_done, c + 1)
                    act.activation(lgt[0:NR, tok], ps[0:NR, c, 0:CH], ACT.Identity, bias=gain("b_r", 0, NR)).then_inc(lg_evac, 1)

                def keep_rows(t):
                    m = P if t < NT else ND
                    act.wait_ge(xr_done, t + 1)
                    if t >= 4:
                        act.wait_ge(row_moved[t % 4], 32 * (t // 4))
                    b = 0 if t % 2 == 0 else 6
                    act.activation(xr[0:m, t % 4, :].rearrange("p (a n) -> p a n", a=2), ps[0:m, b:b + 2, :], ACT.Copy).then_inc(xr_evac, 1)

                keep_rows(0)
                keep_rows(1)
                act.wait_ge(rx_in, 1)
                act.activation(r_exp, r_exp, ACT.Exp).then_inc(rx_out, 1)
                for t in range(2, NT + 1):
                    keep_rows(t)
                stage_end(act, 9)

                def gate_exp(n):
                    act.wait_ge(gu_done, n + 1)
                    act.activation(h_e, ps[:, 2, 0:DE], ACT.Exp, scale=-1.0).then_inc(ge_ready, 1)

                def keep_h(n, p):
                    act.wait_ge(ht_done, n + 1)
                    act.activation(h_t[:, p].rearrange("p k t -> p (k t)"), ps[:, 6, 0:DE], ACT.Copy).then_inc(ht_evac, 1)

                def send_y(n, p, sent):
                    act.wait_ge(dn_done, n + 1)
                    act.wait_ge(y_sent[p], sent)
                    act.sem_inc(turn, 1)
                    act.activation(y_sb[:, p, :].rearrange("p (a n) -> p a n", a=2), ps[:, 4:6, :], ACT.Copy).then_inc(dn_evac, 1)
                    act.wait_ge(dn_evac, n + 1)
                    act.sem_inc(turn, 1)
                    act.dma_start(slots[bass.ds(CAP * n, CAP), :], y_sb[:, p, :]).then_inc(y_sent[p], 16)

                gate_exp(0)
                keep_h(0, 0)
                with act.Fori(0, NE // 4 - 1) as i:
                    for j in range(1, 5):
                        n = 4 * i + j
                        gate_exp(n)
                        send_y(n - 1, (j + 1) % 2, 16 * (2 * i + (j - 1) // 2))
                        keep_h(n, j % 2)
                for n in range(NE - 3, NE):
                    gate_exp(n)
                    send_y(n - 1, (n - 1) % 2, 16 * ((n - 1) // 2))
                    keep_h(n, n % 2)
                send_y(NE - 1, 1, 16 * (NE // 2 - 1))
                for p in range(2):
                    act.wait_ge(y_sent[p], 16 * (NE // 2))
                n_over = act.value_load(over_i[0:1, 0:1], min_val=0, max_val=OVER)
                with act.Fori(0, OVER // 4) as i:
                    for j in range(4):
                        with act.If(n_over > 4 * i + j):
                            n = NE + 4 * i + j
                            gate_exp(n)
                            keep_h(n, j % 2)
                            send_y(n, j % 2, 16 * (NE // 2 + 2 * i + j // 2))
                            act.wait_ge(y_sent[j % 2], 16 * (NE // 2 + 2 * i + j // 2 + 1))
                            act.sem_inc(turn, 1)
                stage_end(act, 10)
                for t in range(NT + 1):
                    m = P if t < NT else ND
                    act.wait_ge(row_moved[t % 4], 32 * ((NT - t % 4) // 4 + 1 + t // 4 + 1))
                    if t >= 2:
                        act.wait_ge(c_done, t - 1)
                    act.activation(comb[0:m, t % 2, :], yg[0:m, t % 4, 0, :], ACT.Copy, scale=gates[0:m, 0, t:t + 1]).then_inc(c_half, 1)
                stage_end(act, 11)
                end_layer(act, l)
            squares(x, sq, CH, NCH, D ** -0.5, sq_ready)
            roots(ps, rstd[:, 0, :], CH, NCH, 0, ssq_ready, std_ready)

        @block.vector
        def _(dve):
            step = Steps(dve, dve_step)
            dve.wait_ge(setup, 80)
            step(dve.tensor_copy(lmask[:, :, :], lmask_f))
            step.restart()
            with dve.Fori(0, DEPTH) as l:
                def norm(base, tiles, src, dst, g, r, width, count, ready, done):
                    for c in range(count):
                        tok = slice(c * width, (c + 1) * width)
                        dve.wait_ge(ready, base + c + 1)
                        step(dve.reciprocal(r[:, tok], r[:, tok]))
                        for k in range(tiles):
                            last = dve.scalar_tensor_tensor(out=dst[:, k, tok], in0=src[:, k, tok], scalar=gain(g, k),
                                                            in1=r[:, tok], op0=ALU.mult, op1=ALU.mult)
                        last.then_inc(done, 1)

                dve.wait_ge(vec_full, 16)
                norm(0, KT, x, xn, "g_mix", rstd[:, 0, :], CH, NCH, std_ready, norm_ready)
                dve.wait_ge(kswap_full, 32)
                dve.wait_ge(lin_evac, IN_MT + 2)
                step.mark(dve.tensor_tensor(kr[64:96, :], pr[64:96, 5, :], rope[64:96, 0, :], ALU.mult))
                step(dve.tensor_tensor(kswap[64:96, :], kswap[64:96, :], rope[64:96, 1, :], ALU.mult))
                dve.tensor_tensor(kr[64:96, :], kr[64:96, :], kswap[64:96, :], ALU.add).then_inc(kr_ready, 1)
                dve.wait_ge(lat_std, 1)
                step(dve.reciprocal(rstd[:, 0, :], rstd[:, 0, :]))
                dve.reciprocal(rstd[:, 1, :], rstd[:, 1, :]).then_inc(lat_norm, 1)
                dve.wait_ge(lat_norm, 1)
                for k in range(2):
                    step.mark(dve.scalar_tensor_tensor(out=pr[:, 2 + k, :], in0=pr[:, 2 + k, :], scalar=gain("g_qn", k),
                                                       in1=rstd[:, 0, :], op0=ALU.mult, op1=ALU.mult))
                dve.scalar_tensor_tensor(out=pr[:, 4, :], in0=pr[:, 4, :], scalar=gain("g_kvn"), in1=rstd[:, 1, :],
                                         op0=ALU.mult, op1=ALU.mult).then_inc(lat_norm, 1)
                dve.wait_ge(lat_norm, 2)
                dve.wait_ge(kr_ready, 1)
                step.mark(dve.tensor_copy(ckv_new, pr[:, 4, SEQ:TOK]))
                step.mark(dve.tensor_copy(kr_new[64:96, :], kr[64:96, SEQ:TOK]))
                for n, (s_, g_) in enumerate(((silu[:, 0:NT, :], vg[:, 0:NT, GW:512]), (silu[0:ND, NT, :], vg[0:ND, NT, GW:512]))):
                    dve.wait_ge(gate_e, n + 1)
                    step(dve.tensor_scalar(s_, s_, 1.0, None, ALU.add))
                    step(dve.reciprocal(s_, s_))
                    step.mark(dve.tensor_tensor(g_, g_, s_, ALU.mult))
                dve.wait_ge(z_evac, 2)
                step(dve.scalar_tensor_tensor(out=la, in0=la, scalar=0.0, in1=la_t, op0=ALU.min, op1=ALU.subtract))
                step(dve.tensor_scalar(la, la, 1.0 / 16.0, None, ALU.mult))
                step.restart()
                stage_end(dve, 1)

                dve.sem_inc(y_free, 2)
                for p in range(2):
                    step.mark(dve.tensor_copy(k_h[64:96, p, :], kr[64:96, :]))
                step.sync()

                def max_of(qb, item):
                    dve.wait_ge(s_done, item + 1)
                    s = ps[:, 2 * (qb % 2):2 * (qb % 2) + 2, :].rearrange("p a n -> p (a n)")[:, 0:(qb + 1) * P]
                    step(dve.reduce_max(nmax[:, qb % 2, 0:1], s, AX))
                    dve.tensor_scalar(nmax[:, qb % 2, 1:2], nmax[:, qb % 2, 0:1], -MLA_SCALE, None, ALU.mult).then_inc(nmax_ready, 1)

                def piece(p, k, b, tp, n_head, h):
                    dve.wait_ge(tp_done, tp)
                    if k < 3:
                        tok = (slice(0, 512), slice(512, 1024), slice(SEQ, TOK))[k]
                        src, dst = ps[0:QK, 4 + b, 0:tok.stop - tok.start], q_h[0:QK, p, tok]
                        dve.tensor_copy(dst, src).then_inc(tp_free[b], 1)
                    elif k < 5:
                        tok = (slice(0, 512), slice(512, 1024))[k - 3]
                        dve.tensor_copy(k_h[0:NOPE, p, tok], ps[0:NOPE, 4 + b, :]).then_inc(tp_free[b], 1)
                    else:
                        dve.wait_ge(zeroed, 1)
                        dve.tensor_copy(q_dec[:, :, bass.ds(96 + DT * h, DT)],
                                        ps[:, 4 + b, 0:ND].rearrange("p (b t) -> p b t", b=DB)).then_inc(tp_free[b], 1)

                def q_pe(p, n, h):
                    dve.wait_ge(q_rope, n)
                    src = q_h[64:96, p, SEQ:TOK].rearrange("p (b t) -> p b t", b=DB)
                    for j in range(4):
                        step.mark(dve.tensor_copy(qpe_dec[32 * j:32 * j + 32, :, j, bass.ds(DT * h, DT)], src))
                    step.mark(dve.tensor_copy(qpe_new[64:96, :, bass.ds(DT * h, DT)], src))

                for k in range(6):
                    piece(0, k, k % 2, k + 1, 1, 0)
                q_pe(0, 1, 0)
                step.sync()
                max_of(0, 0)
                max_of(1, 1)
                step.restart()
                with dve.Fori(0, H // 2) as i:
                    for p in range(2):
                        item = 16 * i + 8 * p
                        m = 0
                        for qb in range(NT):
                            m += 1 + (qb >= 4)
                            max_of((qb + 2) % NT, item + qb + 2)
                            if qb < 6:
                                piece(1 - p, qb, m % 2, 36 * i + 18 * p + 6 + m + 1, 0, (2 * i + p + 1) % H)
                                m += 1
                            if qb == 6:
                                q_pe(1 - p, 2 * i + p + 2, (2 * i + p + 1) % H)
                            if qb % 4 == 3:
                                hf = qb // 4
                                dve.wait_ge(y_done, 4 * i + 2 * p + hf + 1)
                                dve.wait_ge(y_free, 4 * i + 2 * p + hf + 2)
                                step(dve.reciprocal(recip, ps[64:128, 6 + hf, :]))
                                dve.tensor_tensor(mix[64 * p:64 * p + 64, bass.ds(2 + i, 1), 512 * hf:512 * hf + 512]
                                                  .rearrange("p a n -> p (a n)"), ps[0:64, 6 + hf, :], recip,
                                                  ALU.mult).then_inc(y_free, 1)
                        step.sync()
                        step.restart()
                stage_end(dve, 2)

                hm = con("headmask").unsqueeze(2)
                bd = con("bdmask")

                def decays(p, w, lvs):
                    for lv in lvs:
                        z = LEVELS[lv]
                        e = g_e[:, lv, 0:w].rearrange("p (n z) -> p n z", z=2 * z)
                        b = g_b[:, p, 0:w].rearrange("p (n z) -> p n z", z=2 * z)
                        mid = b[:, :, z - 1:z].broadcast_to([P, w // (2 * z), z])
                        step.mark(dve.tensor_tensor(e[:, :, z:2 * z], b[:, :, z:2 * z], mid, ALU.subtract))
                        last = dve.tensor_tensor(e[:, :, 0:z], mid, b[:, :, 0:z], ALU.subtract)
                    return last

                def queries(p, w, lvs):
                    for lv in lvs:
                        last = dve.tensor_tensor(g_q[:, p, lv, :, 0:w], g_e[:, lv, 0:w].unsqueeze(1).broadcast_to([P, GH, w]),
                                                 g_q0[:, p, :, 0:w], ALU.mult)
                    last.then_inc(g_dve, 1)

                def begin(n, p, cols):
                    step(dve.tensor_tensor_scan(g_b[:, p, :], la[:, cols], la[:, cols], 0.0, ALU.add, ALU.bypass))
                    decays(p, P, range(NL - 1)).then_inc(g_sub, 1)

                def evacuate(n8, n, p, w, order):
                    for j, lv in enumerate(order):
                        dve.wait_ge(at_done, n8 + j + 1)
                        src = ps[0:w, j % 4, 0:GH * w].rearrange("p (h t) -> p h t", h=GH)
                        dst = g_att[0:w, p, :, 0:w]
                        if lv == NL - 1:
                            ins_ = dve.tensor_tensor(dst, src, ident[0:w, 0:w].unsqueeze(1).broadcast_to([w, GH, w]), ALU.mult)
                        else:
                            ins_ = dve.copy_predicated(dst, lmask[0:w, lv, 0:w].unsqueeze(1).broadcast_to([w, GH, w]), src)
                        ins_.then_inc(at_free, 1)
                        dve.wait_ge(at_free, n8 + j + 1 + 4)

                def norm_o(n, p, w, gate):
                    dve.wait_ge(o_evac, n + 2)
                    step(dve.tensor_tensor(g_sq[0:w, :], g_o[0:w, p, :], g_o[0:w, p, :], ALU.mult))
                    dve.tensor_reduce(g_ms[0:w, 0, :], g_sq[0:w, :].rearrange("p (h v) -> p h v", h=GH), AX, ALU.add).then_inc(o_sum, 1)
                    dve.wait_ge(o_root, n)
                    step(dve.reciprocal(g_ms[0:w, 1, :], g_ms[0:w, 1, :]))
                    step(dve.tensor_tensor(g_o[0:w, p, :].rearrange("p (h v) -> p h v", h=GH),
                                           g_o[0:w, p, :].rearrange("p (h v) -> p h v", h=GH),
                                           g_ms[0:w, 1, :].unsqueeze(2).broadcast_to([w, GH, GV]), ALU.mult))
                    dve.tensor_tensor(g_o[0:w, p, :], g_o[0:w, p, :], gate, ALU.mult).then_inc(o_norm, 1)

                dve.sem_inc(at_free, 4)
                step.mark(dve.memset(g_e[:, NL - 1, :], 1.0))
                dve.memset(g_o[:, 1, :], 0.0).then_inc(o_norm, 1)
                dve.memset(state, 0.0).then_inc(st_ready, 1)
                begin(1, 0, slice(0, P))
                dve.wait_ge(g_exp, 1)
                dve.wait_ge(g_spread, 1)
                queries(0, P, range(DSPLIT, NL - 1))
                dve.wait_ge(g_pool, 1)
                step.sync()
                step.restart()
                with dve.Fori(0, NT // 2) as i:
                    for p in range(2):
                        n = 2 * i + p
                        nxt = bass.ds(((n + 1) % NT) * P, P)
                        dve.wait_ge(g_pool, n + 1)
                        begin(n + 2, 1 - p, nxt)
                        evacuate_n = 16 * i + 8 * p
                        for j, lv in enumerate([NL - 1] + list(range(NL - 1))):
                            dve.wait_ge(at_done, evacuate_n + j + 1)
                            dve.sem_inc(turn, 1)
                            src = ps[:, j % 4, :].rearrange("p (h t) -> p h t", h=GH)
                            if j == 0:
                                ins_ = dve.tensor_tensor(g_att[:, p], src, ident.unsqueeze(1).broadcast_to([P, GH, P]), ALU.mult)
                            else:
                                ins_ = dve.copy_predicated(g_att[:, p], lmask[:, lv, :].unsqueeze(1).broadcast_to([P, GH, P]), src)
                            ins_.then_inc(at_free, 1)
                            dve.wait_ge(at_free, evacuate_n + j + 1 + 4)
                            dve.sem_inc(turn, 1)
                            if j == 3:
                                dve.wait_ge(g_exp, n + 2)
                                dve.wait_ge(g_spread, n + 2)
                                queries(1 - p, P, range(DSPLIT, NL - 1))
                        dve.wait_ge(st_done, n + 1)
                        step(dve.tensor_tensor(g_tmp, ps[:, 7, 0:GW], bd, ALU.mult))
                        dve.scalar_tensor_tensor(out=state, in0=state, scalar=g_last[:, p, 0:1], in1=g_tmp,
                                                 op0=ALU.mult, op1=ALU.add).then_inc(st_ready, 1)
                        norm_o(n + 1, p, P, vg[:, bass.ds(n, 1), GW:512].rearrange("p a v -> p (a v)"))
                        step.sync()
                        step.restart()
                dve.wait_ge(g_pool, NT + 1)
                dve.wait_ge(st_ready, NT + 1)
                step(dve.tensor_copy(g_b[:, 0, 0:ND], la[:, SEQ:TOK]))
                b4 = g_b[:, 0, 0:ND].rearrange("p (b t) -> p b t", b=DB)
                for t in range(1, DT):
                    step(dve.tensor_tensor(b4[:, :, t:t + 1], b4[:, :, t:t + 1], b4[:, :, t - 1:t], ALU.add))
                step.mark(dve.tensor_tensor(g_ek[:, 0:ND].rearrange("p (b t) -> p b t", b=DB),
                                            b4[:, :, DT - 1:DT].broadcast_to([P, DB, DT]), b4, ALU.subtract))
                decays(0, ND, range(NL - 3, NL - 1)).then_inc(g_sub, 1)
                dve.wait_ge(g_exp, NT + 2)
                dve.wait_ge(at_done, NL * NT)
                for lv in (NL - 3, NL - 2, NL - 1):
                    step.mark(dve.tensor_tensor(g_k[0][:, lv, 0:ND], g_e[:, lv, 0:ND], pr[:, 7, SEQ:TOK], ALU.mult))
                step.mark(dve.tensor_tensor(g_kt[:, 0, 0:ND], g_ek[:, 0:ND], pr[:, 7, SEQ:TOK], ALU.mult))
                step(dve.tensor_tensor(g_qe[:, 0, 0:ND], pr[:, 6, SEQ:TOK], g_eb[:, 0:ND], ALU.mult))
                step.mark(dve.tensor_tensor(d_qe, g_qe[:, 0, 0:ND].unsqueeze(1).broadcast_to([P, DB, ND]),
                                            con("colbatch").rearrange("p (b t) -> p b t", b=DB), ALU.mult))
                step(dve.tensor_tensor(g_q0[:, 0, :, 0:ND], pr[:, 6, SEQ:TOK].unsqueeze(1).broadcast_to([P, GH, ND]),
                                       hm.broadcast_to([P, GH, ND]), ALU.mult))
                queries(0, ND, range(NL - 3, NL - 1))
                evacuate(NL * NT, NT, 0, ND, [NL - 1, NL - 3, NL - 2])
                dve.wait_ge(kt_evac, NT + 1)
                dve.tensor_tensor(d_kt[0:ND], g_ktt[0:ND, 0, :].unsqueeze(1).broadcast_to([ND, DB, P]),
                                  con("rowbatch", ND).unsqueeze(2).broadcast_to([ND, DB, P]), ALU.mult).then_inc(dkt_ready, 1)
                norm_o(NT + 1, 0, ND, vg[0:ND, NT, GW:512])
                for b in range(DB):
                    dve.wait_ge(st_done, NT + b + 1)
                    dve.wait_ge(st_ready, NT + b + 1)
                    step(dve.tensor_tensor(g_tmp, ps[:, 7 - 2 * (b % 2), 0:GW], bd, ALU.mult))
                    dve.scalar_tensor_tensor(out=d_state[:, b, :], in0=d_state[:, b, :], scalar=g_last[:, 0, b:b + 1], in1=g_tmp,
                                             op0=ALU.mult, op1=ALU.add).then_inc(st_ready, 1)
                step.sync()
                step.restart()
                stage_end(dve, 3)

                dve.sem_inc(k4_evac, 1)
                dve.wait_ge(tok_done, 1)
                dve.tensor_copy(ckv_tok[0:ND, :], ps[0:ND, 3, 0:P]).then_inc(tok_evac, 1)

                def take_k4(n, g):
                    dve.wait_ge(k4_done, NGR * n + g + 1)
                    dve.tensor_copy(k4[:, g % 2, :], ps[:, 2, 0:P]).then_inc(k4_evac, 1)

                def blocks_of(n):
                    return ps[:, 4 + 2 * (n % 2):6 + 2 * (n % 2), :].rearrange("p a n -> p (a n)").rearrange("p (j q) -> p q j", q=ND)

                def maxima(n):
                    dve.wait_ge(sc_done, NGR * (n + 1))
                    dve.wait_ge(tail_pe, 5 * n + 1)
                    step.mark(dve.tensor_tensor(p_new[0:ND, :], ps[0:ND, 3, 0:ND],
                                                con("newmask", ND).rearrange("p (b q) -> p b q", b=DB)[:, n, :], ALU.add))
                    step(dve.tensor_reduce(mx, blocks_of(n), AX, ALU.max))
                    dve.tensor_tensor(mx[0:ND, :], mx[0:ND, :], p_new[0:ND, :], ALU.max).then_inc(tail_dve, 1)

                def diagonal(n):
                    dve.wait_ge(tail_pe, 5 * n + 2)
                    step(dve.reduce_max(small[0:ND, 0:1], ps[0:ND, 3, 0:P], AX))
                    dve.tensor_scalar(diag[0:ND, :], ident[0:ND, 0:ND], small[0:ND, 0:1], None, ALU.mult).then_inc(tail_dve, 1)

                def shift(n):
                    dve.wait_ge(tail_pe, 5 * n + 3)
                    step(dve.tensor_copy(mb, ps[:, 3, 0:ND]))
                    step.mark(dve.tensor_tensor(p_new[0:ND, :], p_new[0:ND, :], mb[0:ND, :], ALU.subtract))
                    dve.tensor_tensor(pd.rearrange("p j q -> p q j"), blocks_of(n), mb.unsqueeze(2).broadcast_to([P, ND, BLK]),
                                      ALU.subtract).then_inc(shifted, 1)

                def sums(n):
                    dve.wait_ge(pd_ready, n + 1)
                    step(dve.tensor_reduce(sm, pd.rearrange("p j q -> p q j"), AX, ALU.add))
                    dve.tensor_tensor(sm[0:ND, :], sm[0:ND, :], p_new[0:ND, :], ALU.add).then_inc(tail_dve, 1)

                def normalise(n):
                    dve.wait_ge(tail_pe, 5 * n + 4)
                    step(dve.reciprocal(small[0:ND, 1:2], ps[0:ND, 3, P:P + 1]))
                    dve.tensor_scalar(d_o[0:ND, :], ps[0:ND, 3, 0:P], small[0:ND, 1:2], None, ALU.mult).then_inc(tail_dve, 1)

                def keep_latent(n):
                    dve.wait_ge(tail_pe, 5 * n + 5)
                    dve.tensor_copy(o_lat[:, :, n, :], ps[:, 3, 0:ND].rearrange("p (h t) -> p h t", h=H)).then_inc(tail_dve, 1)
                    dve.wait_ge(tail_dve, 5 * n + 5)

                for n in range(DB):
                    for g in range(NGR):
                        take_k4(n, g)
                        if n >= 1:
                            if g == 1:
                                diagonal(n - 1)
                            if g == 2:
                                shift(n - 1)
                            if g == 3:
                                sums(n - 1)
                            if g == 5:
                                normalise(n - 1)
                            if g == 6:
                                keep_latent(n - 1)
                    maxima(n)
                for f in (diagonal, shift, sums, normalise, keep_latent):
                    f(DB - 1)
                step.sync()
                step.restart()
                stage_end(dve, 4)
                def add_linear(groups, per, first):
                    def body(i):
                        for j in range(per):
                            dve.wait_ge(lin_done, first + per * i + j + 1)
                            xs = x[:, bass.ds(per * i + j, 1), :].rearrange("p a (c n) -> p (a c) n", c=NCH)
                            dve.tensor_tensor(xs, xs, ps[:, (j % 2) * NCH:(j % 2 + 1) * NCH, 0:CH], ALU.add).then_inc(lin_evac, 1)
                    with dve.Fori(0, groups) as i:
                        body(i)

                add_linear(2, 4, IN_MT)
                stage_end(dve, 5)
                dve.wait_ge(mstd_ready, 1)
                step(dve.reciprocal(mem_r, mem_r))
                for k in range(KT):
                    last = dve.scalar_tensor_tensor(out=mem_n[:, k, :], in0=mem[:, k, :], scalar=gain("g_mem", k), in1=mem_r,
                                                    op0=ALU.mult, op1=ALU.mult)
                last.then_inc(mnorm_ready, 1)
                norm(NCH, KT, x, xn, "g_x", rstd[:, 0, :], CH, NCH, std_ready, norm_ready)
                dve.wait_ge(lin_evac, IN_MT + OUT_MT + XK_MT + 2)
                for j in range(XQ_MT):
                    dve.wait_ge(lin_done, IN_MT + OUT_MT + XK_MT + j + 1)
                    dve.tensor_copy(xq[:, j, 0:TOK].rearrange("p (c n) -> p c n", c=NCH),
                                    ps[:, (j % 2) * NCH:(j % 2 + 1) * NCH, 0:CH]).then_inc(lin_evac, 1)
                step.restart()
                stage_end(dve, 6)

                def x_max(n, p, w):
                    dve.wait_ge(xs_done, n)
                    step(dve.tensor_reduce(xm[0:w, p, 0:4], ps[0:w, 2 * p:2 * p + 2, :].rearrange("p a (h m) -> p (a h) m", h=2),
                                           AX, ALU.max))
                    dve.tensor_scalar(xm[0:w, p, 4:8], xm[0:w, p, 0:4], -X_SCALE, None, ALU.mult).then_inc(xm_ready, 1)

                def x_out(n, p, w, dst):
                    dve.wait_ge(xp_ready, n)
                    step(dve.reciprocal(xm[0:w, p, 0:4], xm[0:w, p, 8:12]))
                    dve.wait_ge(xv_done, n if w == P else NT + 1)
                    dve.tensor_tensor(xon[0:w, p], ps[0:w, 6, :].rearrange("p (h v) -> p h v", h=XH),
                                      xm[0:w, p, 0:4].unsqueeze(2).broadcast_to([w, XH, XHD]), ALU.mult).then_inc(xon_ready, 1)
                    dve.wait_ge(xot_done, n if w == P else NT + 1)
                    dve.tensor_copy(dst, ps[:, 7, 0:XH * w].rearrange("p (h t) -> p h t", h=XH)).then_inc(xot_evac, 1)

                x_max(1, 0, P)
                step.restart()
                with dve.Fori(0, NT // 2) as i:
                    for p in range(2):
                        n = 2 * i + p
                        x_max(n + 2, 1 - p, P)
                        x_out(n + 1, p, P, co[:, :, bass.ds(P * n, P)])
                        step.restart()
                x_max(NT + 2, 1, ND)
                for c in range(2 * XH):
                    if c == 0:
                        dve.wait_ge(dt_done, 1)
                    last = dve.tensor_tensor(d_pt[:, c], ps[:, 4, c * ND:(c + 1) * ND].unsqueeze(1).broadcast_to([P, DB, ND]),
                                             con("colbatch").rearrange("p (b t) -> p b t", b=DB), ALU.mult)
                last.then_inc(dpt_ready, 1)
                x_out(NT + 2, 1, ND, co[:, :, SEQ:TOK])
                step.sync()
                step.restart()
                stage_end(dve, 7)
                add_linear(1, 8, IN_MT + OUT_MT + XK_MT + XQ_MT)
                stage_end(dve, 8)
                dve.memset(lgt[0:NR, TOK:NXQ], 0.0).then_inc(lg_evac, 1)
                norm(2 * NCH, KT, x, xn, "g_ffn", rstd[:, 0, :], CH, NCH, std_ready, norm_ready)
                dve.wait_ge(lt_done, 1)
                step(dve.tensor_copy(lg, ps[:, 3, 0:(NT + 1) * NR].rearrange("p (t e) -> p t e", e=NR)))

                def wide(a, n):
                    return a.unsqueeze(2).broadcast_to([P, NT + 1, n])

                def every(a):
                    return a.unsqueeze(1).broadcast_to([P, NT + 1, a.shape[1]])

                def first_of_max(v, n, m, onehot):
                    step(dve.tensor_reduce(m, v, AX, ALU.max))
                    step(dve.tensor_tensor(onehot, v, wide(m, n), ALU.is_equal))
                    tmp = r_tmp[:, :, 0:n]
                    step(dve.tensor_tensor(tmp, onehot, every(con("iota32")[:, 0:n]), ALU.mult))
                    step(dve.tensor_reduce(r_min, tmp, AX, ALU.min))
                    step(dve.tensor_tensor(onehot, tmp, wide(r_min, n), ALU.is_equal))

                first_of_max(lg[:, :, 0:NG], NG, gm, g_oh)
                step(dve.tensor_tensor(r_exp[:, :, 0:NG], lg[:, :, 0:NG], wide(gm, NG), ALU.subtract))
                step(dve.tensor_scalar(g_oh, g_oh, 1.0, -NEG, ALU.subtract, ALU.mult))
                for g in range(NG):
                    step.mark(dve.tensor_tensor(e_all[:, :, g * EPG:(g + 1) * EPG], lg[:, :, NG + g * EPG:NG + (g + 1) * EPG],
                                                g_oh[:, :, g:g + 1].broadcast_to([P, NT + 1, EPG]), ALU.add))
                step.sync()
                first_of_max(e_all, NE, m1, oh1)
                step(dve.scalar_tensor_tensor(out=e_all, in0=oh1, scalar=NEG, in1=e_all, op0=ALU.mult, op1=ALU.add))
                first_of_max(e_all, NE, m2, oh2)
                dve.tensor_tensor(r_exp[:, :, NG:NG + 1], m2.unsqueeze(2), m1.unsqueeze(2), ALU.subtract).then_inc(rx_in, 1)
                for oh in (oh1, oh2):
                    step.mark(dve.memset(oh[32:64, NT, :], 0.0))
                    step.mark(dve.memset(oh[64:128, NT, :], 0.0))
                step.sync()
                dve.tensor_tensor(both, oh1, oh2, ALU.add).then_inc(both_ready, 1)
                dve.wait_ge(rx_out, 1)
                step.mark(dve.tensor_reduce(g_w, r_exp[:, :, 0:NG], AX, ALU.add))
                step(dve.tensor_scalar(m1, r_exp[:, :, NG], 1.0, None, ALU.add))
                step(dve.tensor_tensor(g_w, g_w, m1, ALU.mult))
                step(dve.reciprocal(gates[:, 0, :], g_w))
                step(dve.tensor_tensor(gates[:, 1, :], gates[:, 0, :], r_exp[:, :, NG], ALU.mult))
                step.mark(dve.memset(cum[:, 0, :], 0.0))
                dve.wait_ge(ranked, 1)
                step.sync()
                for t in range(NT + 1):
                    step(dve.tensor_tensor(cum[:, t + 1, :], cum[:, t, :], ps[:, 5, t * NE:(t + 1) * NE], ALU.add))
                step(dve.tensor_tensor(rank, ps[:, 4, 0:(NT + 1) * NE].rearrange("p (t e) -> p t e", e=NE), cum[:, 0:NT + 1, :], ALU.add))
                step(dve.tensor_tensor(steps8, cum[:, NT + 1, :].unsqueeze(2).broadcast_to([P, NE, 8]),
                                       con("steps128").unsqueeze(1).broadcast_to([P, NE, 8]), ALU.is_gt))
                step(dve.tensor_reduce(nov, steps8, AX, ALU.add))
                step(dve.tensor_tensor_scan(oend, nov, nov, 0.0, ALU.add, ALU.bypass))
                step.mark(dve.tensor_scalar(base, con("iota32"), float(CAP), float(CAP * NE), ALU.mult, ALU.add))
                step(dve.tensor_tensor(jump, oend, nov, ALU.subtract))
                step(dve.tensor_tensor(jump, jump, con("iota32"), ALU.subtract))
                step(dve.tensor_scalar(jump, jump, float(CAP), float(-CAP), ALU.mult, ALU.add))
                step(dve.tensor_scalar(r_tmp, rank, float(CAP), None, ALU.is_ge))
                step(dve.tensor_tensor(r_tmp, r_tmp, every(jump), ALU.mult))
                step(dve.tensor_tensor(rank, rank, r_tmp, ALU.add))
                step(dve.tensor_tensor(rank, rank, every(base), ALU.add))
                for s_, oh in enumerate((oh1, oh2)):
                    step(dve.tensor_tensor(oh, oh, rank, ALU.mult))
                    step(dve.tensor_reduce(r_f[:, s_, :], oh, AX, ALU.add))
                step.mark(dve.tensor_copy(dest[:, :, :], r_f))
                step(dve.tensor_tensor(over_f, oend.unsqueeze(1).broadcast_to([P, OVER, NE]),
                                       con("over").unsqueeze(2).broadcast_to([P, OVER, NE]), ALU.is_le))
                step.mark(dve.tensor_copy(over_c[:, 0:1], oend[:, NE - 1:NE]))
                step(dve.tensor_reduce(over_c[:, 1:1 + OVER], over_f, AX, ALU.add))
                step(dve.tensor_scalar(over_c[:, 1:1 + OVER], over_c[:, 1:1 + OVER], float(NE - 1), None, ALU.min))
                dve.tensor_copy(over_i[:, :], over_c).then_inc(routed, 1)
                step.restart()
                stage_end(dve, 9)

                def take_x(n, p):
                    dve.wait_ge(tx_done, n + 1)
                    dve.tensor_copy(xb_t[:, p].rearrange("p (a k) t -> p a (k t)", a=2), ps[:, 0:2, :]).then_inc(tx_evac, 1)

                def hidden(n):
                    dve.wait_ge(ge_ready, n + 1)
                    step(dve.tensor_scalar(h_e, h_e, 1.0, None, ALU.add))
                    step(dve.reciprocal(h_e, h_e))
                    step(dve.tensor_tensor(h_e, ps[:, 2, 0:DE], h_e, ALU.mult))
                    dve.tensor_tensor(h_b, ps[:, 2, DE:2 * DE], h_e, ALU.mult).then_inc(h_ready, 1)
                    step.restart()

                take_x(0, 0)
                hidden(0)
                take_x(1, 1)
                with dve.Fori(0, NE // 4 - 1) as i:
                    for j in range(1, 5):
                        hidden(4 * i + j)
                        take_x(4 * i + j + 1, (j + 1) % 2)
                for n in range(NE - 3, NE):
                    hidden(n)
                    if n < NE - 1:
                        take_x(n + 1, (n + 1) % 2)
                n_over = dve.value_load(over_i[0:1, 0:1], min_val=0, max_val=OVER)
                with dve.Fori(0, OVER // 4) as i:
                    for j in range(4):
                        with dve.If(n_over > 4 * i + j):
                            take_x(NE + 4 * i + j, j % 2)
                            hidden(NE + 4 * i + j)
                stage_end(dve, 10)
                for t in range(NT + 2):
                    if t <= NT:
                        m = P if t < NT else ND
                        dve.wait_ge(c_half, t + 1)
                        dve.scalar_tensor_tensor(out=comb[0:m, t % 2, :], in0=yg[0:m, t % 4, 1, :], scalar=gates[0:m, 1, t:t + 1],
                                                 in1=comb[0:m, t % 2, :], op0=ALU.mult, op1=ALU.add).then_inc(c_ready, 1)
                    if t >= 1:
                        u = t - 1
                        m = P if u < NT else ND
                        dve.wait_ge(c_done, u + 1)
                        xs = x[:, :, u * P:u * P + m]
                        for f in range(2):
                            xs = x[:, 4 * f:4 * f + 4, u * P:u * P + m]
                            last = dve.tensor_tensor(xs, xs, ps[:, 2 * (u % 2) + f, 0:4 * m].rearrange("p (k t) -> p k t", k=4), ALU.add)
                        last.then_inc(c_added, 1)
                stage_end(dve, 11)
                end_layer(dve, l)
            for c, tok in chunks:
                dve.wait_ge(std_ready, c + 1)
                step(dve.reciprocal(rstd[:, 0, tok], rstd[:, 0, tok]))
                for k in range(KT):
                    last = dve.scalar_tensor_tensor(out=xn[:, k, tok], in0=x[:, k, tok], scalar=gain("g_final", k),
                                                    in1=rstd[:, 0, tok], op0=ALU.mult, op1=ALU.mult)
                last.then_inc(norm_ready, 1)

        @block.gpsimd
        def _(pool):
            step = Steps(pool, pool_step)
            pool.wait_ge(setup, 80)
            step(pool.tensor_copy(page_f[:, :], pages[:, :]))
            step(pool.tensor_scalar(page_f[:, :], page_f[:, :], float(PAGE // KROW), None, ALU.mult))
            step(pool.tensor_tensor(page_f[:, :], page_f[:, :], con("pmod").broadcast_to([P, DB]), ALU.add))
            step.restart()
            step(pool.memset(zeros, 0.0))
            step.restart()
            pool.dma_start(slots.rearrange("(p n) (f c) -> p (n f) c", p=P, c=512),
                           zeros.unsqueeze(1).broadcast_to([P, NBLK * CAP // P * 2, 512])).then_inc(slots_clear, 16)
            with pool.Fori(0, DEPTH) as l:
                pool.wait_ge(vg_done, NT + 1)
                pool.wait_ge(lin_evac, IN_MT + 2)
                pool.wait_ge(pre_full, 48)
                for k in range(2):
                    step.mark(pool.tensor_copy(dbuf[:, k, :, POOL_BUF:POOL_BUF + DT],
                                               pr[:, k, SEQ:TOK].rearrange("p (b t) -> p b t", b=DB)))
                u = pr[:, 0:2, :]
                a, b2 = psum_a, psum_b
                da, d2 = dsum[:, 0], dsum[:, 1]
                E = POOL_BUF + DT
                step.mark(pool.tensor_copy(a[:, :, 0:1], u[:, :, 0:1]))
                step(pool.tensor_tensor(a[:, :, 1:SEQ], u[:, :, 1:SEQ], u[:, :, 0:SEQ - 1], ALU.add))
                step.mark(pool.tensor_copy(b2[:, :, 0:2], a[:, :, 0:2]))
                step(pool.tensor_tensor(b2[:, :, 2:SEQ], a[:, :, 2:SEQ], a[:, :, 0:SEQ - 2], ALU.add))
                step.mark(pool.tensor_copy(a[:, 1, 0:4], b2[:, 1, 0:4]))
                step(pool.tensor_tensor(a[:, 1, 4:SEQ], b2[:, 1, 4:SEQ], b2[:, 1, 0:SEQ - 4], ALU.add))
                step.mark(pool.tensor_copy(b2[64:128, 1, 0:8], a[64:128, 1, 0:8]))
                step(pool.tensor_tensor(b2[64:128, 1, 8:SEQ], a[64:128, 1, 8:SEQ], a[64:128, 1, 0:SEQ - 8], ALU.add))
                for k in range(2):
                    step.mark(pool.tensor_tensor(da[:, k, :, 1:E], dbuf[:, k, :, 1:E], dbuf[:, k, :, 0:E - 1], ALU.add))
                step.sync()
                for k in range(2):
                    step.mark(pool.tensor_tensor(d2[:, k, :, 3:E], da[:, k, :, 3:E], da[:, k, :, 1:E - 2], ALU.add))
                step.sync()
                step(pool.tensor_tensor(da[:, 1, :, 7:E], d2[:, 1, :, 7:E], d2[:, 1, :, 3:E - 4], ALU.add))
                step(pool.tensor_tensor(d2[64:128, 1, :, 15:E], da[64:128, 1, :, 15:E], da[64:128, 1, :, 7:E - 8], ALU.add))
                groups = ((slice(0, 64), 0, a, da), (slice(64, 128), 0, b2, d2), (slice(0, 64), 1, a, da), (slice(64, 128), 1, b2, d2))
                fix = con("pool_fix").rearrange("p (k n) -> p k n", k=2)
                for rows, k, s_, _ in groups:
                    step.mark(pool.tensor_tensor(s_[rows, k, 0:16], s_[rows, k, 0:16], fix[rows, k, :], ALU.mult))
                step.sync()
                inv = con("pool_inv")
                fresh = [ds_[rows, k, :, POOL_BUF:E] for rows, k, _, ds_ in groups]
                for (rows, k, s_, _), f in zip(groups, fresh):
                    step.mark(pool.tensor_scalar(s_[rows, k, 0:SEQ], s_[rows, k, 0:SEQ], inv[rows, k:k + 1], None, ALU.mult))
                    step.mark(pool.tensor_scalar(f, f, inv[rows, k:k + 1], None, ALU.mult))
                step.sync()
                for (rows, k, s_, _), f in zip(groups, fresh):
                    step.mark(pool.tensor_tensor(a[rows, k, 0:SEQ], s_[rows, k, 0:SEQ], u[rows, k, 0:SEQ], ALU.subtract))
                    last = pool.tensor_tensor(a[rows, k, SEQ:TOK].rearrange("p (b t) -> p b t", b=DB), f,
                                              dbuf[rows, k, :, POOL_BUF:E], ALU.subtract)
                last.then_inc(pooled, 1)
                step.sync()
                step.restart()
                stage_end(pool, 1)

                step.mark(pool.memset(q_dec[:, :, :], 0.0))
                step.mark(pool.memset(qpe_dec[:, :, :, :], 0.0))
                pool.memset(v_h[:, :, :, 64:128], 1.0).then_inc(zeroed, 1)

                def copy_v(p, h):
                    step(pool.tensor_copy(v_h[:, p, 0:4, 0:64], vv[0][:, :, bass.ds(VD * h, VD)]))
                    pool.tensor_copy(v_h[:, p, 4:8, 0:64], vv[1][:, :, bass.ds(VD * h, VD)]).then_inc(v_ready, 1)

                def rope_q(p, n):
                    pool.wait_ge(v_ready, n)
                    pool.wait_ge(qswap_full, 32 * n)
                    step(pool.tensor_tensor(q_h[64:96, p, :], q_h[64:96, p, :], rope[64:96, 0, :], ALU.mult))
                    step(pool.tensor_tensor(qswap[64:96, :], qswap[64:96, :], rope[64:96, 1, :], ALU.mult))
                    pool.tensor_tensor(q_h[64:96, p, :], q_h[64:96, p, :], qswap[64:96, :], ALU.add).then_inc(q_rope, 1)

                pool.wait_ge(zeroed, 1)
                copy_v(0, 0)
                rope_q(0, 1)
                step.restart()
                with pool.Fori(0, H // 2) as i:
                    for p in range(2):
                        pool.wait_ge(y_done, 4 * i + 2 * p)
                        pool.wait_ge(q_rope, 2 * i + p + 1)
                        copy_v(1 - p, (2 * i + p + 1) % H)
                        rope_q(1 - p, 2 * i + p + 2)
                        step.restart()
                stage_end(pool, 2)

                scale_mask = con("headmask").unsqueeze(2).broadcast_to([P, GH, P])

                def prepare(n, p, cols):
                    q, k = pr[:, 6, cols], pr[:, 7, cols]
                    pool.tensor_tensor(g_q0[:, p], q.unsqueeze(1).broadcast_to([P, GH, P]), scale_mask, ALU.mult).then_inc(g_spread, 1)
                    pool.wait_ge(g_exp, n)
                    pool.wait_ge(g_spread, n)
                    for lv in range(DSPLIT):
                        step(pool.tensor_tensor(g_q[:, p, lv], g_e[:, lv, :].unsqueeze(1).broadcast_to([P, GH, P]), g_q0[:, p], ALU.mult))
                    step(pool.tensor_tensor(g_k[p], g_e, k.unsqueeze(1).broadcast_to([P, NL, P]), ALU.mult))
                    step(pool.tensor_tensor(g_kt[:, p, :], g_ek, k, ALU.mult))
                    pool.tensor_tensor(g_qe[:, p, :], g_eb, q, ALU.mult).then_inc(g_pool, 1)

                prepare(1, 0, slice(0, P))
                step.restart()
                with pool.Fori(0, NT // 2) as i:
                    for p in range(2):
                        n = 2 * i + p
                        pool.wait_ge(g_pool, n + 1)
                        pool.wait_ge(at_done, 16 * i + 8 * p)
                        pool.wait_ge(o_done, n)
                        prepare(n + 2, 1 - p, bass.ds(((n + 1) % NT) * P, P))
                        step.restart()
                pool.wait_ge(at_done, NL * NT)
                pool.wait_ge(g_dve, NT + 1)
                pool.wait_ge(g_pool, NT + 1)
                pool.memset(d_state, 0.0).then_inc(ds_clear, 1)
                stage_end(pool, 3)

                step(pool.tensor_copy(page_i[:, :], page_f[:, :]))
                for n in range(DB):
                    if n >= NSLOT:
                        pool.wait_ge(tail_pe, 5 * (n - NSLOT) + 4)
                    for dst, cache in ((ck[n % NSLOT], "cache_ckv"), (kr_c[n % NSLOT], "cache_kpe")):
                        pool.indirect_dma_start(dst.rearrange("p j c -> p (j c)"), None,
                                                ins[cache].rearrange("l n (q k) c -> (l n q) (k c)", k=KROW),
                                                bass.IndirectOffsetOnAxis(ap=page_i[:, n:n + 1], axis=0)).then_inc(ck_full[n % NSLOT], 16)
                for j in range(NSLOT):
                    pool.wait_ge(ck_full[j], 32 * (DB // NSLOT))
                step(pool.tensor_scalar(page_f[:, :], page_f[:, :], float(NPHYS * PAGE // KROW), None, ALU.add))
                step.restart()
                stage_end(pool, 4)
                stage_end(pool, 5)
                step(pool.memset(xq[:, :, TOK:NXQ], 0.0))
                stage_end(pool, 6)
                pool.tensor_copy(qt[:, 0], xq[:, :, 0:P]).then_inc(qt_ready, 1)
                with pool.Fori(0, NT // 2) as i:
                    for p in range(2):
                        n = 2 * i + p
                        pool.wait_ge(qt_ready, n + 1)
                        pool.wait_ge(xs_done, n)
                        pool.tensor_copy(qt[:, 1 - p], xq[:, :, bass.ds(P * (n + 1), P)]).then_inc(qt_ready, 1)
                pool.wait_ge(qt_ready, NT + 1)
                for h in range(XH):
                    step(pool.tensor_tensor(d_qm[:, h], xq[:, h, SEQ:TOK].unsqueeze(1).broadcast_to([P, DB, ND]),
                                            con("colbatch").rearrange("p (b t) -> p b t", b=DB), ALU.mult))
                pool.memset(xm[:, 0, 12:13], 0.0).then_inc(qt_ready, 1)
                step.restart()
                stage_end(pool, 7)
                stage_end(pool, 8)
                pool.wait_ge(slots_clear, 16)
                pool.wait_ge(routed, 1)
                for t in range(NT + 1):
                    m = P if t < NT else ND
                    pool.wait_ge(xr_evac, t + 1)
                    for s_ in range(2):
                        pool.indirect_dma_start(slots, bass.IndirectOffsetOnAxis(ap=dest[0:m, s_, t:t + 1], axis=0),
                                                xr[0:m, t % 4, :], None).then_inc(row_moved[t % 4], 16)
                for j in range(4):
                    pool.wait_ge(row_moved[j], 32 * ((NT - j) // 4 + 1))
                pool.sem_inc(rows_ready, 1)
                stage_end(pool, 9)
                stage_end(pool, 10)
                for t in range(NT + 1):
                    m = P if t < NT else ND
                    if t >= 4:
                        pool.wait_ge(c_ready, t - 3)
                    for s_ in range(2):
                        pool.indirect_dma_start(yg[0:m, t % 4, s_, :], None, slots,
                                                bass.IndirectOffsetOnAxis(ap=dest[0:m, s_, t:t + 1], axis=0)).then_inc(row_moved[t % 4], 16)
                stage_end(pool, 11)
                end_layer(pool, l, clears=True)


_INS = ("x", "ring", "wvg", "wpool", "wgk", "wuv", "w_h", "vec", "consts", "rope", "lmask", "pool_prev", "pool_old", "state_gla", "pages", "cache_ckv", "cache_kpe", "mem", "wxv", "mem_k", "mem_v", "w_r", "w_e")
_OUTS = (("y", (P, KT, TOK)), ("ckv", (DEPTH, P, TOK)), ("kpe", (DEPTH, ROPE, TOK)), ("pool_p", (DEPTH, POOL_BUF, GW)),
         ("pool_s", (DEPTH, DB, POOL_BUF, GW)), ("gla_p", (DEPTH, GH, GK, GV)), ("gla_s", (DEPTH, DB, GH, GK, GV)),
         ("mk", (DEPTH, P, XH, NMEM)), ("mv", (DEPTH, P, 2, XH * XHD)))


def layout(i):
    L = DEPTH
    f = {n: np.asarray(a) for n, a in i.items()}
    o = {}

    def tiles(w, m=P):
        l_, k_, m_ = w.shape
        return w.reshape(l_, k_ // P, P, m_ // m, m).transpose(0, 3, 2, 1, 4)

    xs = np.concatenate([f["x_prompt"].reshape(SEQ, D), f["x_sample"].reshape(ND, D)])
    o["x"] = xs.T.reshape(KT, P, TOK).transpose(1, 0, 2)
    w = f["w_in"]
    at = np.cumsum([0, 256, 256, 128, ROPE, 128, 128, GW, 16, GW])
    u, cq, ckv, kpe, gq, gk, gv, ga, go = (w[:, :, a:b] for a, b in zip(at[:-1], at[1:]))
    z = np.zeros((L, D, 48), w.dtype)
    mixed = np.concatenate([ga, z, kpe, z[:, :, :32]], 2)
    w_a = np.concatenate([u, cq, ckv, mixed, gq, gk], 2)
    xo = tiles(f["w_xo"]).reshape(L, 4, 2, P, 4, P).transpose(0, 1, 3, 2, 4, 5).reshape(L, 4, P, KT, P)
    o["ring"] = np.concatenate([tiles(w_a), tiles(f["w_out"]), tiles(f["w_xk"]), tiles(f["w_xq"]), xo], 1)
    o["wvg"] = tiles(np.concatenate([gv, go], 2), 512)[:, 0]
    wp = np.zeros((L, P, 2, P), w.dtype)
    for g in range(4):
        r = slice(64 * (g % 2), 64 * (g % 2) + 64)
        wp[:, r, g // 2, r] = f["w_pool"][:, g]
    o["wpool"] = wp
    o["wgk"] = f["w_gk2"]
    o["wuv"] = f["w_uv"].reshape(L, P, H * VD)
    wh = np.zeros((L, H + 2, P, 384), w.dtype)
    uq = f["w_uq"].reshape(L, 2, P, H, QK).transpose(0, 3, 2, 1, 4)
    wh[:, :H, :, 0:192] = uq.reshape(L, H, P, 192)
    wh[:, :H, :, 192:256] = f["w_uk"].transpose(0, 2, 1, 3)
    wh[:, :H, 0:NOPE, 256:384] = f["w_uk"].transpose(0, 2, 3, 1)
    wh[:, H:] = wh[:, 0:2]
    o["w_h"] = wh
    v = np.zeros((L, P, NVEC), w.dtype)

    def put(name, a):
        at, n = _v[name]
        a = np.broadcast_to(a.reshape(-1, a.shape[-1]), (L, a.shape[-1]))
        v[:, :, at:at + n] = a.reshape(L, n, P).transpose(0, 2, 1)

    for n in ("g_mix", "g_x", "g_ffn", "g_mem", "g_qn", "g_kvn", "b_gk", "pool_scale", "g_final"):
        put(n, f[n])
    put("g_gla", np.concatenate([f["g_gla"], f["g_gla"]], 1))
    put("b_r", np.concatenate([f["b_rg"], f["b_re"], np.zeros((L, P - NG - NE), w.dtype)], 1))
    o["vec"] = v
    o["consts"], o["rope"], o["lmask"] = constants()
    o["pool_prev"] = f["state_pool"].reshape(L, DB, POOL_BUF, 2, P).transpose(0, 4, 3, 1, 2)
    o["pool_old"] = f["state_pool"]
    o["state_gla"] = f["state_gla"]
    o["pages"] = np.repeat(f["page_table"].T, P // PAGES, axis=0)
    o["cache_ckv"], o["cache_kpe"] = f["cache_ckv"], f["cache_kpe"]
    o["mem"] = f["mem_prompt"][0].T.reshape(KT, P, NMEM).transpose(1, 0, 2)
    o["wxv"] = tiles(f["w_xv"], 512)[:, 0]
    o["mem_k"] = f["cache_mem_k"].transpose(0, 1, 4, 3, 2)
    o["mem_v"] = f["cache_mem_v"]
    o["w_r"] = np.concatenate([f["w_rg"], f["w_re"]], 2).reshape(L, KT, P, NR).transpose(0, 2, 1, 3)
    gu = np.concatenate([f["w_eg"], f["w_eu"]], 3).reshape(L, NE, KT, P, 2 * DE).transpose(0, 1, 3, 2, 4).reshape(L, NE, P, -1)
    o["w_e"] = np.concatenate([gu, f["w_ed"].reshape(L, NE, 2, P, D).transpose(0, 1, 3, 2, 4).reshape(L, NE, P, -1)], 3)
    return {n: np.ascontiguousarray(a) for n, a in o.items()}


def kernel(**inputs):
    import concourse.bacc as bacc
    from concourse.bass_utils import run_bass_kernel_spmd

    nc = bacc.Bacc("TRN2", target_bir_lowering=False, num_devices=1)
    arrays, ins, outs = {}, {}, {}
    for name, a in layout(inputs).items():
        arrays["in_" + name] = a
        ins[name] = nc.dram_tensor("in_" + name, a.shape, mybir.dt.from_np(a.dtype), kind="ExternalInput").ap()
    for name, shape in _OUTS:
        outs[name] = nc.dram_tensor("out_" + name, shape, F32, kind="ExternalOutput").ap()
    build(nc, ins, outs)
    r = run_bass_kernel_spmd(nc, [arrays], core_ids=[0]).results[0]
    o = {name: np.asarray(r["out_" + name]) for name, _ in _OUTS}
    y = o["y"].transpose(2, 1, 0).reshape(TOK, D)
    ckv, kpe = o["ckv"].transpose(0, 2, 1), o["kpe"].transpose(0, 2, 1)
    mk = o["mk"].transpose(0, 3, 2, 1).reshape(DEPTH, 1, NMEM, XH, XHD)
    mv = o["mv"].transpose(0, 2, 1, 3).reshape(DEPTH, 1, NMEM, XH, XHD)
    got = (y[:SEQ].reshape(1, SEQ, D), y[SEQ:].reshape(DB, DT, D),
           ckv[:, :SEQ].reshape(DEPTH, 1, SEQ, P), kpe[:, :SEQ].reshape(DEPTH, 1, SEQ, ROPE),
           o["pool_p"].reshape(DEPTH, 1, POOL_BUF, GW), o["gla_p"].reshape(DEPTH, 1, GH, GK, GV), mk, mv,
           ckv[:, SEQ:].reshape(DEPTH, DB, DT, P), kpe[:, SEQ:].reshape(DEPTH, DB, DT, ROPE), o["pool_s"], o["gla_s"])
    return tuple(np.ascontiguousarray(a) for a in got)
```

```python
from contextlib import ExitStack

import numpy as np

import concourse.bass as bass
from concourse import mybir

F32 = mybir.dt.float32
I32 = mybir.dt.int32
U8 = mybir.dt.uint8
ALU = mybir.AluOpType
ACT = mybir.ActivationFunctionType
AX = mybir.AxisListType.X

P = 128
DEPTH, D, SEQ, DB, DT = 2, 1024, 1024, 8, 4
KT = D // P
ND = DB * DT
TOK = SEQ + ND
NCH = 3
CH = TOK // NCH
NT = SEQ // P
EPS = 1e-6
H, NOPE, ROPE, VD = 8, 64, 32, 64
QK = NOPE + ROPE
MLA_SCALE = float(QK) ** -0.5
GH, GK, GV = 4, 32, 64
GW = GH * GV
LEVELS = (64, 32, 16, 8, 4, 2, 1)
POOL_BUF = 15
WINDOWS = (2, 4, 8, 16)
PAGES, PAGE = 32, 128
PAST = PAGES * PAGE
KROW = 32
BLK = PAST // P
XH, XHD, NMEM = 4, 128, 256
X_SCALE = float(XHD) ** -0.5
NG, EPG, NE, DE = 4, 8, 32, 256
CAP = 128
OVER = 16
NBLK = NE + OVER
WE = KT * 2 * DE + DE // P * D
NR = NG + NE
NEG = -1e30
SCRATCH = 6640
DSPLIT = 5
NSLOT, NGR = 4, BLK // 4
NPHYS = 320
NXQ = (NT + 1) * P
LOG_SCALE = float(np.log(GK ** -0.5))

IN_MT, OUT_MT, XK_MT, XQ_MT, XO_MT = 8, 8, 4, 4, 8
RING = 4
RING_USES = IN_MT + OUT_MT + XK_MT + XQ_MT + XO_MT // 2

_c = {}
_at = 0
for _n, _w in (("ident", 128), ("ones", 128), ("causal", 128), ("below", 128), ("headmask", GH), ("bdmask", GW),
               ("newmask", DB * ND), ("rowbatch", DB), ("colbatch", DB * ND), ("pool_inv", 2), ("pool_fix", 32),
               ("iota32", 32), ("steps128", 8), ("pmod", 1), ("over", OVER)):
    _c[_n] = (_at, _w)
    _at += _w
NCONST = _at

_v = {}
_at = 0
for _n, _w in (("g_mix", 8), ("g_x", 8), ("g_ffn", 8), ("g_mem", 8), ("g_qn", 2), ("g_kvn", 1), ("b_gk", 1),
               ("pool_scale", 2), ("g_gla", 1), ("b_r", 1), ("g_final", 8)):
    _v[_n] = (_at, _w)
    _at += _w
NVEC = _at


def constants():
    c = np.zeros((P, NCONST), np.float32)

    def put(name, a):
        at, w = _c[name]
        c[:, at:at + w] = np.asarray(a, np.float32).reshape(-1, w) if np.ndim(a) == 2 else a

    i = np.arange(P)
    put("ident", np.eye(P))
    put("ones", 1.0)
    put("causal", np.where(i[None, :] <= i[:, None], 0.0, NEG))
    put("below", (i[:, None] < i[None, :]).astype(np.float32))
    put("headmask", (i[:, None] // GK == np.arange(GH)[None, :]) * np.float32(GK ** -0.5))
    put("bdmask", (i[:, None] // GK == np.arange(GW)[None, :] // GV).astype(np.float32))
    key = np.arange(P)[:, None, None]
    b = np.arange(DB)[None, :, None]
    t = (np.arange(ND) % DT)[None, None, :]
    ok = (key // DT == b) & (key % DT <= t) & (key < ND)
    put("newmask", np.where(ok, 0.0, NEG).reshape(P, -1))
    put("rowbatch", (i[:, None] // DT == np.arange(DB)[None, :]).astype(np.float32))
    col = (np.arange(ND)[None, :] // DT == np.arange(DB)[:, None]).astype(np.float32)
    put("colbatch", np.broadcast_to(col.reshape(1, -1), (P, DB * ND)))
    w = np.array([[WINDOWS[2 * k + p // 64] for k in range(2)] for p in range(P)], np.float32)
    put("pool_inv", 1.0 / w)
    n = np.arange(1, 17, dtype=np.float32)[None, None, :]
    put("pool_fix", (w[:, :, None] / np.minimum(n, w[:, :, None])).reshape(P, -1))
    put("iota32", np.broadcast_to(np.arange(NE)[None, :] - NE, (P, NE)))
    put("steps128", np.broadcast_to(128.0 * np.arange(1, 9)[None, :], (P, 8)))
    put("pmod", (i % (P // PAGES))[:, None])
    put("over", np.broadcast_to(np.arange(OVER)[None, :], (P, OVER)))
    pos = np.concatenate([np.arange(SEQ), PAST + np.arange(ND) % DT]).astype(np.float32)
    half = ROPE // 2
    inv = np.float32(10000.0) ** (-np.arange(half, dtype=np.float32) * np.float32(2.0) / np.float32(ROPE))
    ang = (pos[None, :] * inv[:, None].astype(np.float32)).astype(np.float32)
    cos, sin = np.cos(ang), np.sin(ang)
    rope = np.stack([np.concatenate([cos, cos]), np.concatenate([-sin, sin])], 1).astype(np.float32)
    s, t = np.arange(P)[:, None], np.arange(P)[None, :]
    masks = [((s // (2 * z) == t // (2 * z)) & (s % (2 * z) < z) & (t % (2 * z) >= z)) for z in LEVELS]
    return c, rope, np.stack(masks, 1).astype(np.float32)


def build(nc, ins, outs):
    with ExitStack() as ctx:
        def sb(name, shape, dt=F32):
            return ctx.enter_context(nc.sbuf_tensor(name, shape, dt))

        sems = []

        def sem(name):
            s = ctx.enter_context(nc.semaphore(name))
            sems.append(s)
            return s

        x = sb("x", [P, KT, TOK])
        ring = sb("ring", [P, RING, KT, P])
        consts = sb("consts", [P, NCONST])
        rope = sb("rope", [P, 2, TOK])
        lmask = sb("lmask", [P, len(LEVELS), P], U8)
        vec = sb("vec", [P, NVEC])
        W = KT * TOK
        pages, page_i, page_f = sb("pages", [P, DB], I32), sb("page_i", [P, DB], I32), sb("page_f", [P, DB])
        nmax = sb("nmax", [P, 2, 2])
        gates, dest = sb("gates", [P, 2, NT + 1]), sb("dest", [P, 2, NT + 1], I32)
        over_i = sb("over_i", [P, 1 + OVER], I32)
        slots = nc.dram_tensor("slots", [NBLK * CAP, D], F32).ap()
        arena = sb("arena", [P, 3 * W + (NT + 1) * 512 + SCRATCH])
        ps = ctx.enter_context(nc.psum_tensor("ps", [P, 8, 512], F32))

        def view(at, *shape):
            n = int(np.prod(shape))
            v = arena[:, at:at + n]
            names = [f"a{k}" for k in range(len(shape))]
            if len(shape) == 1:
                return v
            return v.rearrange(f"p ({' '.join(names)}) -> p {' '.join(names)}",
                               **{n_: s for n_, s in zip(names[1:], shape[1:])})

        MIX, XN, PR, VG = 0, W, 2 * W, 3 * W
        SC = 3 * W + (NT + 1) * 512

        def con(name, rows=P):
            at, w = _c[name]
            return consts[0:rows, at:at + w]

        def gain(name, k=0, rows=P):
            at, _ = _v[name]
            return vec[0:rows, at + k:at + k + 1]

        ident, ones = con("ident"), con("ones")
        mix = view(MIX, KT, TOK)
        rstd = view(MIX + 6 * TOK, 2, TOK)
        recip = rope[0:64, 0, 0:512]
        xn = view(XN, KT, TOK)
        lmask_f = view(XN, len(LEVELS), P)
        sq = view(PR, KT, TOK)
        pr = view(PR, KT, TOK)
        vg = view(VG, NT + 1, 512)
        wvg = view(SC, KT, 512)
        sq2 = view(VG, 3, TOK)
        psum_a, psum_b = view(MIX, 2, TOK), view(PR + 6 * TOK, 2, TOK)
        dbuf = view(MIX + 7 * TOK, 2, DB, POOL_BUF + DT)
        dsum = view(MIX + 7 * TOK + 304, 2, 2, DB, POOL_BUF + DT)
        wpool = view(SC, 2, P)
        wgk = view(MIX + 4928, P)
        q_h = view(XN, 2, TOK)
        k_h = view(XN + 2 * TOK, 2, TOK)
        v_h = view(XN + 4 * TOK, 2, NT, P)
        prob = view(XN + 4 * TOK + 2048, 2, SEQ)
        q_dec = view(SC, DB, 224)
        qpe_dec = view(SC + 1792, DB, 4, ND)
        qpe_new = view(SC + 2816, DB, ND)
        S2 = SC + 3072
        qswap = view(S2, TOK)
        pt = view(S2 + TOK, 2, 512)
        w_h = view(S2 + TOK + 1024, 2, 384)
        kswap = view(VG + 3 * TOK, TOK)
        vv = [view(PR, 4, 512), view(MIX + 6 * TOK, 4, 512)]
        wuv = view(S2 + TOK + 1024 + 768, 512)
        keep = S2 + TOK + 1024 + 768 + 512
        ckv_new, kr_new, ckv_tok = view(keep, ND), view(keep + 32, ND), view(keep + 64, P)
        u_out = view(MIX + 2 * TOK + (NT + 1) * GW, 2, GW)
        kr = view(MIX + 5 * TOK, TOK)
        silu = view(MIX + 2 * TOK, NT + 1, GW)
        la = pr[:, 5, :]
        la_t = view(SC + 3072 + TOK, TOK)

        NL = len(LEVELS) + 1
        g_q = view(XN, 2, NL - 1, GH, P)
        g_k = [view(XN + 2 * (NL - 1) * GH * P, NL, P), view(PR, NL, P)]
        state = view(XN + 8192, GW)
        g_q0 = view(PR + 1024, 2, GH, P)
        g_att = view(PR + 2 * TOK, 2, GH, P)
        g_e = view(PR + 2 * TOK + 1024, 2, NL, P)
        g_b = view(S2, 2, P)
        g_eb, g_ek = ([view(S2 + at + k, P) for at in (256, 2336)] for k in (0, P))
        g_qe, g_kt, g_ktt = view(S2 + 512, 2, P), view(S2 + 768, 2, P), view(S2 + 1024, 2, P)
        g_o, g_sq, g_tmp = view(S2 + 1280, 2, GW), view(S2 + 1792, GW), view(S2 + 2048, GW)
        g_last, g_ms = view(S2 + 2304, 2, DB), view(S2 + 2320, 2, GH)
        d_state, d_qe, d_kt = view(XN + 3584, DB, GW), view(XN + 5632, DB, ND), view(XN + 5888, DB, P)

        ck = [view(XN + j * 5120, BLK, P) for j in range(NSLOT)]
        kr_c = [view(XN + j * 5120 + 4096, BLK, ROPE) for j in range(NSLOT)]
        ct, k4 = view(S2, 2, 512), view(S2 + 1024, 2, P)
        pd = view(S2 + 1280, BLK, ND)
        mx, diag, mb, sm, p_new = (view(S2 + 2304 + 32 * k, ND) for k in range(5))
        small, d_o, o_lat = nmax[:, 0, :], view(S2 + 2464, P), view(S2 + 2592, H, DB, DT)
        mem, mem_n, mem_sq = view(VG, KT, NMEM), view(VG + 2048, KT, NMEM), view(SC + 4096, KT, NMEM)
        wxv = view(SC, KT, 512)
        xq, mk = view(MIX, XH, TOK), view(MIX + XH * NXQ, XH, NMEM)
        mem_r, mv = view(SC + 6144, NMEM), view(MIX + 7 * TOK, 2, 512)
        qt, xon = view(XN, 2, XH, P), view(XN + 1024, 2, XH, XHD)
        kd, vd = view(XN + 2048, 2, XH, NMEM), view(XN + 4096, 2, 2, 512)
        d_qm = view(XN + 6144, XH, DB, ND)
        co = view(PR, XH, TOK)
        px, pxt = view(PR + 4 * TOK, 2, XH, NMEM), view(PR + 4 * TOK + 2048, 2, 2, 512)
        d_pt = view(VG, 2 * XH, DB, ND)
        xm = view(SC, 2, 16)

        w_r = view(SC, KT, NR)
        lgt = view(SC + 288, NXQ)
        R = SC + 288 + NXQ
        lg = view(R, NT + 1, NR)
        e_all, oh1, oh2, both, r_tmp, rank = (view(R + 324 + 288 * k, NT + 1, NE) for k in range(6))
        cum = view(R + 2052, NT + 2, NE)
        r_exp, g_oh = view(R + 2372, NT + 1, NG + 1), view(R + 2420, NT + 1, NG)
        gm, r_min, m1, m2, g_w = (view(R + 2456 + 9 * k, NT + 1) for k in range(5))
        nov, oend, base, jump = (view(R + 2504 + 32 * k, NE) for k in range(4))
        steps8, over_f = view(R + 2632, NE, 8), view(R + 2632, OVER, NE)
        r_f, over_c = view(R + 3144, 2, NT + 1), view(R + 3162, 1 + OVER)
        xr = view(VG, 4, D)
        w_e = [view(j * WE, WE) for j in range(4)]
        xb, xb_t, y_sb = view(VG, 2, D), view(VG + 2 * D, 2, KT, P), view(VG + 4 * D, 2, D)
        h_e, h_b, h_t = view(VG + 6 * D, DE), view(VG + 6 * D + DE, DE), view(VG + 6 * D + 2 * DE, 2, 2, P)
        zeros = vg[:, NT, :]
        yg, comb = view(MIX, 4, 2, D), view(XN, 2, D)
        assert R + 3200 <= SC + SCRATCH and 4 * WE <= VG

        slots_clear = ctx.enter_context(nc.semaphore("slots_clear"))
        next_layer = ctx.enter_context(nc.semaphore("next_layer"))
        setup = ctx.enter_context(nc.semaphore("setup"))
        y_stored = ctx.enter_context(nc.semaphore("y_stored"))
        layer_done = sem("layer_done")
        stage_done = sem("stage_done")
        std_ready, lat_std, turn = sem("std_ready"), sem("lat_std"), sem("turn")
        ring_full = [sem(f"ring_full{j}") for j in range(RING)]
        vec_full, dbuf_full = sem("vec_full"), sem("dbuf_full")
        sq_ready, ssq_ready, norm_ready = sem("sq_ready"), sem("ssq_ready"), sem("norm_ready")
        lin_done, lin_evac = sem("lin_done"), sem("lin_evac")
        act_step, dve_step, pool_step = sem("act_step"), sem("dve_step"), sem("pool_step")
        wvg_full, vg_done, vg_evac = sem("wvg_full"), sem("vg_done"), sem("vg_evac")
        lat_sq, lat_ssq, lat_norm = sem("lat_sq"), sem("lat_ssq"), sem("lat_norm")
        pre_full, kswap_full, kr_ready = sem("pre_full"), sem("kswap_full"), sem("kr_ready")
        z_done, z_evac, gate_e = sem("z_done"), sem("z_evac"), sem("gate_e")
        zeroed = sem("zeroed")
        pooled, pool_mm = sem("pooled"), sem("pool_mm")
        vv_done, vv_evac, wuv_full = sem("vv_done"), sem("vv_evac"), sem("wuv_full")
        utr_done, utr_evac, states_stored = sem("utr_done"), sem("utr_evac"), sem("states_stored")
        w_full = [sem(f"w_full{j}") for j in range(2)]
        s_done, nmax_ready, p_ready = sem("s_done"), sem("nmax_ready"), sem("p_ready")
        tp_done = sem("tp_done")
        tp_free = [sem(f"tp_free{j}") for j in range(2)]
        qswap_full, q_rope, v_ready = sem("qswap_full"), sem("q_rope"), sem("v_ready")
        y_done, y_free = sem("y_done"), sem("y_free")

        g_sub, g_exp, g_pool, g_dve = sem("g_sub"), sem("g_exp"), sem("g_pool"), sem("g_dve")
        at_done, at_free, g_spread = sem("at_done"), sem("at_free"), sem("g_spread")
        kt_done, kt_evac, st_done, st_ready = sem("kt_done"), sem("kt_evac"), sem("st_done"), sem("st_ready")
        o_done, o_evac, o_sum, o_root, o_norm = sem("o_done"), sem("o_evac"), sem("o_sum"), sem("o_root"), sem("o_norm")
        ot_done, ot_evac, ds_full = sem("ot_done"), sem("ot_evac"), sem("ds_full")
        ds_clear, dkt_ready = sem("ds_clear"), sem("dkt_ready")
        tok_done, tok_evac = sem("tok_done"), sem("tok_evac")
        ct_done, ct_evac, k4_done, k4_evac = sem("ct_done"), sem("ct_evac"), sem("k4_done"), sem("k4_evac")
        sc_done, shifted, pd_ready = sem("sc_done"), sem("shifted"), sem("pd_ready")
        tail_pe, tail_dve = sem("tail_pe"), sem("tail_dve")
        ck_full = [sem(f"ck_full{j}") for j in range(NSLOT)]
        mem_full, wxv_full, msq_ready, mssq_ready = sem("mem_full"), sem("wxv_full"), sem("msq_ready"), sem("mssq_ready")
        mstd_ready, mnorm_ready, mv_done, mv_evac = sem("mstd_ready"), sem("mnorm_ready"), sem("mv_done"), sem("mv_evac")
        qt_ready = sem("qt_ready")
        xs_done, xm_ready, xp_ready = sem("xs_done"), sem("xm_ready"), sem("xp_ready")
        xt_done, xt_evac, xv_done = sem("xt_done"), sem("xt_evac"), sem("xv_done")
        xon_ready, xot_done, xot_evac = sem("xon_ready"), sem("xot_done"), sem("xot_evac")
        dt_done, dpt_ready = sem("dt_done"), sem("dpt_ready")
        kd_full, vd_full = [sem(f"kd_full{j}") for j in range(2)], [sem(f"vd_full{j}") for j in range(2)]
        kd_used, vd_used = sem("kd_used"), sem("vd_used")
        wr_full, lg_done, lg_evac, lt_done = sem("wr_full"), sem("lg_done"), sem("lg_evac"), sem("lt_done")
        rx_in, rx_out = sem("rx_in"), sem("rx_out")
        both_ready, ranked, routed = sem("both_ready"), sem("ranked"), sem("routed")
        xr_done, xr_evac, rows_ready = sem("xr_done"), sem("xr_evac"), sem("rows_ready")
        row_moved = [sem(f"row_moved{j}") for j in range(4)]
        we_full, xb_full, y_sent = [sem(f"we_full{j}") for j in range(4)], [sem(f"xb_full{j}") for j in range(2)], [sem(f"y_sent{j}") for j in range(2)]
        tx_done, tx_evac, gu_done, ge_ready, h_ready = sem("tx_done"), sem("tx_evac"), sem("gu_done"), sem("ge_ready"), sem("h_ready")
        ht_done, ht_evac, dn_done, dn_evac = sem("ht_done"), sem("ht_evac"), sem("dn_done"), sem("dn_evac")
        c_half, c_ready = sem("c_half"), sem("c_ready")
        c_done, c_added = sem("c_done"), sem("c_added")
        assert keep + 192 <= SC + SCRATCH

        class Steps:

            def __init__(self, eng, s):
                self.eng, self.sem, self.n = eng, s, 0

            def mark(self, ins):
                self.n += 1
                return ins.then_inc(self.sem, 1)

            def sync(self):
                self.eng.wait_ge(self.sem, self.n)

            def __call__(self, ins):
                self.mark(ins)
                self.sync()

            def restart(self):
                self.eng.sem_clear(self.sem)
                self.n = 0

        def stage_end(eng, n):
            eng.drain().then_inc(stage_done, 1)
            eng.wait_ge(stage_done, 4 * n)

        def end_layer(eng, l, clears=False):
            eng.drain().then_inc(layer_done, 1)
            if clears:
                eng.wait_ge(layer_done, 5)
                nums = sorted(s.num for s in sems)
                eng.dma_reset(range(nums[0], nums[-1] + 1))
                eng.sem_clear(range(nums[0], nums[-1] + 1))
                eng.drain().then_inc(next_layer, 1)
            eng.wait_ge(next_layer, l + 1)

        chunks = [(c, slice(c * CH, (c + 1) * CH)) for c in range(NCH)]

        block = ctx.enter_context(nc.Block())

        @block.sync
        def _(sp):
            sp.dma_start(consts[:, :], ins["consts"]).then_inc(setup, 16)
            sp.dma_start(rope[64:96, :, :], ins["rope"]).then_inc(setup, 16)
            sp.dma_start(lmask_f, ins["lmask"]).then_inc(setup, 16)
            sp.dma_start(x[:, :, :], ins["x"]).then_inc(setup, 16)
            sp.dma_start(pages[:, :], ins["pages"]).then_inc(setup, 16)
            with sp.Fori(0, DEPTH) as l:
                def ring_load(u, j):
                    sp.dma_start(ring[:, j, :, :], ins["ring"][bass.ds(l, 1), bass.ds(u, 1)]
                                 .rearrange("a b p k m -> p (a b k) m")).then_inc(ring_full[j], 16)

                half = ROPE // 2
                sp.dma_start(vec[:, :], ins["vec"][bass.ds(l, 1)].rearrange("a p n -> p (a n)")).then_inc(vec_full, 16)
                for j in range(RING):
                    ring_load(j, j)
                sp.dma_start(dbuf[:, :, :, 0:POOL_BUF], ins["pool_prev"][bass.ds(l, 1)]
                             .rearrange("a p k b t -> p (a k) b t")).then_inc(dbuf_full, 16)
                sp.dma_start(wvg, ins["wvg"][bass.ds(l, 1)].rearrange("a p k m -> p (a k) m")).then_inc(wvg_full, 16)
                sp.dma_start(wgk[0:16, :], ins["wgk"][bass.ds(l, 1)].rearrange("a p n -> p (a n)")).then_inc(pre_full, 16)
                sp.dma_start(wuv, ins["wuv"][bass.ds(l, 1)].rearrange("a p n -> p (a n)")).then_inc(wuv_full, 16)
                for j in range(RING):
                    sp.wait_ge(lin_done, j + 1)
                    ring_load(RING + j, j)
                for j in range(RING):
                    sp.wait_ge(lin_done, RING + j + 1)
                    ring_load(2 * RING + j, j)
                    if j == 2:
                        sp.wait_ge(lin_evac, 6 + 2)
                        sp.wait_ge(slots_clear, 16)
                        sp.dma_start(kswap[64:64 + half, :], pr[64 + half:96, 5, :]).then_inc(kswap_full, 16)
                        sp.dma_start(kswap[64 + half:96, :], pr[64:64 + half, 5, :]).then_inc(kswap_full, 16)
                sp.wait_ge(vg_done, NT + 1)
                sp.dma_start(wpool, ins["wpool"][bass.ds(l, 1)].rearrange("a p k m -> p (a k) m")).then_inc(pre_full, 16)
                sp.wait_ge(stage_done, 4)
                for p in range(2):
                    sp.dma_start(w_h[:, p, :], ins["w_h"][bass.ds(l, 1), p].rearrange("a p n -> p (a n)")).then_inc(w_full[p], 16)
                sp.wait_ge(tp_free[0], 2)
                sp.wait_ge(tp_free[1], 1)
                sp.dma_start(qswap[64:64 + half, :], q_h[64 + half:96, 0, :]).then_inc(qswap_full, 16)
                sp.dma_start(qswap[64 + half:96, :], q_h[64:64 + half, 0, :]).then_inc(qswap_full, 16)
                with sp.Fori(0, H // 2) as i:
                    for p in range(2):
                        sp.wait_ge(tp_free[1], 18 * i + 9 * p + 6)
                        sp.wait_ge(q_rope, 2 * i + p + 1)
                        sp.dma_start(qswap[64:64 + half, :], q_h[64 + half:96, 1 - p, :]).then_inc(qswap_full, 16)
                        sp.dma_start(qswap[64 + half:96, :], q_h[64:64 + half, 1 - p, :]).then_inc(qswap_full, 16)
                        sp.wait_ge(tp_done, 36 * i + 18 * p + 6)
                        sp.sem_inc(turn, 1)
                        sp.dma_start(w_h[:, p, :], ins["w_h"][bass.ds(l, 1), bass.ds(2 * i + p + 2, 1)]
                                     .rearrange("a b p n -> p (a b n)")).then_inc(w_full[p], 16)
                sp.wait_ge(w_full[0], 16 * (H // 2 + 1))
                sp.wait_ge(w_full[1], 16 * (H // 2 + 1))
                sp.wait_ge(stage_done, 8)
                sp.wait_ge(ds_clear, 1)
                for h in range(GH):
                    sp.dma_start(d_state[GK * h:GK * (h + 1), :, GV * h:GV * (h + 1)],
                                 ins["state_gla"][bass.ds(l, 1), :, h].rearrange("a b k v -> (a k) b v")).then_inc(ds_full, 16)
                sp.wait_ge(stage_done, 12)

                sp.wait_ge(stage_done, 16)
                sp.dma_start(mem, ins["mem"]).then_inc(mem_full, 16)
                sp.dma_start(wxv, ins["wxv"][bass.ds(l, 1)].rearrange("a p k m -> p (a k) m")).then_inc(wxv_full, 16)
                for u in range(12, RING_USES):
                    sp.wait_ge(lin_done, u - RING + 1)
                    ring_load(u, u % RING)
                    if u == 23:
                        sp.wait_ge(stage_done, 24)
                        for b in range(DB):
                            if b >= 2:
                                sp.wait_ge(kd_used, b - 1)
                            sp.dma_start(kd[:, b % 2], ins["mem_k"][bass.ds(l, 1), b].rearrange("a p h m -> p (a h) m")).then_inc(kd_full[b % 2], 16)
                            if b < 2:
                                sp.dma_start(vd[:, b], ins["mem_v"][bass.ds(l, 1), b].rearrange("a (f m) h c -> m (a f) (h c)", f=2)).then_inc(vd_full[b], 16)
                        for b in range(2, DB):
                            sp.wait_ge(vd_used, b - 1)
                            sp.dma_start(vd[:, b % 2], ins["mem_v"][bass.ds(l, 1), b].rearrange("a (f m) h c -> m (a f) (h c)", f=2)).then_inc(vd_full[b % 2], 16)
                sp.wait_ge(stage_done, 32)
                def load_w(j, e):
                    sp.dma_start(w_e[j], ins["w_e"][bass.ds(l, 1), bass.ds(e, 1)].rearrange("a b p n -> p (a b n)")).then_inc(we_full[j], 16)

                def load_x(p, n):
                    sp.dma_start(xb[:, p, :], slots[bass.ds(CAP * n, CAP), :]).then_inc(xb_full[p], 16)

                sp.dma_start(w_r, ins["w_r"][bass.ds(l, 1)].rearrange("a p k n -> p (a k) n")).then_inc(wr_full, 16)
                load_w(0, 0)
                sp.wait_ge(ssq_ready, 3 * NCH)
                load_w(3, 3)
                sp.wait_ge(rows_ready, 1)
                load_x(0, 0)
                load_x(1, 1)
                sp.wait_ge(xr_done, NT + 1)
                load_w(1, 1)
                load_w(2, 2)
                for n in range(2):
                    sp.wait_ge(tx_done, n + 1)
                    load_x(n, n + 2)
                with sp.Fori(0, NE // 4 - 1) as i:
                    for j in range(4):
                        n = 4 * i + j
                        sp.wait_ge(tx_done, n + 3)
                        sp.sem_inc(turn, 1)
                        load_x(j % 2, n + 4)
                        sp.wait_ge(dn_done, n + 1)
                        sp.sem_inc(turn, 1)
                        load_w(j, n + 4)
                n_over = sp.value_load(over_i[0:1, 0:1], min_val=0, max_val=OVER)
                with sp.If(n_over > 0):
                    with sp.Fori(0, OVER // 4) as i:
                        for j in range(4):
                            o = 4 * i + j
                            with sp.If(n_over > o):
                                sp.wait_ge(dn_done, NE + o)
                                sp.sem_inc(turn, 1)
                                load_x(j % 2, NE + o)
                                e = sp.value_load(over_i[0:1, bass.ds(o + 1, 1)], min_val=0, max_val=NE - 1)
                                load_w(j, e)
                sp.wait_ge(stage_done, 44)
                end_layer(sp, l)
                sp.sem_inc(turn, 1)
            sp.wait_ge(norm_ready, NCH)
            sp.dma_start(outs["y"], xn).then_inc(y_stored, 16)
            sp.wait_ge(y_stored, 16)

        @block.tensor
        def _(pe):
            pe.wait_ge(setup, 80)
            with pe.Fori(0, DEPTH) as l:
                def sum_squares(src, n, tiles, count, base, ready, done, width=CH):
                    for c in range(count):
                        if n is not None:
                            pe.wait_ge(ready, n + c + 1)
                        for k in range(tiles):
                            mm = pe.matmul(ps[:, base + c, 0:width], ones, src(k, c), start=k == 0, stop=k == tiles - 1)
                        mm.then_inc(done, 1)

                def linear(groups, first, use, src, units=8, per=1, normed=None):
                    def body(i):
                        for j in range(RING * per):
                            slot = j // per
                            n = first + RING * per * i + j
                            if j % per == 0:
                                pe.wait_ge(ring_full[slot], (use + i + 1) * 16)
                            pe.wait_ge(lin_evac, n + 1)
                            for c, tok in chunks:
                                if normed is not None and j == 0:
                                    pe.wait_ge(norm_ready, normed + c + 1)
                                for k in range(units):
                                    mm = pe.matmul(ps[:, (j % 2) * NCH + c, 0:CH], ring[:, slot, (j % per) * units + k, :],
                                                   src[:, k, tok], start=k == 0, stop=k == units - 1)
                            mm.then_inc(lin_done, 1)
                    if groups == 1:
                        body(0)
                    else:
                        with pe.Fori(0, groups) as i:
                            body(i)

                sum_squares(lambda k, c: sq[:, k, chunks[c][1]], 0, KT, NCH, 0, sq_ready, ssq_ready)
                pe.wait_ge(ssq_ready, NCH)
                linear(2, 0, 0, xn, normed=0)
                pe.wait_ge(lat_sq, 1)
                pe.wait_ge(lin_evac, IN_MT + 1)
                for c, tok in chunks:
                    for k in range(2):
                        pe.matmul(ps[:, c, 0:CH], ones, sq2[:, k, tok], start=k == 0, stop=k == 1)
                pe.wait_ge(lin_evac, IN_MT + 2)
                for c, tok in chunks:
                    mm = pe.matmul(ps[:, NCH + c, 0:CH], ones, sq2[:, 2, tok], start=True, stop=True)
                mm.then_inc(lat_ssq, 1)
                for k in range(2):
                    pe.transpose(ps[0:POOL_BUF, 6, k * P:(k + 1) * P], pr[:, k, SEQ - POOL_BUF:SEQ], ident)
                for k in range(2):
                    mm = pe.transpose(ps[0:ND, 7, k * P:(k + 1) * P], pr[:, k, SEQ:TOK], ident)
                mm.then_inc(utr_done, 1)
                pe.wait_ge(wvg_full, 16)
                pe.wait_ge(utr_evac, 1)
                for t in range(NT + 1):
                    m = P if t < NT else ND
                    if t >= 2:
                        pe.wait_ge(vg_evac, t - 1)
                    for k in range(KT):
                        mm = pe.matmul(ps[0:m, 6 + t % 2, :], xn[:, k, t * P:t * P + m], wvg[:, k, :],
                                       start=k == 0, stop=k == KT - 1)
                    mm.then_inc(vg_done, 1)
                    if t == 1:
                        pe.wait_ge(pre_full, 16)
                        pe.wait_ge(lat_std, 1)
                        for c, tok in chunks:
                            mm = pe.matmul(ps[:, c, 0:CH], wgk[0:16, :], pr[0:16, 5, tok], start=True, stop=True)
                        mm.then_inc(z_done, 1)
                pe.wait_ge(wuv_full, 16)
                pe.wait_ge(lat_norm, 2)
                pe.wait_ge(pooled, 1)
                pe.wait_ge(vg_evac, NT + 1)
                for t in range(NT):
                    if t >= 2:
                        pe.wait_ge(vv_evac, t - 1)
                    pe.matmul(ps[:, 6 + t % 2, :], pr[:, 4, t * P:(t + 1) * P], wuv, start=True, stop=True).then_inc(vv_done, 1)
                pe.wait_ge(z_evac, 1)
                pe.wait_ge(pre_full, 32)
                for k in range(2):
                    for c, tok in chunks:
                        mm = pe.matmul(ps[:, k * NCH + c, 0:CH], wpool[:, k, :], psum_a[:, k, tok], start=True, stop=True)
                mm.then_inc(pool_mm, 1)

                stage_end(pe, 1)

                pe.sem_inc(y_done, 1)

                def proj(q, k, b):
                    bank = 4 + b
                    if k < 3:
                        tok = (slice(0, 512), slice(512, 1024), slice(SEQ, TOK))[k]
                        for kk in range(2):
                            mm = pe.matmul(ps[0:QK, bank, 0:tok.stop - tok.start], w_h[:, q, kk * QK:(kk + 1) * QK],
                                           pr[:, 2 + kk, tok], start=kk == 0, stop=kk == 1)
                    elif k < 5:
                        tok = (slice(0, 512), slice(512, 1024))[k - 3]
                        mm = pe.matmul(ps[0:NOPE, bank, :], w_h[:, q, 192:256], pr[:, 4, tok], start=True, stop=True)
                    else:
                        mm = pe.matmul(ps[:, bank, 0:ND], w_h[0:NOPE, q, 256:384], q_h[0:NOPE, q, SEQ:TOK],
                                       start=True, stop=True)
                    mm.then_inc(tp_done, 1)

                def scores(p, qb, s):
                    w = (qb + 1) * P
                    lhs = q_h[0:QK, p, qb * P:(qb + 1) * P]
                    for at in range(0, w, 512):
                        e = min(at + 512, w)
                        last = e == w
                        mm = pe.matmul(ps[:, 2 * s + at // 512, 0:e - at], lhs, k_h[0:QK, p, at:e], start=True, stop=not last)
                    at = (qb * P) % 512
                    pe.matmul(ps[:, 2 * s + qb // 4, at:at + P], ident, con("causal"), start=False, stop=True).then_inc(s_done, 1)

                for k in range(6):
                    if k == 0:
                        pe.wait_ge(w_full[0], 16)
                    if k >= 2:
                        pe.wait_ge(tp_free[k % 2], k // 2)
                    if k == 5:
                        pe.wait_ge(tp_free[0], 2)
                    proj(0, k, k % 2)
                pe.wait_ge(tp_free[0], 3)
                pe.wait_ge(tp_free[1], 3)
                pe.wait_ge(q_rope, 1)
                scores(0, 0, 0)
                scores(0, 1, 1)
                with pe.Fori(0, H // 2) as i:
                    for p in range(2):
                        n9 = 18 * i + 9 * p + 3
                        item = 16 * i + 8 * p
                        m = 0

                        def transposes(qb):
                            nonlocal m
                            pe.wait_ge(p_ready, item + qb + 1)
                            used = []
                            for at in range(0, qb + 1, 4):
                                pe.wait_ge(tp_free[m % 2], n9 + m // 2)
                                for kb in range(at, min(at + 4, qb + 1)):
                                    mm = pe.transpose(ps[:, 4 + m % 2, (kb - at) * P:(kb - at + 1) * P],
                                                      prob[:, qb % 2, kb * P:(kb + 1) * P], ident)
                                mm.then_inc(tp_done, 1)
                                used.append(m)
                                m += 1
                            return used

                        def values(qb, used):
                            for g, s in enumerate(used):
                                pe.wait_ge(tp_free[s % 2], n9 + s // 2 + 1)
                                for kb in range(4 * g, min(4 * g + 4, qb + 1)):
                                    if qb % 4 == 0 and kb == 0:
                                        pe.wait_ge(y_free, 4 * i + 2 * p + qb // 4 + 1)
                                    mm = pe.matmul(ps[:, 6 + qb // 4, (qb % 4) * P:(qb % 4 + 1) * P], v_h[:, p, kb, :],
                                                   pt[:, s % 2, (kb - 4 * g) * P:(kb - 4 * g + 1) * P],
                                                   start=kb == 0, stop=kb == qb)
                            if qb % 4 == 3:
                                mm.then_inc(y_done, 1)

                        def piece(k):
                            nonlocal m
                            if k == 0:
                                pe.wait_ge(w_full[1 - p], 16 * (i + 1) if p == 0 else 16 * (i + 2))
                            pe.wait_ge(tp_free[m % 2], n9 + m // 2)
                            proj(1 - p, k, m % 2)
                            m += 1

                        pe.wait_ge(v_ready, 2 * i + p + 1)
                        for qb in range(NT):
                            used = transposes(qb)
                            nxt = qb + 2
                            if nxt == NT:
                                pe.wait_ge(q_rope, 2 * i + p + 2)
                                pe.wait_ge(tp_free[0], n9 + 6)
                                pe.wait_ge(tp_free[1], n9 + 7)
                            scores(p if nxt < NT else 1 - p, nxt % NT, nxt % 2)
                            if qb < 6:
                                piece(qb)
                            values(qb, used)
                stage_end(pe, 2)

                pe.sem_inc(at_done, 1)
                pe.sem_inc(o_done, 1)

                def levels(p, first, w, idx):
                    for j, lv in enumerate(idx):
                        pe.wait_ge(at_free, first + j + 1)
                        q = g_q0[:, p, :, 0:w] if lv == NL - 1 else g_q[:, p, lv, :, 0:w]
                        pe.matmul(ps[0:w, j % 4, 0:GH * w].rearrange("p (h t) -> p h t", h=GH), g_k[p][:, lv, 0:w], q,
                                  start=True, stop=True).then_inc(at_done, 1)

                order = [NL - 1] + list(range(NL - 1))

                def tile(i, p):
                    n = 2 * i + p
                    pe.wait_ge(g_dve, n + 1 + 1)
                    pe.wait_ge(g_pool, n + 1 + 1)
                    levels(p, 16 * i + 8 * p, P, order)
                    pe.wait_ge(o_norm, n + 1)
                    pe.wait_ge(ot_evac, n + 1)
                    for k in range(2):
                        mm = pe.transpose(ps[:, 6, k * P:(k + 1) * P], g_o[:, 1 - p, k * P:(k + 1) * P], ident)
                    mm.then_inc(ot_done, 1)
                    pe.wait_ge(st_ready, n + 1)
                    pe.transpose(ps[:, 7, 0:P], g_kt[:, p, :], ident).then_inc(kt_done, 1)
                    pe.wait_ge(o_evac, n + 1)
                    pe.wait_ge(at_free, 16 * i + 8 * p + 12)
                    pe.matmul(ps[:, 4 + p, 0:GW], g_qe[:, p, :], state, start=True, stop=False, skip_group_check=True)
                    for h in range(GH):
                        mm = pe.matmul(ps[:, 4 + p, h * GV:(h + 1) * GV], g_att[:, p, h, :],
                                       vg[:, bass.ds(n, 1), h * GV:(h + 1) * GV].rearrange("p a v -> p (a v)"),
                                       start=False, stop=h == GH - 1, skip_group_check=True)
                    mm.then_inc(o_done, 1)
                    pe.wait_ge(kt_evac, n + 1)
                    pe.matmul(ps[:, 7, 0:GW], g_ktt[:, p, :],
                              vg[:, bass.ds(n, 1), 0:GW].rearrange("p a v -> p (a v)"), start=True, stop=True).then_inc(st_done, 1)

                with pe.Fori(0, NT // 2) as i:
                    for p in range(2):
                        tile(i, p)
                pe.wait_ge(g_dve, NT + 2 + 1)
                levels(0, NL * NT, ND, [NL - 1, NL - 3, NL - 2])
                pe.wait_ge(o_norm, NT + 1)
                pe.wait_ge(ot_evac, NT + 1)
                for k in range(2):
                    mm = pe.transpose(ps[:, 6, k * P:(k + 1) * P], g_o[:, 1, k * P:(k + 1) * P], ident)
                mm.then_inc(ot_done, 1)
                pe.wait_ge(st_ready, NT + 1)
                pe.transpose(ps[0:ND, 7, 0:P], g_kt[:, 0, 0:ND], ident).then_inc(kt_done, 1)
                pe.wait_ge(ds_full, 16 * GH)
                pe.wait_ge(o_evac, NT + 2)
                pe.wait_ge(at_free, NL * NT + 3 + 4)
                for b in range(DB):
                    pe.matmul(ps[0:ND, 4, 0:GW], d_qe[:, b, :], d_state[:, b, :], start=b == 0, stop=False, skip_group_check=True)
                for h in range(GH):
                    mm = pe.matmul(ps[0:ND, 4, h * GV:(h + 1) * GV], g_att[0:ND, 0, h, 0:ND], vg[0:ND, NT, h * GV:(h + 1) * GV],
                                   start=False, stop=h == GH - 1, skip_group_check=True)
                mm.then_inc(o_done, 1)
                pe.wait_ge(dkt_ready, 1)
                for b in range(DB):
                    if b >= 2:
                        pe.wait_ge(st_ready, NT + 1 + b - 1)
                    pe.matmul(ps[:, 7 - 2 * (b % 2), 0:GW], d_kt[0:ND, b, :], vg[0:ND, NT, 0:GW],
                              start=True, stop=True).then_inc(st_done, 1)
                pe.wait_ge(o_norm, NT + 2)
                pe.wait_ge(ot_evac, NT + 2)
                for k in range(2):
                    mm = pe.transpose(ps[:, 6, k * ND:(k + 1) * ND], g_o[0:ND, 0, k * P:(k + 1) * P], ident[0:ND, 0:ND])
                mm.then_inc(ot_done, 1)
                stage_end(pe, 3)

                pe.transpose(ps[0:ND, 3, 0:P], ckv_new, ident).then_inc(tok_done, 1)
                pe.wait_ge(tok_evac, 1)

                def turn_over(n, g):
                    s = n % NSLOT
                    if g == 0:
                        pe.wait_ge(ck_full[s], 32 * (n // NSLOT + 1))
                    pe.wait_ge(ct_evac, NGR * n + g + 1)
                    for j in range(4):
                        mm = pe.transpose(ps[:, g % 2, j * P:(j + 1) * P], ck[s][:, 4 * g + j, :], ident)
                    mm.then_inc(ct_done, 1)
                    pe.wait_ge(k4_evac, NGR * n + g + 1)
                    pe.transpose(ps[:, 2, 0:P], kr_c[s][:, 4 * g:4 * g + 4, :].rearrange("p j r -> p (j r)"), ident).then_inc(k4_done, 1)

                def block_scores(n, g):
                    out = ps[:, 4 + 2 * (n % 2) + g // 4, (g % 4) * P:(g % 4 + 1) * P]
                    pe.wait_ge(ct_evac, NGR * n + g + 3)
                    pe.wait_ge(k4_evac, NGR * n + g + 2)
                    pe.matmul(out, k4[:, g % 2, :], qpe_dec[:, n, :, :].rearrange("p j q -> p (j q)"), start=True, stop=False)
                    for j in range(4):
                        mm = pe.matmul(out, ct[:, g % 2, j * P:(j + 1) * P], q_dec[:, n, 96 - ND * j:224 - ND * j],
                                       start=False, stop=j == 3)
                    mm.then_inc(sc_done, 1)

                def new_scores(n):
                    if n:
                        pe.wait_ge(tail_dve, 5 * n)
                    pe.matmul(ps[0:ND, 3, 0:ND], ckv_new, q_dec[:, n, 96:128], start=True, stop=False)
                    pe.matmul(ps[0:ND, 3, 0:ND], kr_new[64:96, :], qpe_new[64:96, n, :], start=False, stop=True).then_inc(tail_pe, 1)

                def max_rows(n):
                    pe.wait_ge(tail_dve, 5 * n + 1)
                    pe.transpose(ps[0:ND, 3, 0:P], mx, ident).then_inc(tail_pe, 1)

                def max_everywhere(n):
                    pe.wait_ge(tail_dve, 5 * n + 2)
                    pe.matmul(ps[:, 3, 0:ND], ones[0:ND, :], diag[0:ND, :], start=True, stop=True).then_inc(tail_pe, 1)

                def latents(n):
                    pe.wait_ge(tail_dve, 5 * n + 3)
                    for j in range(BLK):
                        pe.matmul(ps[0:ND, 3, 0:P], pd[:, j, :], ck[n % NSLOT][:, j, :], start=j == 0, stop=False)
                    pe.matmul(ps[0:ND, 3, 0:P], p_new[0:ND, :], ckv_tok[0:ND, :], start=False, stop=True)
                    pe.matmul(ps[0:ND, 3, P:P + 1], sm, ones[:, 0:1], start=True, stop=True).then_inc(tail_pe, 1)

                def latents_back(n):
                    pe.wait_ge(tail_dve, 5 * n + 4)
                    pe.transpose(ps[:, 3, 0:ND], d_o[0:ND, :], ident[0:ND, 0:ND]).then_inc(tail_pe, 1)

                for n in range(DB):
                    turn_over(n, 0)
                    for g in range(NGR):
                        if g + 1 < NGR:
                            turn_over(n, g + 1)
                        block_scores(n, g)
                        if n >= 1:
                            if g == 0:
                                max_rows(n - 1)
                            if g == 1:
                                max_everywhere(n - 1)
                            if g == 3:
                                latents(n - 1)
                            if g == 5:
                                latents_back(n - 1)
                    new_scores(n)
                for f in (max_rows, max_everywhere, latents, latents_back):
                    f(DB - 1)
                pe.wait_ge(tail_dve, 5 * DB)
                for h in range(H):
                    mm = pe.matmul(ps[64 * (h % 2):64 * (h % 2) + 64, 0, (h // 2) * ND:(h // 2 + 1) * ND],
                                   wuv[:, h * VD:(h + 1) * VD], o_lat[:, h].rearrange("p b t -> p (b t)"),
                                   start=True, stop=True, skip_group_check=True)
                mm.then_inc(tail_pe, 1)
                stage_end(pe, 4)
                linear(1, IN_MT, 2, mix)
                pe.wait_ge(msq_ready, 1)
                for k in range(KT):
                    mm = pe.matmul(ps[:, 6, 0:NMEM], ones, mem_sq[:, k, :], start=k == 0, stop=k == KT - 1)
                mm.then_inc(mssq_ready, 1)
                linear(1, IN_MT + RING, 3, mix)
                stage_end(pe, 5)
                pe.wait_ge(sq_ready, NCH + KT)
                sum_squares(lambda k, c: sq[:, k, chunks[c][1]], None, KT, NCH, 0, sq_ready, ssq_ready)
                pe.wait_ge(mnorm_ready, 1)
                pe.wait_ge(wxv_full, 16)
                for t in range(2):
                    for k in range(KT):
                        mm = pe.matmul(ps[:, 6 + t, :], mem_n[:, k, t * P:(t + 1) * P], wxv[:, k, :], start=k == 0, stop=k == KT - 1)
                    mm.then_inc(mv_done, 1)
                pe.wait_ge(std_ready, 2 * NCH)
                for j in range(XK_MT):
                    pe.wait_ge(ring_full[j], 16 * 5)
                    pe.wait_ge(lin_evac, IN_MT + OUT_MT + j + 1)
                    for k in range(KT):
                        mm = pe.matmul(ps[:, (j % 2) * NCH, 0:NMEM], ring[:, j, k, :], mem_n[:, k, :], start=k == 0, stop=k == KT - 1)
                    mm.then_inc(lin_done, 1)
                linear(1, IN_MT + OUT_MT + XK_MT, 5, xn, normed=NCH)
                stage_end(pe, 6)

                def x_scores(n, p):
                    pe.wait_ge(qt_ready, n + 1)
                    for h in range(XH):
                        mm = pe.matmul(ps[:, 2 * p + h // 2, (h % 2) * NMEM:(h % 2 + 1) * NMEM], qt[:, p, h, :], mk[:, h, :],
                                       start=True, stop=True)
                    mm.then_inc(xs_done, 1)

                def x_turn(n, p):
                    pe.wait_ge(xp_ready, n + 1)
                    for g in range(2):
                        pe.wait_ge(xt_evac, 2 * n + g)
                        for h in range(XH):
                            mm = pe.transpose(ps[:, 4 + g, h * P:(h + 1) * P], px[:, p, h, g * P:(g + 1) * P], ident)
                        mm.then_inc(xt_done, 1)

                def x_values(n, p):
                    pe.wait_ge(xt_evac, 2 * n + 2)
                    pe.wait_ge(xon_ready, n)
                    for h in range(XH):
                        for g in range(2):
                            mm = pe.matmul(ps[:, 6, h * P:(h + 1) * P], pxt[:, p, g, h * P:(h + 1) * P], mv[:, g, h * P:(h + 1) * P],
                                           start=g == 0, stop=g == 1)
                    mm.then_inc(xv_done, 1)

                def x_back(n, p, w):
                    pe.wait_ge(xon_ready, n + 1)
                    pe.wait_ge(xot_evac, n)
                    for h in range(XH):
                        mm = pe.transpose(ps[:, 7, h * w:(h + 1) * w], xon[0:w, p, h, :], ident[0:w, 0:w])
                    mm.then_inc(xot_done, 1)

                def x_tile(n, p, before=True, ahead=True):
                    x_turn(n, p)
                    if ahead:
                        x_scores(n + 2, p)
                    if before:
                        x_back(n - 1, 1 - p, P)
                    x_values(n, p)

                x_scores(0, 0)
                x_scores(1, 1)
                x_tile(0, 0, before=False)
                x_tile(1, 1)
                with pe.Fori(0, (NT - 4) // 2) as i:
                    for p in range(2):
                        x_tile(2 * i + p + 2, p)
                x_tile(NT - 2, 0, ahead=False)
                x_turn(NT - 1, 1)
                pe.wait_ge(qt_ready, NT + 1)
                for b in range(DB):
                    pe.wait_ge(kd_full[b % 2], 16 * (b // 2 + 1))
                    for h in range(XH):
                        mm = pe.matmul(ps[0:ND, h // 2, (h % 2) * NMEM:(h % 2 + 1) * NMEM], d_qm[:, h, b, :], kd[:, b % 2, h, :],
                                       start=b == 0 and h % 2 == 0, stop=b == DB - 1, skip_group_check=True)
                    mm.then_inc(kd_used if b < DB - 1 else xs_done, 1)
                x_back(NT - 2, 0, P)
                x_values(NT - 1, 1)
                x_back(NT - 1, 1, P)
                pe.wait_ge(xp_ready, NT + 1)
                pe.wait_ge(xt_evac, 2 * NT)
                for g in range(2):
                    for h in range(XH):
                        mm = pe.transpose(ps[:, 4, (g * XH + h) * ND:(g * XH + h + 1) * ND], px[0:ND, 0, h, g * P:(g + 1) * P],
                                          ident[0:ND, 0:ND])
                mm.then_inc(dt_done, 1)
                pe.wait_ge(dpt_ready, 1)
                for b in range(DB):
                    pe.wait_ge(vd_full[b % 2], 16 * (b // 2 + 1))
                    for g in range(2):
                        for h in range(XH):
                            mm = pe.matmul(ps[0:ND, 6, h * P:(h + 1) * P], d_pt[:, g * XH + h, b, :], vd[:, b % 2, g, h * P:(h + 1) * P],
                                           start=b + g + h == 0, stop=b == DB - 1 and g == 1, skip_group_check=True)
                    mm.then_inc(vd_used if b < DB - 1 else xv_done, 1)
                x_back(NT, 0, ND)
                stage_end(pe, 7)
                linear(1, IN_MT + OUT_MT + XK_MT + XQ_MT, 6, co, units=4, per=2)
                stage_end(pe, 8)
                pe.wait_ge(sq_ready, NCH + 2 * KT)
                sum_squares(lambda k, c: xn[:, k, chunks[c][1]], None, KT, NCH, 0, sq_ready, ssq_ready)
                pe.wait_ge(wr_full, 16)
                for c, tok in chunks:
                    pe.wait_ge(norm_ready, 2 * NCH + c + 1)
                    for k in range(KT):
                        mm = pe.matmul(ps[0:NR, c, 0:CH], w_r[:, k, :], xn[:, k, tok], start=k == 0, stop=k == KT - 1)
                    mm.then_inc(lg_done, 1)
                pe.wait_ge(lg_evac, NCH + 1)
                for t in range(NT + 1):
                    mm = pe.transpose(ps[:, 3, t * NR:(t + 1) * NR], lgt[0:NR, t * P:(t + 1) * P], ident[0:NR, 0:NR])
                mm.then_inc(lt_done, 1)

                def rows_of(t):
                    m = P if t < NT else ND
                    if t >= 2:
                        pe.wait_ge(xr_evac, t - 1)
                    for k in range(KT):
                        b = (k // 4) + (0 if t % 2 == 0 else 6)
                        mm = pe.transpose(ps[0:m, b, (k % 4) * P:(k % 4 + 1) * P], xn[:, k, t * P:t * P + m], ident)
                    mm.then_inc(xr_done, 1)

                for t in range(4):
                    rows_of(t)
                pe.wait_ge(both_ready, 1)
                pe.matmul(ps[:, 4, 0:(NT + 1) * NE], con("below"), both.rearrange("p t e -> p (t e)"), start=True, stop=True)
                pe.matmul(ps[:, 5, 0:(NT + 1) * NE], ones, both.rearrange("p t e -> p (t e)"), start=True, stop=True).then_inc(ranked, 1)
                for t in range(4, NT + 1):
                    rows_of(t)
                stage_end(pe, 9)

                def turn_x(n, p, full):
                    pe.wait_ge(xb_full[p], full)
                    pe.wait_ge(tx_evac, n)
                    for k in range(KT):
                        mm = pe.transpose(ps[:, k // 4, (k % 4) * P:(k % 4 + 1) * P], xb[:, p, k * P:(k + 1) * P], ident)
                    mm.then_inc(tx_done, 1)

                def gate_up(n, p, j, full):
                    pe.wait_ge(we_full[j], full)
                    pe.wait_ge(tx_evac, n + 1)
                    for k in range(KT):
                        mm = pe.matmul(ps[:, 2, :], xb_t[:, p, k, :], w_e[j][:, k * 512:(k + 1) * 512], start=k == 0, stop=k == KT - 1)
                    mm.then_inc(gu_done, 1)

                def turn_h(n):
                    pe.wait_ge(h_ready, n + 1)
                    pe.wait_ge(ht_evac, n)
                    for k in range(2):
                        mm = pe.transpose(ps[:, 6, k * P:(k + 1) * P], h_b[:, k * P:(k + 1) * P], ident)
                    mm.then_inc(ht_done, 1)

                def down(n, p, j):
                    pe.wait_ge(ht_evac, n + 1)
                    pe.wait_ge(dn_evac, n + 1)
                    for f in range(2):
                        for k in range(2):
                            at = KT * 512 + k * D + f * 512
                            mm = pe.matmul(ps[:, 4 + f, :], h_t[:, p, k, :], w_e[j][:, at:at + 512], start=k == 0, stop=k == 1)
                    mm.then_inc(dn_done, 1)

                def block(n, j, i, j1, i1, more=True):
                    gate_up(n, j % 2, j, 16 * (i + 1))
                    if more:
                        turn_x(n + 1, j1 % 2, 16 * (2 * i1 + j1 // 2 + 1))
                    down(n - 1, (j + 1) % 2, (j + 3) % 4)
                    turn_h(n)

                turn_x(0, 0, 16)
                gate_up(0, 0, 0, 16)
                turn_x(1, 1, 16)
                turn_h(0)
                with pe.Fori(0, NE // 4 - 1) as i:
                    for j in range(1, 5):
                        nxt = j + 1
                        block(4 * i + j, j % 4, i + j // 4, nxt % 4, i + nxt // 4)
                for n in range(NE - 3, NE):
                    block(n, n % 4, n // 4, (n + 1) % 4, (n + 1) // 4, more=n < NE - 1)
                down(NE - 1, 1, 3)
                n_over = pe.value_load(over_i[0:1, 0:1], min_val=0, max_val=OVER)
                with pe.If(n_over > 0):
                    with pe.Fori(0, OVER // 4) as i:
                        for j in range(4):
                            with pe.If(n_over > 4 * i + j):
                                n = NE + 4 * i + j
                                turn_x(n, j % 2, 16 * (NE // 2 + 2 * i + j // 2 + 1))
                                gate_up(n, j % 2, j, 16 * (NE // 4 + i + 1))
                                turn_h(n)
                                down(n, j % 2, j)
                stage_end(pe, 10)
                for t in range(NT + 1):
                    m = P if t < NT else ND
                    if t >= 2:
                        pe.wait_ge(c_added, t - 1)
                    pe.wait_ge(c_ready, t + 1)
                    for k in range(KT):
                        mm = pe.transpose(ps[:, 2 * (t % 2) + k // 4, (k % 4) * m:(k % 4 + 1) * m], comb[0:m, t % 2, k * P:(k + 1) * P],
                                          ident[0:m, 0:m])
                    mm.then_inc(c_done, 1)
                stage_end(pe, 11)
                end_layer(pe, l)
            sum_squares(lambda k, c: sq[:, k, chunks[c][1]], 0, KT, NCH, 0, sq_ready, ssq_ready)

        @block.scalar
        def _(act):
            step = Steps(act, act_step)
            act.wait_ge(setup, 80)
            with act.Fori(0, DEPTH) as l:
                def squares(src, dst, width, count, scale, ready):
                    for c in range(count):
                        tok = slice(c * width, (c + 1) * width)
                        act.activation(dst[:, :, tok], src[:, :, tok], ACT.Square, scale=scale).then_inc(ready, 1)

                def squares_of(n, dst, k):
                    act.wait_ge(lin_evac, n + 1 + 2)
                    act.activation(dst[:, k, :], x[:, k, :], ACT.Square, scale=D ** -0.5).then_inc(sq_ready, 1)

                def roots(src, r, width, count, base, ready, done):
                    for c in range(count):
                        act.wait_ge(ready, base + c + 1)
                        act.activation(r[:, c * width:(c + 1) * width], src[:, c, 0:width], ACT.Sqrt,
                                       bias=EPS).then_inc(done, 1)

                act.sem_inc(lin_evac, 2)
                squares(x, sq, CH, NCH, D ** -0.5, sq_ready)
                roots(ps, rstd[:, 0, :], CH, NCH, 0, ssq_ready, std_ready)
                for j in range(IN_MT):
                    act.wait_ge(lin_done, j + 1)
                    if j == 6:
                        act.wait_ge(pooled, 1)
                    act.activation(pr[:, j, :].rearrange("p (c n) -> p c n", c=NCH), ps[:, (j % 2) * NCH:(j % 2 + 1) * NCH, 0:CH],
                                   ACT.Copy).then_inc(lin_evac, 1)
                    if j == 4:
                        act.wait_ge(lin_evac, j + 1 + 2)
                        step.mark(act.activation(sq2[:, 0:2, :], pr[:, 2:4, :], ACT.Square, scale=1.0 / 16))
                        act.activation(sq2[:, 2, :], pr[:, 4, :], ACT.Square, scale=float(P) ** -0.5).then_inc(lat_sq, 1)
                act.wait_ge(lat_ssq, 1)
                step.mark(act.activation(rstd[:, 0, :].rearrange("p (c n) -> p c n", c=NCH), ps[:, 0:NCH, 0:CH], ACT.Sqrt, bias=EPS))
                act.activation(rstd[:, 1, :].rearrange("p (c n) -> p c n", c=NCH), ps[:, NCH:2 * NCH, 0:CH], ACT.Sqrt,
                               bias=EPS).then_inc(lat_std, 1)
                act.wait_ge(utr_done, 1)
                step.mark(act.activation(u_out[0:POOL_BUF, 0, :], ps[0:POOL_BUF, 6, 0:GW], ACT.Copy))
                act.activation(u_out[0:ND, 1, :], ps[0:ND, 7, 0:GW], ACT.Copy).then_inc(utr_evac, 1)
                for t in range(NT + 1):
                    m = P if t < NT else ND
                    act.wait_ge(vg_done, t + 1)
                    if t == NT:
                        act.wait_ge(slots_clear, 16)
                    act.activation(silu[0:m, t, :], ps[0:m, 6 + t % 2, GW:512], ACT.Exp, scale=-1.0).then_inc(gate_e, 1)
                    act.activation(vg[0:m, t, :], ps[0:m, 6 + t % 2, :], ACT.Copy).then_inc(vg_evac, 1)
                    if t == 2:
                        act.wait_ge(z_done, 1)
                        act.wait_ge(kr_ready, 1)
                        act.activation(la.rearrange("p (c n) -> p c n", c=NCH), ps[:, 0:NCH, 0:CH], ACT.Identity,
                                       bias=gain("b_gk")).then_inc(z_evac, 1)
                        act.wait_ge(z_evac, 1)
                        step(act.activation(la_t, la, ACT.Abs))
                        step(act.activation(la_t, la_t, ACT.Exp, scale=-1.0))
                        act.activation(la_t, la_t, ACT.Ln, bias=1.0).then_inc(z_evac, 1)
                act.wait_ge(utr_evac, 1)
                step.sync()
                act.dma_start(outs["pool_p"][bass.ds(l, 1)].rearrange("a t c -> (a t) c"), u_out[0:POOL_BUF, 0, :]).then_inc(states_stored, 16)
                for b in range(DB):
                    act.dma_start(outs["pool_s"][bass.ds(l, 1), b, POOL_BUF - DT:POOL_BUF, :].rearrange("a t c -> (a t) c"),
                                  u_out[b * DT:(b + 1) * DT, 1, :]).then_inc(states_stored, 16)
                act.dma_start(outs["pool_s"][bass.ds(l, 1), :, 0:POOL_BUF - DT, :].rearrange("a b t c -> (a b) t c"),
                              ins["pool_old"][bass.ds(l, 1), :, DT:POOL_BUF, :].rearrange("a b t c -> (a b) t c")).then_inc(states_stored, 16)
                for t in range(NT):
                    act.wait_ge(vv_done, t + 1)
                    act.activation(vv[t // 4][:, t % 4, :], ps[:, 6 + t % 2, :], ACT.Copy).then_inc(vv_evac, 1)
                act.wait_ge(pool_mm, 1)
                for k in range(2):
                    ev = act.activation(mix[:, k, :].rearrange("p (c n) -> p c n", c=NCH), ps[:, k * NCH:(k + 1) * NCH, 0:CH],
                                        ACT.Copy, scale=gain("pool_scale", k))
                    step.mark(ev)
                act.wait_ge(kr_ready, 1)
                act.wait_ge(lat_norm, 2)
                act.dma_start(outs["ckv"][bass.ds(l, 1)].rearrange("a p n -> p (a n)"), pr[:, 4, :]).then_inc(states_stored, 16)
                act.dma_start(outs["kpe"][bass.ds(l, 1)].rearrange("a p n -> p (a n)"), kr[64:96, :]).then_inc(states_stored, 16)
                act.wait_ge(states_stored, 16 * (DB + 4))
                step.sync()
                step.restart()
                stage_end(act, 1)

                def evacuate(m, w):
                    act.activation(pt[:, m % 2, 0:w], ps[:, 4 + m % 2, 0:w], ACT.Copy).then_inc(tp_free[m % 2], 1)

                def expo(qb, item):
                    act.wait_ge(nmax_ready, item + 1)
                    act.activation(prob[:, qb % 2, 0:(qb + 1) * P],
                                   ps[:, 2 * (qb % 2):2 * (qb % 2) + 2, :].rearrange("p a n -> p (a n)")[:, 0:(qb + 1) * P],
                                   ACT.Exp, bias=nmax[:, qb % 2, 1:2], scale=MLA_SCALE).then_inc(p_ready, 1)

                expo(0, 0)
                expo(1, 1)
                with act.Fori(0, H // 2) as i:
                    for p in range(2):
                        m = 0
                        item = 16 * i + 8 * p
                        for qb in range(NT):
                            for at in range(0, qb + 1, 4):
                                act.wait_ge(tp_done, 36 * i + 18 * p + 6 + m + 1)
                                evacuate(m, (min(at + 4, qb + 1) - at) * P)
                                m += 1
                            if qb < 6:
                                expo(qb + 2, item + qb + 2)
                                m += 1
                            else:
                                expo(qb - 6, item + qb + 2)
                stage_end(act, 2)

                act.wait_ge(w_full[0], 16 * (H // 2 + 1))
                act.wait_ge(w_full[1], 16 * (H // 2 + 1))
                act.sem_inc(o_evac, 2)
                act.sem_inc(ot_evac, 1)

                def exps(n, p, w, lv):
                    act.wait_ge(g_sub, n)
                    step.mark(act.activation(g_e[:, p, lv:NL - 1, 0:w], g_e[:, p, lv:NL - 1, 0:w], ACT.Exp))
                    act.wait_ge(g_pool, n - 2 + 1)
                    act.wait_ge(g_dve, n - 2 + 1)
                    step.mark(act.activation(g_eb[p][:, 0:w], g_b[:, p, 0:w], ACT.Exp, bias=LOG_SCALE))
                    if w == P:
                        step.mark(act.activation(g_ek[p], g_b[:, p, :], ACT.Exp, scale=-1.0, bias=g_b[:, p, P - 1:P]))
                        act.activation(g_last[:, p, 0:1], g_b[:, p, P - 1:P], ACT.Exp).then_inc(g_exp, 1)
                    else:
                        step.mark(act.activation(g_ek[0][:, 0:w], g_ek[0][:, 0:w], ACT.Exp))
                        act.activation(g_last[:, 0, :], g_b[:, 0, 0:ND].rearrange("p (b t) -> p b t", b=DB)[:, :, DT - 1], ACT.Exp).then_inc(g_exp, 1)

                def take_kt(n, p, w):
                    act.wait_ge(kt_done, n)
                    act.activation(g_ktt[0:w, p, :], ps[0:w, 7, 0:P], ACT.Copy).then_inc(kt_evac, 1)

                def take_o(n, p, w):
                    act.wait_ge(o_done, n + 1)
                    act.activation(g_o[0:w, p, :], ps[0:w, 4 + p, 0:GW], ACT.Copy).then_inc(o_evac, 1)
                    act.wait_ge(o_sum, n)
                    act.activation(g_ms[0:w, 1, :], g_ms[0:w, 0, :], ACT.Sqrt, bias=EPS, scale=1.0 / GV).then_inc(o_root, 1)

                def take_ot(n, w, cols):
                    act.wait_ge(ot_done, n)
                    act.activation(mix[:, 6:8, cols], ps[:, 6, 0:2 * w].rearrange("p (k t) -> p k t", k=2), ACT.Copy,
                                   scale=gain("g_gla")).then_inc(ot_evac, 1)

                act.wait_ge(g_sub, 1)
                step.mark(act.activation(g_e[:, 0, 0:NL - 1, :], g_e[:, 0, 0:NL - 1, :], ACT.Exp))
                step.mark(act.activation(g_eb[0], g_b[:, 0, :], ACT.Exp, bias=LOG_SCALE))
                step.mark(act.activation(g_ek[0], g_b[:, 0, :], ACT.Exp, scale=-1.0, bias=g_b[:, 0, P - 1:P]))
                act.activation(g_last[:, 0, 0:1], g_b[:, 0, P - 1:P], ACT.Exp).then_inc(g_exp, 1)
                step.sync()
                step.restart()
                with act.Fori(0, NT // 2) as i:
                    for p in range(2):
                        n = 2 * i + p
                        exps(n + 2, 1 - p, P, 0)
                        take_ot(n + 1, P, bass.ds(P * ((n + NT - 1) % NT), P))
                        take_kt(n + 1, p, P)
                        take_o(n + 1, p, P)
                        step.sync()
                        step.restart()
                exps(NT + 2, 0, ND, NL - 3)
                take_ot(NT + 1, P, slice(SEQ - P, SEQ))
                take_kt(NT + 1, 0, ND)
                take_o(NT + 1, 0, ND)
                take_ot(NT + 2, ND, slice(SEQ, TOK))
                act.wait_ge(st_ready, NT + DB + 1)
                act.wait_ge(g_dve, NT + 2 + 1)
                for h in range(GH):
                    rows, cols = slice(GK * h, GK * (h + 1)), slice(GV * h, GV * (h + 1))
                    act.dma_start(outs["gla_p"][bass.ds(l, 1), h].rearrange("a k v -> (a k) v"), state[rows, cols]).then_inc(states_stored, 16)
                    act.dma_start(outs["gla_s"][bass.ds(l, 1), :, h].rearrange("a b k v -> (a k) b v"), d_state[rows, :, cols]).then_inc(states_stored, 16)
                act.wait_ge(states_stored, 16 * (DB + 4 + 2 * GH))
                step.sync()
                step.restart()
                stage_end(act, 3)

                act.sem_inc(ct_evac, 2)
                for n in range(DB + 1):
                    for g in range(NGR if n < DB else 0):
                        act.wait_ge(ct_done, NGR * n + g + 1)
                        act.activation(ct[:, g % 2, :], ps[:, g % 2, :], ACT.Copy).then_inc(ct_evac, 1)
                        if n >= 1 and g == 3:
                            act.wait_ge(shifted, n)
                            step.mark(act.activation(pd, pd, ACT.Exp, scale=MLA_SCALE))
                            act.activation(p_new[0:ND, :], p_new[0:ND, :], ACT.Exp, scale=MLA_SCALE).then_inc(pd_ready, 1)
                    if n == DB:
                        act.wait_ge(shifted, n)
                        step.mark(act.activation(pd, pd, ACT.Exp, scale=MLA_SCALE))
                        act.activation(p_new[0:ND, :], p_new[0:ND, :], ACT.Exp, scale=MLA_SCALE).then_inc(pd_ready, 1)
                act.wait_ge(tail_pe, 5 * DB + 1)
                act.activation(mix[:, 2:6, SEQ:TOK], ps[:, 0, 0:4 * ND].rearrange("p (k t) -> p k t", k=4), ACT.Copy).then_inc(act_step, 1)
                step.n += 1
                step.sync()
                step.restart()
                stage_end(act, 4)
                act.wait_ge(mem_full, 16)
                act.activation(mem_sq, mem, ACT.Square, scale=D ** -0.5).then_inc(msq_ready, 1)
                for k in range(KT):
                    if k == RING:
                        act.wait_ge(mssq_ready, 1)
                        act.activation(mem_r, ps[:, 6, 0:NMEM], ACT.Sqrt, bias=EPS).then_inc(mstd_ready, 1)
                    squares_of(IN_MT + k, sq, k)
                stage_end(act, 5)
                roots(ps, rstd[:, 0, :], CH, NCH, NCH, ssq_ready, std_ready)
                for j in range(XK_MT):
                    act.wait_ge(lin_done, IN_MT + OUT_MT + j + 1)
                    act.activation(mk[:, j, :], ps[:, (j % 2) * NCH, 0:NMEM], ACT.Copy).then_inc(lin_evac, 1)
                for t in range(2):
                    act.wait_ge(mv_done, t + 1)
                    act.activation(mv[:, t, :], ps[:, 6 + t, :], ACT.Copy).then_inc(mv_evac, 1)
                act.wait_ge(lin_evac, IN_MT + OUT_MT + XK_MT + 2)
                act.wait_ge(mv_evac, 2)
                act.dma_start(outs["mk"][bass.ds(l, 1)].rearrange("a p h m -> p (a h) m"), mk).then_inc(states_stored, 16)
                act.dma_start(outs["mv"][bass.ds(l, 1)].rearrange("a p h m -> p (a h) m"), mv).then_inc(states_stored, 16)
                stage_end(act, 6)

                def x_exps(n, p, w):
                    act.wait_ge(xm_ready, n)
                    for h in range(XH):
                        last = act.activation(px[0:w, p, h, :], ps[0:w, 2 * p + h // 2, (h % 2) * NMEM:(h % 2 + 1) * NMEM], ACT.Exp,
                                              bias=xm[0:w, p, 4 + h:5 + h], scale=X_SCALE, accum_out=xm[0:w, p, 8 + h:9 + h])
                    last.then_inc(xp_ready, 1)

                def keep_pt(n, p):
                    for g in range(2):
                        act.wait_ge(xt_done, 2 * n + g + 1)
                        act.activation(pxt[:, p, g, :], ps[:, 4 + g, :], ACT.Copy).then_inc(xt_evac, 1)

                x_exps(1, 0, P)
                x_exps(2, 1, P)
                with act.Fori(0, (NT - 2) // 2) as i:
                    for p in range(2):
                        n = 2 * i + p
                        keep_pt(n, p)
                        x_exps(n + 3, p, P)
                for n in (NT - 2, NT - 1):
                    keep_pt(n, n % 2)
                x_exps(NT + 1, 0, ND)
                act.wait_ge(states_stored, 16 * (DB + 6 + 2 * GH))
                stage_end(act, 7)
                for k in range(KT):
                    squares_of(IN_MT + OUT_MT + XK_MT + XQ_MT + k, xn, k)
                stage_end(act, 8)
                roots(ps, rstd[:, 0, :], CH, NCH, 2 * NCH, ssq_ready, std_ready)
                for c, tok in chunks:
                    act.wait_ge(lg_done, c + 1)
                    act.activation(lgt[0:NR, tok], ps[0:NR, c, 0:CH], ACT.Identity, bias=gain("b_r", 0, NR)).then_inc(lg_evac, 1)

                def keep_rows(t):
                    m = P if t < NT else ND
                    act.wait_ge(xr_done, t + 1)
                    if t >= 4:
                        act.wait_ge(row_moved[t % 4], 32 * (t // 4))
                    b = 0 if t % 2 == 0 else 6
                    act.activation(xr[0:m, t % 4, :].rearrange("p (a n) -> p a n", a=2), ps[0:m, b:b + 2, :], ACT.Copy).then_inc(xr_evac, 1)

                keep_rows(0)
                keep_rows(1)
                act.wait_ge(rx_in, 1)
                act.activation(r_exp, r_exp, ACT.Exp).then_inc(rx_out, 1)
                for t in range(2, NT + 1):
                    keep_rows(t)
                stage_end(act, 9)

                def gate_exp(n):
                    act.wait_ge(gu_done, n + 1)
                    act.activation(h_e, ps[:, 2, 0:DE], ACT.Exp, scale=-1.0).then_inc(ge_ready, 1)

                def keep_h(n, p):
                    act.wait_ge(ht_done, n + 1)
                    act.activation(h_t[:, p].rearrange("p k t -> p (k t)"), ps[:, 6, 0:DE], ACT.Copy).then_inc(ht_evac, 1)

                def send_y(n, p, sent):
                    act.wait_ge(dn_done, n + 1)
                    act.wait_ge(y_sent[p], sent + 16)
                    act.sem_inc(turn, 1)
                    act.activation(y_sb[:, p, :].rearrange("p (a n) -> p a n", a=2), ps[:, 4:6, :], ACT.Copy).then_inc(dn_evac, 1)
                    act.wait_ge(dn_evac, n + 1 + 1)
                    act.sem_inc(turn, 1)
                    act.dma_start(slots[bass.ds(CAP * n, CAP), :], y_sb[:, p, :]).then_inc(y_sent[p], 16)

                act.sem_inc(dn_evac, 1)
                for p in range(2):
                    act.sem_inc(y_sent[p], 16)
                gate_exp(0)
                keep_h(0, 0)
                with act.Fori(0, NE // 4 - 1) as i:
                    for j in range(1, 5):
                        n = 4 * i + j
                        gate_exp(n)
                        send_y(n - 1, (j + 1) % 2, 16 * (2 * i + (j - 1) // 2))
                        keep_h(n, j % 2)
                for n in range(NE - 3, NE):
                    gate_exp(n)
                    send_y(n - 1, (n - 1) % 2, 16 * ((n - 1) // 2))
                    keep_h(n, n % 2)
                send_y(NE - 1, 1, 16 * (NE // 2 - 1))
                for p in range(2):
                    act.wait_ge(y_sent[p], 16 * (NE // 2) + 16)
                n_over = act.value_load(over_i[0:1, 0:1], min_val=0, max_val=OVER)
                with act.If(n_over > 0):
                    with act.Fori(0, OVER // 4) as i:
                        for j in range(4):
                            with act.If(n_over > 4 * i + j):
                                n = NE + 4 * i + j
                                gate_exp(n)
                                keep_h(n, j % 2)
                                send_y(n, j % 2, 16 * (NE // 2 + 2 * i + j // 2))
                                act.wait_ge(y_sent[j % 2], 16 * (NE // 2 + 2 * i + j // 2 + 1) + 16)
                                act.sem_inc(turn, 1)
                stage_end(act, 10)
                for t in range(NT + 1):
                    m = P if t < NT else ND
                    act.wait_ge(row_moved[t % 4], 32 * ((NT - t % 4) // 4 + 1 + t // 4 + 1))
                    if t >= 2:
                        act.wait_ge(c_done, t - 1)
                    act.activation(comb[0:m, t % 2, :], yg[0:m, t % 4, 0, :], ACT.Copy, scale=gates[0:m, 0, t:t + 1]).then_inc(c_half, 1)
                stage_end(act, 11)
                end_layer(act, l)
            squares(x, sq, CH, NCH, D ** -0.5, sq_ready)
            roots(ps, rstd[:, 0, :], CH, NCH, 0, ssq_ready, std_ready)

        @block.vector
        def _(dve):
            step = Steps(dve, dve_step)
            dve.wait_ge(setup, 80)
            step(dve.tensor_copy(lmask[:, :, :], lmask_f))
            step.restart()
            with dve.Fori(0, DEPTH) as l:
                def norm(base, tiles, src, dst, g, r, width, count, ready, done):
                    for c in range(count):
                        tok = slice(c * width, (c + 1) * width)
                        dve.wait_ge(ready, base + c + 1)
                        step(dve.reciprocal(r[:, tok], r[:, tok]))
                        for k in range(tiles):
                            last = dve.scalar_tensor_tensor(out=dst[:, k, tok], in0=src[:, k, tok], scalar=gain(g, k),
                                                            in1=r[:, tok], op0=ALU.mult, op1=ALU.mult)
                        last.then_inc(done, 1)

                dve.wait_ge(vec_full, 16)
                norm(0, KT, x, xn, "g_mix", rstd[:, 0, :], CH, NCH, std_ready, norm_ready)
                dve.wait_ge(lin_evac, 2 + 2)
                dve.wait_ge(dbuf_full, 16)
                for k in range(2):
                    step.mark(dve.tensor_copy(dbuf[:, k, :, POOL_BUF:POOL_BUF + DT],
                                               pr[:, k, SEQ:TOK].rearrange("p (b t) -> p b t", b=DB)))
                u = pr[:, 0:2, :]
                a, b2 = psum_a, psum_b
                da, d2 = dsum[:, 0], dsum[:, 1]
                E = POOL_BUF + DT
                step.mark(dve.tensor_copy(a[:, :, 0:1], u[:, :, 0:1]))
                step(dve.tensor_tensor(a[:, :, 1:SEQ], u[:, :, 1:SEQ], u[:, :, 0:SEQ - 1], ALU.add))
                step.mark(dve.tensor_copy(b2[:, :, 0:2], a[:, :, 0:2]))
                step(dve.tensor_tensor(b2[:, :, 2:SEQ], a[:, :, 2:SEQ], a[:, :, 0:SEQ - 2], ALU.add))
                step.mark(dve.tensor_copy(a[:, 1, 0:4], b2[:, 1, 0:4]))
                step(dve.tensor_tensor(a[:, 1, 4:SEQ], b2[:, 1, 4:SEQ], b2[:, 1, 0:SEQ - 4], ALU.add))
                step.mark(dve.tensor_copy(b2[64:128, 1, 0:8], a[64:128, 1, 0:8]))
                step(dve.tensor_tensor(b2[64:128, 1, 8:SEQ], a[64:128, 1, 8:SEQ], a[64:128, 1, 0:SEQ - 8], ALU.add))
                for k in range(2):
                    step.mark(dve.tensor_tensor(da[:, k, :, 1:E], dbuf[:, k, :, 1:E], dbuf[:, k, :, 0:E - 1], ALU.add))
                step.sync()
                for k in range(2):
                    step.mark(dve.tensor_tensor(d2[:, k, :, 3:E], da[:, k, :, 3:E], da[:, k, :, 1:E - 2], ALU.add))
                step.sync()
                step(dve.tensor_tensor(da[:, 1, :, 7:E], d2[:, 1, :, 7:E], d2[:, 1, :, 3:E - 4], ALU.add))
                step(dve.tensor_tensor(d2[64:128, 1, :, 15:E], da[64:128, 1, :, 15:E], da[64:128, 1, :, 7:E - 8], ALU.add))
                groups = ((slice(0, 64), 0, a, da), (slice(64, 128), 0, b2, d2), (slice(0, 64), 1, a, da), (slice(64, 128), 1, b2, d2))
                fix = con("pool_fix").rearrange("p (k n) -> p k n", k=2)
                for rows, k, s_, _ in groups:
                    step.mark(dve.tensor_tensor(s_[rows, k, 0:16], s_[rows, k, 0:16], fix[rows, k, :], ALU.mult))
                step.sync()
                inv = con("pool_inv")
                fresh = [ds_[rows, k, :, POOL_BUF:E] for rows, k, _, ds_ in groups]
                for (rows, k, s_, _), f in zip(groups, fresh):
                    step.mark(dve.tensor_scalar(s_[rows, k, 0:SEQ], s_[rows, k, 0:SEQ], inv[rows, k:k + 1], None, ALU.mult))
                    step.mark(dve.tensor_scalar(f, f, inv[rows, k:k + 1], None, ALU.mult))
                step.sync()
                for (rows, k, s_, _), f in zip(groups, fresh):
                    step.mark(dve.tensor_tensor(a[rows, k, 0:SEQ], s_[rows, k, 0:SEQ], u[rows, k, 0:SEQ], ALU.subtract))
                    last = dve.tensor_tensor(a[rows, k, SEQ:TOK].rearrange("p (b t) -> p b t", b=DB), f,
                                              dbuf[rows, k, :, POOL_BUF:E], ALU.subtract)
                last.then_inc(pooled, 1)
                step.sync()
                dve.wait_ge(kswap_full, 32)
                step.mark(dve.tensor_tensor(kr[64:96, :], pr[64:96, 5, :], rope[64:96, 0, :], ALU.mult))
                step(dve.tensor_tensor(kswap[64:96, :], kswap[64:96, :], rope[64:96, 1, :], ALU.mult))
                dve.tensor_tensor(kr[64:96, :], kr[64:96, :], kswap[64:96, :], ALU.add).then_inc(kr_ready, 1)
                dve.wait_ge(lat_std, 1)
                step(dve.reciprocal(rstd[:, 0, :], rstd[:, 0, :]))
                dve.reciprocal(rstd[:, 1, :], rstd[:, 1, :]).then_inc(lat_norm, 1)
                dve.wait_ge(lat_norm, 1)
                for k in range(2):
                    step.mark(dve.scalar_tensor_tensor(out=pr[:, 2 + k, :], in0=pr[:, 2 + k, :], scalar=gain("g_qn", k),
                                                       in1=rstd[:, 0, :], op0=ALU.mult, op1=ALU.mult))
                dve.scalar_tensor_tensor(out=pr[:, 4, :], in0=pr[:, 4, :], scalar=gain("g_kvn"), in1=rstd[:, 1, :],
                                         op0=ALU.mult, op1=ALU.mult).then_inc(lat_norm, 1)
                dve.wait_ge(lat_norm, 2)
                dve.wait_ge(kr_ready, 1)
                step.mark(dve.tensor_copy(ckv_new, pr[:, 4, SEQ:TOK]))
                step.mark(dve.tensor_copy(kr_new[64:96, :], kr[64:96, SEQ:TOK]))
                for t in range(NT + 1):
                    m = P if t < NT else ND
                    s_, g_ = silu[0:m, t, :], vg[0:m, t, GW:512]
                    dve.wait_ge(gate_e, t + 1)
                    step(dve.tensor_scalar(s_, s_, 1.0, None, ALU.add))
                    step(dve.reciprocal(s_, s_))
                    dve.wait_ge(vg_evac, t + 1)
                    step.mark(dve.tensor_tensor(g_, g_, s_, ALU.mult))
                    if t == 4:
                        dve.wait_ge(z_evac, 2)
                        step(dve.scalar_tensor_tensor(out=la, in0=la, scalar=0.0, in1=la_t, op0=ALU.min, op1=ALU.subtract))
                        step(dve.tensor_scalar(la, la, 1.0 / 16.0, None, ALU.mult))
                step.sync()
                step.restart()
                stage_end(dve, 1)

                dve.sem_inc(y_free, 2)
                for p in range(2):
                    step.mark(dve.tensor_copy(k_h[64:96, p, :], kr[64:96, :]))
                step.sync()

                def max_of(qb, item):
                    dve.wait_ge(s_done, item + 1)
                    s = ps[:, 2 * (qb % 2):2 * (qb % 2) + 2, :].rearrange("p a n -> p (a n)")[:, 0:(qb + 1) * P]
                    step(dve.reduce_max(nmax[:, qb % 2, 0:1], s, AX))
                    dve.tensor_scalar(nmax[:, qb % 2, 1:2], nmax[:, qb % 2, 0:1], -MLA_SCALE, None, ALU.mult).then_inc(nmax_ready, 1)

                def piece(p, k, b, tp, h):
                    dve.wait_ge(tp_done, tp)
                    if k < 3:
                        tok = (slice(0, 512), slice(512, 1024), slice(SEQ, TOK))[k]
                        src, dst = ps[0:QK, 4 + b, 0:tok.stop - tok.start], q_h[0:QK, p, tok]
                        dve.tensor_copy(dst, src).then_inc(tp_free[b], 1)
                    elif k < 5:
                        tok = (slice(0, 512), slice(512, 1024))[k - 3]
                        dve.tensor_copy(k_h[0:NOPE, p, tok], ps[0:NOPE, 4 + b, :]).then_inc(tp_free[b], 1)
                    else:
                        dve.wait_ge(zeroed, 1)
                        dve.tensor_copy(q_dec[:, :, bass.ds(96 + DT * h, DT)],
                                        ps[:, 4 + b, 0:ND].rearrange("p (b t) -> p b t", b=DB)).then_inc(tp_free[b], 1)

                def q_pe(p, n, h):
                    dve.wait_ge(q_rope, n)
                    src = q_h[64:96, p, SEQ:TOK].rearrange("p (b t) -> p b t", b=DB)
                    for j in range(4):
                        step.mark(dve.tensor_copy(qpe_dec[32 * j:32 * j + 32, :, j, bass.ds(DT * h, DT)], src))
                    step.mark(dve.tensor_copy(qpe_new[64:96, :, bass.ds(DT * h, DT)], src))

                for k in range(6):
                    piece(0, k, k % 2, k + 1, 0)
                q_pe(0, 1, 0)
                step.sync()
                max_of(0, 0)
                max_of(1, 1)
                step.restart()
                with dve.Fori(0, H // 2) as i:
                    for p in range(2):
                        item = 16 * i + 8 * p
                        m = 0
                        for qb in range(NT):
                            m += 1 + (qb >= 4)
                            max_of((qb + 2) % NT, item + qb + 2)
                            if qb < 6:
                                piece(1 - p, qb, m % 2, 36 * i + 18 * p + 6 + m + 1, (2 * i + p + 1) % H)
                                m += 1
                            if qb == 6:
                                q_pe(1 - p, 2 * i + p + 2, (2 * i + p + 1) % H)
                            if qb % 4 == 3:
                                hf = qb // 4
                                dve.wait_ge(y_done, 4 * i + 2 * p + hf + 1 + 1)
                                dve.wait_ge(y_free, 4 * i + 2 * p + hf + 2)
                                step(dve.reciprocal(recip, ps[64:128, 6 + hf, :]))
                                dve.tensor_tensor(mix[64 * p:64 * p + 64, bass.ds(2 + i, 1), 512 * hf:512 * hf + 512]
                                                  .rearrange("p a n -> p (a n)"), ps[0:64, 6 + hf, :], recip,
                                                  ALU.mult).then_inc(y_free, 1)
                        step.sync()
                        step.restart()
                stage_end(dve, 2)

                hm = con("headmask").unsqueeze(2)
                bd = con("bdmask")

                def decays(p, w, lvs):
                    for lv in lvs:
                        z = LEVELS[lv]
                        e = g_e[:, p, lv, 0:w].rearrange("p (n z) -> p n z", z=2 * z)
                        b = g_b[:, p, 0:w].rearrange("p (n z) -> p n z", z=2 * z)
                        mid = b[:, :, z - 1:z].broadcast_to([P, w // (2 * z), z])
                        step.mark(dve.tensor_tensor(e[:, :, z:2 * z], b[:, :, z:2 * z], mid, ALU.subtract))
                        last = dve.tensor_tensor(e[:, :, 0:z], mid, b[:, :, 0:z], ALU.subtract)
                    return last

                def queries(p, w, lvs):
                    for lv in lvs:
                        last = dve.tensor_tensor(g_q[:, p, lv, :, 0:w], g_e[:, p, lv, 0:w].unsqueeze(1).broadcast_to([P, GH, w]),
                                                 g_q0[:, p, :, 0:w], ALU.mult)
                    last.then_inc(g_dve, 1)

                def begin(n, p, cols):
                    step(dve.tensor_tensor_scan(g_b[:, p, :], la[:, cols], la[:, cols], 0.0, ALU.add, ALU.bypass))
                    decays(p, P, range(NL - 1)).then_inc(g_sub, 1)

                def take_levels(n8, p, w, order):
                    for j, lv in enumerate(order):
                        dve.wait_ge(at_done, n8 + j + 1 + 1)
                        src = ps[0:w, j % 4, 0:GH * w].rearrange("p (h t) -> p h t", h=GH)
                        dst = g_att[0:w, p, :, 0:w]
                        if lv == NL - 1:
                            ins_ = dve.tensor_tensor(dst, src, ident[0:w, 0:w].unsqueeze(1).broadcast_to([w, GH, w]), ALU.mult)
                        else:
                            ins_ = dve.copy_predicated(dst, lmask[0:w, lv, 0:w].unsqueeze(1).broadcast_to([w, GH, w]), src)
                        ins_.then_inc(at_free, 1)
                        dve.wait_ge(at_free, n8 + j + 1 + 4)

                def norm_o(n, p, w, gate):
                    dve.wait_ge(o_evac, n + 2)
                    step(dve.tensor_tensor(g_sq[0:w, :], g_o[0:w, p, :], g_o[0:w, p, :], ALU.mult))
                    dve.tensor_reduce(g_ms[0:w, 0, :], g_sq[0:w, :].rearrange("p (h v) -> p h v", h=GH), AX, ALU.add).then_inc(o_sum, 1)
                    dve.wait_ge(o_root, n)
                    step(dve.reciprocal(g_ms[0:w, 1, :], g_ms[0:w, 1, :]))
                    step(dve.tensor_tensor(g_o[0:w, p, :].rearrange("p (h v) -> p h v", h=GH),
                                           g_o[0:w, p, :].rearrange("p (h v) -> p h v", h=GH),
                                           g_ms[0:w, 1, :].unsqueeze(2).broadcast_to([w, GH, GV]), ALU.mult))
                    dve.tensor_tensor(g_o[0:w, p, :], g_o[0:w, p, :], gate, ALU.mult).then_inc(o_norm, 1)

                dve.sem_inc(at_free, 4)
                dve.sem_inc(g_dve, 1)
                step.mark(dve.memset(g_e[:, :, NL - 1, :], 1.0))
                dve.memset(g_o[:, 1, :], 0.0).then_inc(o_norm, 1)
                dve.memset(state, 0.0).then_inc(st_ready, 1)
                begin(1, 0, slice(0, P))
                dve.wait_ge(g_exp, 1)
                dve.wait_ge(g_spread, 1)
                queries(0, P, range(DSPLIT, NL - 1))
                dve.wait_ge(g_pool, 1 + 1)
                step.sync()
                step.restart()
                with dve.Fori(0, NT // 2) as i:
                    for p in range(2):
                        n = 2 * i + p
                        nxt = bass.ds(((n + 1) % NT) * P, P)
                        dve.wait_ge(g_pool, n + 1)
                        begin(n + 2, 1 - p, nxt)
                        taken = 16 * i + 8 * p
                        for j, lv in enumerate([NL - 1] + list(range(NL - 1))):
                            dve.wait_ge(at_done, taken + j + 1 + 1)
                            dve.sem_inc(turn, 1)
                            src = ps[:, j % 4, :].rearrange("p (h t) -> p h t", h=GH)
                            if j == 0:
                                ins_ = dve.tensor_tensor(g_att[:, p], src, ident.unsqueeze(1).broadcast_to([P, GH, P]), ALU.mult)
                            else:
                                ins_ = dve.copy_predicated(g_att[:, p], lmask[:, lv, :].unsqueeze(1).broadcast_to([P, GH, P]), src)
                            ins_.then_inc(at_free, 1)
                            dve.wait_ge(at_free, taken + j + 1 + 4)
                            dve.sem_inc(turn, 1)
                            if j == 3:
                                dve.wait_ge(g_exp, n + 2)
                                dve.wait_ge(g_spread, n + 2)
                                queries(1 - p, P, range(DSPLIT, NL - 1))
                        dve.wait_ge(st_done, n + 1)
                        step(dve.tensor_tensor(g_tmp, ps[:, 7, 0:GW], bd, ALU.mult))
                        dve.scalar_tensor_tensor(out=state, in0=state, scalar=g_last[:, p, 0:1], in1=g_tmp,
                                                 op0=ALU.mult, op1=ALU.add).then_inc(st_ready, 1)
                        norm_o(n + 1, p, P, vg[:, bass.ds(n, 1), GW:512].rearrange("p a v -> p (a v)"))
                        step.sync()
                        step.restart()
                dve.wait_ge(g_pool, NT + 1 + 1)
                dve.wait_ge(st_ready, NT + 1)
                step(dve.tensor_copy(g_b[:, 0, 0:ND], la[:, SEQ:TOK]))
                b4 = g_b[:, 0, 0:ND].rearrange("p (b t) -> p b t", b=DB)
                for t in range(1, DT):
                    step(dve.tensor_tensor(b4[:, :, t:t + 1], b4[:, :, t:t + 1], b4[:, :, t - 1:t], ALU.add))
                step.mark(dve.tensor_tensor(g_ek[0][:, 0:ND].rearrange("p (b t) -> p b t", b=DB),
                                            b4[:, :, DT - 1:DT].broadcast_to([P, DB, DT]), b4, ALU.subtract))
                decays(0, ND, range(NL - 3, NL - 1)).then_inc(g_sub, 1)
                dve.wait_ge(g_exp, NT + 2)
                dve.wait_ge(at_done, NL * NT + 1)
                for lv in (NL - 3, NL - 2, NL - 1):
                    step.mark(dve.tensor_tensor(g_k[0][:, lv, 0:ND], g_e[:, 0, lv, 0:ND], pr[:, 7, SEQ:TOK], ALU.mult))
                step.mark(dve.tensor_tensor(g_kt[:, 0, 0:ND], g_ek[0][:, 0:ND], pr[:, 7, SEQ:TOK], ALU.mult))
                step(dve.tensor_tensor(g_qe[:, 0, 0:ND], pr[:, 6, SEQ:TOK], g_eb[0][:, 0:ND], ALU.mult))
                step.mark(dve.tensor_tensor(d_qe, g_qe[:, 0, 0:ND].unsqueeze(1).broadcast_to([P, DB, ND]),
                                            con("colbatch").rearrange("p (b t) -> p b t", b=DB), ALU.mult))
                step(dve.tensor_tensor(g_q0[:, 0, :, 0:ND], pr[:, 6, SEQ:TOK].unsqueeze(1).broadcast_to([P, GH, ND]),
                                       hm.broadcast_to([P, GH, ND]), ALU.mult))
                queries(0, ND, range(NL - 3, NL - 1))
                take_levels(NL * NT, 0, ND, [NL - 1, NL - 3, NL - 2])
                dve.wait_ge(kt_evac, NT + 1)
                dve.tensor_tensor(d_kt[0:ND], g_ktt[0:ND, 0, :].unsqueeze(1).broadcast_to([ND, DB, P]),
                                  con("rowbatch", ND).unsqueeze(2).broadcast_to([ND, DB, P]), ALU.mult).then_inc(dkt_ready, 1)
                norm_o(NT + 1, 0, ND, vg[0:ND, NT, GW:512])
                for b in range(DB):
                    dve.wait_ge(st_done, NT + b + 1)
                    dve.wait_ge(st_ready, NT + b + 1)
                    step(dve.tensor_tensor(g_tmp, ps[:, 7 - 2 * (b % 2), 0:GW], bd, ALU.mult))
                    dve.scalar_tensor_tensor(out=d_state[:, b, :], in0=d_state[:, b, :], scalar=g_last[:, 0, b:b + 1], in1=g_tmp,
                                             op0=ALU.mult, op1=ALU.add).then_inc(st_ready, 1)
                step.sync()
                step.restart()
                stage_end(dve, 3)

                dve.sem_inc(k4_evac, 1)
                dve.wait_ge(tok_done, 1)
                dve.tensor_copy(ckv_tok[0:ND, :], ps[0:ND, 3, 0:P]).then_inc(tok_evac, 1)

                def take_k4(n, g):
                    dve.wait_ge(k4_done, NGR * n + g + 1)
                    dve.tensor_copy(k4[:, g % 2, :], ps[:, 2, 0:P]).then_inc(k4_evac, 1)

                def blocks_of(n):
                    return ps[:, 4 + 2 * (n % 2):6 + 2 * (n % 2), :].rearrange("p a n -> p (a n)").rearrange("p (j q) -> p q j", q=ND)

                def maxima(n):
                    dve.wait_ge(sc_done, NGR * (n + 1))
                    dve.wait_ge(tail_pe, 5 * n + 1)
                    step.mark(dve.tensor_tensor(p_new[0:ND, :], ps[0:ND, 3, 0:ND],
                                                con("newmask", ND).rearrange("p (b q) -> p b q", b=DB)[:, n, :], ALU.add))
                    step(dve.tensor_reduce(mx, blocks_of(n), AX, ALU.max))
                    dve.tensor_tensor(mx[0:ND, :], mx[0:ND, :], p_new[0:ND, :], ALU.max).then_inc(tail_dve, 1)

                def diagonal(n):
                    dve.wait_ge(tail_pe, 5 * n + 2)
                    step(dve.reduce_max(small[0:ND, 0:1], ps[0:ND, 3, 0:P], AX))
                    dve.tensor_scalar(diag[0:ND, :], ident[0:ND, 0:ND], small[0:ND, 0:1], None, ALU.mult).then_inc(tail_dve, 1)

                def shift(n):
                    dve.wait_ge(tail_pe, 5 * n + 3)
                    step(dve.tensor_copy(mb, ps[:, 3, 0:ND]))
                    step.mark(dve.tensor_tensor(p_new[0:ND, :], p_new[0:ND, :], mb[0:ND, :], ALU.subtract))
                    dve.tensor_tensor(pd.rearrange("p j q -> p q j"), blocks_of(n), mb.unsqueeze(2).broadcast_to([P, ND, BLK]),
                                      ALU.subtract).then_inc(shifted, 1)

                def sums(n):
                    dve.wait_ge(pd_ready, n + 1)
                    step(dve.tensor_reduce(sm, pd.rearrange("p j q -> p q j"), AX, ALU.add))
                    dve.tensor_tensor(sm[0:ND, :], sm[0:ND, :], p_new[0:ND, :], ALU.add).then_inc(tail_dve, 1)

                def normalise(n):
                    dve.wait_ge(tail_pe, 5 * n + 4)
                    step(dve.reciprocal(small[0:ND, 1:2], ps[0:ND, 3, P:P + 1]))
                    dve.tensor_scalar(d_o[0:ND, :], ps[0:ND, 3, 0:P], small[0:ND, 1:2], None, ALU.mult).then_inc(tail_dve, 1)

                def keep_latent(n):
                    dve.wait_ge(tail_pe, 5 * n + 5)
                    dve.tensor_copy(o_lat[:, :, n, :], ps[:, 3, 0:ND].rearrange("p (h t) -> p h t", h=H)).then_inc(tail_dve, 1)
                    dve.wait_ge(tail_dve, 5 * n + 5)

                for n in range(DB):
                    for g in range(NGR):
                        take_k4(n, g)
                        if n >= 1:
                            if g == 1:
                                diagonal(n - 1)
                            if g == 2:
                                shift(n - 1)
                            if g == 3:
                                sums(n - 1)
                            if g == 5:
                                normalise(n - 1)
                            if g == 6:
                                keep_latent(n - 1)
                    maxima(n)
                for f in (diagonal, shift, sums, normalise, keep_latent):
                    f(DB - 1)
                step.sync()
                step.restart()
                stage_end(dve, 4)
                def add_linear(tiles, first, at=0):
                    for j in range(tiles):
                        dve.wait_ge(lin_done, first + j + 1)
                        xs = x[:, at + j, :].rearrange("p (c n) -> p c n", c=NCH)
                        dve.tensor_tensor(xs, xs, ps[:, (j % 2) * NCH:(j % 2 + 1) * NCH, 0:CH], ALU.add).then_inc(lin_evac, 1)

                add_linear(RING, IN_MT)
                dve.wait_ge(mstd_ready, 1)
                step(dve.reciprocal(mem_r, mem_r))
                for k in range(KT):
                    last = dve.scalar_tensor_tensor(out=mem_n[:, k, :], in0=mem[:, k, :], scalar=gain("g_mem", k), in1=mem_r,
                                                    op0=ALU.mult, op1=ALU.mult)
                last.then_inc(mnorm_ready, 1)
                add_linear(RING, IN_MT + RING, RING)
                stage_end(dve, 5)
                norm(NCH, KT, x, xn, "g_x", rstd[:, 0, :], CH, NCH, std_ready, norm_ready)
                dve.wait_ge(lin_evac, IN_MT + OUT_MT + XK_MT + 2)
                for j in range(XQ_MT):
                    dve.wait_ge(lin_done, IN_MT + OUT_MT + XK_MT + j + 1)
                    dve.tensor_copy(xq[:, j, 0:TOK].rearrange("p (c n) -> p c n", c=NCH),
                                    ps[:, (j % 2) * NCH:(j % 2 + 1) * NCH, 0:CH]).then_inc(lin_evac, 1)
                step.restart()
                stage_end(dve, 6)

                def x_max(n, p, w):
                    dve.wait_ge(xs_done, n)
                    step(dve.tensor_reduce(xm[0:w, p, 0:4], ps[0:w, 2 * p:2 * p + 2, :].rearrange("p a (h m) -> p (a h) m", h=2),
                                           AX, ALU.max))
                    dve.tensor_scalar(xm[0:w, p, 4:8], xm[0:w, p, 0:4], -X_SCALE, None, ALU.mult).then_inc(xm_ready, 1)

                def x_recip(n, p, w):
                    dve.wait_ge(xp_ready, n)
                    step.mark(dve.reciprocal(xm[0:w, p, 12:16], xm[0:w, p, 8:12]))

                def x_norm(n, p, w):
                    dve.wait_ge(xv_done, n)
                    step.sync()
                    dve.tensor_tensor(xon[0:w, p], ps[0:w, 6, :].rearrange("p (h v) -> p h v", h=XH),
                                      xm[0:w, p, 12:16].unsqueeze(2).broadcast_to([w, XH, XHD]), ALU.mult).then_inc(xon_ready, 1)

                def x_keep(n, w, dst):
                    dve.wait_ge(xot_done, n)
                    dve.tensor_copy(dst, ps[:, 7, 0:XH * w].rearrange("p (h t) -> p h t", h=XH)).then_inc(xot_evac, 1)

                def x_tile(n, p, before=True, ahead=True):
                    x_recip(n, p, P)
                    if ahead:
                        step.sync()
                        x_max(n + 2, p, P)
                    x_norm(n, p, P)
                    if before:
                        x_keep(n - 1, P, co[:, :, bass.ds(P * (n - 2), P)])
                    step.restart()

                x_max(1, 0, P)
                x_max(2, 1, P)
                x_tile(1, 0, before=False)
                x_tile(2, 1)
                with dve.Fori(0, (NT - 4) // 2) as i:
                    for p in range(2):
                        x_tile(2 * i + p + 3, p)
                x_tile(NT - 1, 0, ahead=False)
                x_recip(NT, 1, P)
                x_max(NT + 1, 0, ND)
                x_keep(NT - 1, P, co[:, :, SEQ - 2 * P:SEQ - P])
                x_norm(NT, 1, P)
                x_keep(NT, P, co[:, :, SEQ - P:SEQ])
                x_recip(NT + 1, 0, ND)
                for c in range(2 * XH):
                    if c == 0:
                        dve.wait_ge(dt_done, 1)
                    last = dve.tensor_tensor(d_pt[:, c], ps[:, 4, c * ND:(c + 1) * ND].unsqueeze(1).broadcast_to([P, DB, ND]),
                                             con("colbatch").rearrange("p (b t) -> p b t", b=DB), ALU.mult)
                last.then_inc(dpt_ready, 1)
                x_norm(NT + 1, 0, ND)
                x_keep(NT + 1, ND, co[:, :, SEQ:TOK])
                step.restart()
                stage_end(dve, 7)
                add_linear(KT, IN_MT + OUT_MT + XK_MT + XQ_MT)
                stage_end(dve, 8)
                dve.memset(lgt[0:NR, TOK:NXQ], 0.0).then_inc(lg_evac, 1)
                norm(2 * NCH, KT, x, xn, "g_ffn", rstd[:, 0, :], CH, NCH, std_ready, norm_ready)
                dve.wait_ge(lt_done, 1)
                step(dve.tensor_copy(lg, ps[:, 3, 0:(NT + 1) * NR].rearrange("p (t e) -> p t e", e=NR)))

                def wide(a, n):
                    return a.unsqueeze(2).broadcast_to([P, NT + 1, n])

                def every(a):
                    return a.unsqueeze(1).broadcast_to([P, NT + 1, a.shape[1]])

                def first_of_max(v, n, m, onehot):
                    step(dve.tensor_reduce(m, v, AX, ALU.max))
                    step(dve.tensor_tensor(onehot, v, wide(m, n), ALU.is_equal))
                    tmp = r_tmp[:, :, 0:n]
                    step(dve.tensor_tensor(tmp, onehot, every(con("iota32")[:, 0:n]), ALU.mult))
                    step(dve.tensor_reduce(r_min, tmp, AX, ALU.min))
                    step(dve.tensor_tensor(onehot, tmp, wide(r_min, n), ALU.is_equal))

                first_of_max(lg[:, :, 0:NG], NG, gm, g_oh)
                step(dve.tensor_tensor(r_exp[:, :, 0:NG], lg[:, :, 0:NG], wide(gm, NG), ALU.subtract))
                step(dve.tensor_scalar(g_oh, g_oh, 1.0, -NEG, ALU.subtract, ALU.mult))
                for g in range(NG):
                    step.mark(dve.tensor_tensor(e_all[:, :, g * EPG:(g + 1) * EPG], lg[:, :, NG + g * EPG:NG + (g + 1) * EPG],
                                                g_oh[:, :, g:g + 1].broadcast_to([P, NT + 1, EPG]), ALU.add))
                step.sync()
                first_of_max(e_all, NE, m1, oh1)
                step(dve.scalar_tensor_tensor(out=e_all, in0=oh1, scalar=NEG, in1=e_all, op0=ALU.mult, op1=ALU.add))
                first_of_max(e_all, NE, m2, oh2)
                dve.tensor_tensor(r_exp[:, :, NG:NG + 1], m2.unsqueeze(2), m1.unsqueeze(2), ALU.subtract).then_inc(rx_in, 1)
                for oh in (oh1, oh2):
                    step.mark(dve.memset(oh[32:64, NT, :], 0.0))
                    step.mark(dve.memset(oh[64:128, NT, :], 0.0))
                step.sync()
                dve.tensor_tensor(both, oh1, oh2, ALU.add).then_inc(both_ready, 1)
                dve.wait_ge(rx_out, 1)
                step.mark(dve.tensor_reduce(g_w, r_exp[:, :, 0:NG], AX, ALU.add))
                step(dve.tensor_scalar(m1, r_exp[:, :, NG], 1.0, None, ALU.add))
                step(dve.tensor_tensor(g_w, g_w, m1, ALU.mult))
                step(dve.reciprocal(gates[:, 0, :], g_w))
                step(dve.tensor_tensor(gates[:, 1, :], gates[:, 0, :], r_exp[:, :, NG], ALU.mult))
                step.mark(dve.memset(cum[:, 0, :], 0.0))
                dve.wait_ge(ranked, 1)
                step.sync()
                for t in range(NT + 1):
                    step(dve.tensor_tensor(cum[:, t + 1, :], cum[:, t, :], ps[:, 5, t * NE:(t + 1) * NE], ALU.add))
                step(dve.tensor_tensor(rank, ps[:, 4, 0:(NT + 1) * NE].rearrange("p (t e) -> p t e", e=NE), cum[:, 0:NT + 1, :], ALU.add))
                step(dve.tensor_tensor(steps8, cum[:, NT + 1, :].unsqueeze(2).broadcast_to([P, NE, 8]),
                                       con("steps128").unsqueeze(1).broadcast_to([P, NE, 8]), ALU.is_gt))
                step(dve.tensor_reduce(nov, steps8, AX, ALU.add))
                step(dve.tensor_tensor_scan(oend, nov, nov, 0.0, ALU.add, ALU.bypass))
                step.mark(dve.tensor_scalar(base, con("iota32"), float(CAP), float(CAP * NE), ALU.mult, ALU.add))
                step(dve.tensor_tensor(jump, oend, nov, ALU.subtract))
                step(dve.tensor_tensor(jump, jump, con("iota32"), ALU.subtract))
                step(dve.tensor_scalar(jump, jump, float(CAP), float(-CAP), ALU.mult, ALU.add))
                step(dve.tensor_scalar(r_tmp, rank, float(CAP), None, ALU.is_ge))
                step(dve.tensor_tensor(r_tmp, r_tmp, every(jump), ALU.mult))
                step(dve.tensor_tensor(rank, rank, r_tmp, ALU.add))
                step(dve.tensor_tensor(rank, rank, every(base), ALU.add))
                for s_, oh in enumerate((oh1, oh2)):
                    step(dve.tensor_tensor(oh, oh, rank, ALU.mult))
                    step(dve.tensor_reduce(r_f[:, s_, :], oh, AX, ALU.add))
                step.mark(dve.tensor_copy(dest[:, :, :], r_f))
                step(dve.tensor_tensor(over_f, oend.unsqueeze(1).broadcast_to([P, OVER, NE]),
                                       con("over").unsqueeze(2).broadcast_to([P, OVER, NE]), ALU.is_le))
                step.mark(dve.tensor_copy(over_c[:, 0:1], oend[:, NE - 1:NE]))
                step(dve.tensor_reduce(over_c[:, 1:1 + OVER], over_f, AX, ALU.add))
                step(dve.tensor_scalar(over_c[:, 1:1 + OVER], over_c[:, 1:1 + OVER], float(NE - 1), None, ALU.min))
                dve.tensor_copy(over_i[:, :], over_c).then_inc(routed, 1)
                step.restart()
                stage_end(dve, 9)

                def take_x(n, p):
                    dve.wait_ge(tx_done, n + 1)
                    dve.tensor_copy(xb_t[:, p].rearrange("p (a k) t -> p a (k t)", a=2), ps[:, 0:2, :]).then_inc(tx_evac, 1)

                def hidden(n):
                    dve.wait_ge(ge_ready, n + 1)
                    step(dve.tensor_scalar(h_e, h_e, 1.0, None, ALU.add))
                    step(dve.reciprocal(h_e, h_e))
                    step(dve.tensor_tensor(h_e, ps[:, 2, 0:DE], h_e, ALU.mult))
                    dve.tensor_tensor(h_b, ps[:, 2, DE:2 * DE], h_e, ALU.mult).then_inc(h_ready, 1)
                    step.restart()

                take_x(0, 0)
                hidden(0)
                take_x(1, 1)
                with dve.Fori(0, NE // 4 - 1) as i:
                    for j in range(1, 5):
                        hidden(4 * i + j)
                        take_x(4 * i + j + 1, (j + 1) % 2)
                for n in range(NE - 3, NE):
                    hidden(n)
                    if n < NE - 1:
                        take_x(n + 1, (n + 1) % 2)
                n_over = dve.value_load(over_i[0:1, 0:1], min_val=0, max_val=OVER)
                with dve.If(n_over > 0):
                    with dve.Fori(0, OVER // 4) as i:
                        for j in range(4):
                            with dve.If(n_over > 4 * i + j):
                                take_x(NE + 4 * i + j, j % 2)
                                hidden(NE + 4 * i + j)
                stage_end(dve, 10)
                for t in range(NT + 2):
                    if t <= NT:
                        m = P if t < NT else ND
                        dve.wait_ge(c_half, t + 1)
                        dve.scalar_tensor_tensor(out=comb[0:m, t % 2, :], in0=yg[0:m, t % 4, 1, :], scalar=gates[0:m, 1, t:t + 1],
                                                 in1=comb[0:m, t % 2, :], op0=ALU.mult, op1=ALU.add).then_inc(c_ready, 1)
                    if t >= 1:
                        u = t - 1
                        m = P if u < NT else ND
                        dve.wait_ge(c_done, u + 1)
                        xs = x[:, :, u * P:u * P + m]
                        for f in range(2):
                            xs = x[:, 4 * f:4 * f + 4, u * P:u * P + m]
                            last = dve.tensor_tensor(xs, xs, ps[:, 2 * (u % 2) + f, 0:4 * m].rearrange("p (k t) -> p k t", k=4), ALU.add)
                        last.then_inc(c_added, 1)
                stage_end(dve, 11)
                end_layer(dve, l)
            for c, tok in chunks:
                dve.wait_ge(std_ready, c + 1)
                step(dve.reciprocal(rstd[:, 0, tok], rstd[:, 0, tok]))
                for k in range(KT):
                    last = dve.scalar_tensor_tensor(out=xn[:, k, tok], in0=x[:, k, tok], scalar=gain("g_final", k),
                                                    in1=rstd[:, 0, tok], op0=ALU.mult, op1=ALU.mult)
                last.then_inc(norm_ready, 1)

        @block.gpsimd
        def _(pool):
            step = Steps(pool, pool_step)
            pool.wait_ge(setup, 80)
            step(pool.tensor_copy(page_f[:, :], pages[:, :]))
            step(pool.tensor_scalar(page_f[:, :], page_f[:, :], float(PAGE // KROW), None, ALU.mult))
            step(pool.tensor_tensor(page_f[:, :], page_f[:, :], con("pmod").broadcast_to([P, DB]), ALU.add))
            step.restart()
            step(pool.memset(zeros, 0.0))
            step.restart()
            pool.dma_start(slots.rearrange("(p n) (f c) -> p (n f) c", p=P, c=512),
                           zeros.unsqueeze(1).broadcast_to([P, NBLK * CAP // P * 2, 512])).then_inc(slots_clear, 16)
            with pool.Fori(0, DEPTH) as l:
                stage_end(pool, 1)

                step.mark(pool.memset(q_dec[:, :, :], 0.0))
                step.mark(pool.memset(qpe_dec[:, :, :, :], 0.0))
                pool.memset(v_h[:, :, :, 64:128], 1.0).then_inc(zeroed, 1)

                def copy_v(p, h):
                    step(pool.tensor_copy(v_h[:, p, 0:4, 0:64], vv[0][:, :, bass.ds(VD * h, VD)]))
                    pool.tensor_copy(v_h[:, p, 4:8, 0:64], vv[1][:, :, bass.ds(VD * h, VD)]).then_inc(v_ready, 1)

                def rope_q(p, n):
                    pool.wait_ge(v_ready, n)
                    pool.wait_ge(qswap_full, 32 * n)
                    step(pool.tensor_tensor(q_h[64:96, p, :], q_h[64:96, p, :], rope[64:96, 0, :], ALU.mult))
                    step(pool.tensor_tensor(qswap[64:96, :], qswap[64:96, :], rope[64:96, 1, :], ALU.mult))
                    pool.tensor_tensor(q_h[64:96, p, :], q_h[64:96, p, :], qswap[64:96, :], ALU.add).then_inc(q_rope, 1)

                pool.wait_ge(zeroed, 1)
                copy_v(0, 0)
                rope_q(0, 1)
                step.restart()
                with pool.Fori(0, H // 2) as i:
                    for p in range(2):
                        pool.wait_ge(y_done, 4 * i + 2 * p + 1)
                        pool.wait_ge(q_rope, 2 * i + p + 1)
                        copy_v(1 - p, (2 * i + p + 1) % H)
                        rope_q(1 - p, 2 * i + p + 2)
                        step.restart()
                stage_end(pool, 2)

                pool.sem_inc(g_pool, 1)
                scale_mask = con("headmask").unsqueeze(2).broadcast_to([P, GH, P])

                def prepare(n, p, cols):
                    q, k = pr[:, 6, cols], pr[:, 7, cols]
                    pool.tensor_tensor(g_q0[:, p], q.unsqueeze(1).broadcast_to([P, GH, P]), scale_mask, ALU.mult).then_inc(g_spread, 1)
                    pool.wait_ge(g_exp, n)
                    pool.wait_ge(g_spread, n)
                    for lv in range(DSPLIT):
                        step(pool.tensor_tensor(g_q[:, p, lv], g_e[:, p, lv, :].unsqueeze(1).broadcast_to([P, GH, P]), g_q0[:, p], ALU.mult))
                    step(pool.tensor_tensor(g_k[p], g_e[:, p], k.unsqueeze(1).broadcast_to([P, NL, P]), ALU.mult))
                    step(pool.tensor_tensor(g_kt[:, p, :], g_ek[p], k, ALU.mult))
                    pool.tensor_tensor(g_qe[:, p, :], g_eb[p], q, ALU.mult).then_inc(g_pool, 1)

                prepare(1, 0, slice(0, P))
                step.restart()
                with pool.Fori(0, NT // 2) as i:
                    for p in range(2):
                        n = 2 * i + p
                        pool.wait_ge(g_pool, n + 1 + 1)
                        pool.wait_ge(at_done, 16 * i + 8 * p + 1)
                        pool.wait_ge(o_done, n + 1)
                        prepare(n + 2, 1 - p, bass.ds(((n + 1) % NT) * P, P))
                        step.restart()
                pool.wait_ge(at_done, NL * NT + 1)
                pool.wait_ge(g_dve, NT + 1 + 1)
                pool.wait_ge(g_pool, NT + 1 + 1)
                pool.memset(d_state, 0.0).then_inc(ds_clear, 1)
                stage_end(pool, 3)

                step(pool.tensor_copy(page_i[:, :], page_f[:, :]))
                for n in range(DB):
                    if n >= NSLOT:
                        pool.wait_ge(tail_pe, 5 * (n - NSLOT) + 4)
                    for dst, cache in ((ck[n % NSLOT], "cache_ckv"), (kr_c[n % NSLOT], "cache_kpe")):
                        pool.indirect_dma_start(dst.rearrange("p j c -> p (j c)"), None,
                                                ins[cache].rearrange("l n (q k) c -> (l n q) (k c)", k=KROW),
                                                bass.IndirectOffsetOnAxis(ap=page_i[:, n:n + 1], axis=0)).then_inc(ck_full[n % NSLOT], 16)
                for j in range(NSLOT):
                    pool.wait_ge(ck_full[j], 32 * (DB // NSLOT))
                step(pool.tensor_scalar(page_f[:, :], page_f[:, :], float(NPHYS * PAGE // KROW), None, ALU.add))
                step.restart()
                stage_end(pool, 4)
                stage_end(pool, 5)
                stage_end(pool, 6)
                for p in range(2):
                    pool.tensor_copy(qt[:, p], xq[:, :, p * P:(p + 1) * P]).then_inc(qt_ready, 1)
                with pool.Fori(0, (NT - 2) // 2) as i:
                    for p in range(2):
                        n = 2 * i + p
                        pool.wait_ge(qt_ready, n + 2)
                        pool.wait_ge(xs_done, n + 1)
                        pool.tensor_copy(qt[:, p], xq[:, :, bass.ds(P * (n + 2), P)]).then_inc(qt_ready, 1)
                pool.wait_ge(qt_ready, NT)
                for h in range(XH):
                    step(pool.tensor_tensor(d_qm[:, h], xq[:, h, SEQ:TOK].unsqueeze(1).broadcast_to([P, DB, ND]),
                                            con("colbatch").rearrange("p (b t) -> p b t", b=DB), ALU.mult))
                pool.sem_inc(qt_ready, 1)
                step.restart()
                stage_end(pool, 7)
                stage_end(pool, 8)
                pool.wait_ge(slots_clear, 16)
                pool.wait_ge(routed, 1)
                for t in range(NT + 1):
                    m = P if t < NT else ND
                    pool.wait_ge(xr_evac, t + 1)
                    for s_ in range(2):
                        pool.indirect_dma_start(slots, bass.IndirectOffsetOnAxis(ap=dest[0:m, s_, t:t + 1], axis=0),
                                                xr[0:m, t % 4, :], None).then_inc(row_moved[t % 4], 16)
                for j in range(4):
                    pool.wait_ge(row_moved[j], 32 * ((NT - j) // 4 + 1))
                pool.sem_inc(rows_ready, 1)
                stage_end(pool, 9)
                stage_end(pool, 10)
                for t in range(NT + 1):
                    m = P if t < NT else ND
                    if t >= 4:
                        pool.wait_ge(c_ready, t - 3)
                    for s_ in range(2):
                        pool.indirect_dma_start(yg[0:m, t % 4, s_, :], None, slots,
                                                bass.IndirectOffsetOnAxis(ap=dest[0:m, s_, t:t + 1], axis=0)).then_inc(row_moved[t % 4], 16)
                stage_end(pool, 11)
                end_layer(pool, l, clears=True)


_INS = ("x", "ring", "wvg", "wpool", "wgk", "wuv", "w_h", "vec", "consts", "rope", "lmask", "pool_prev", "pool_old", "state_gla", "pages", "cache_ckv", "cache_kpe", "mem", "wxv", "mem_k", "mem_v", "w_r", "w_e")
_OUTS = (("y", (P, KT, TOK)), ("ckv", (DEPTH, P, TOK)), ("kpe", (DEPTH, ROPE, TOK)), ("pool_p", (DEPTH, POOL_BUF, GW)),
         ("pool_s", (DEPTH, DB, POOL_BUF, GW)), ("gla_p", (DEPTH, GH, GK, GV)), ("gla_s", (DEPTH, DB, GH, GK, GV)),
         ("mk", (DEPTH, P, XH, NMEM)), ("mv", (DEPTH, P, 2, XH * XHD)))


def layout(i):
    L = DEPTH
    f = {n: np.asarray(a) for n, a in i.items()}
    o = {}

    def tiles(w, m=P):
        l_, k_, m_ = w.shape
        return w.reshape(l_, k_ // P, P, m_ // m, m).transpose(0, 3, 2, 1, 4)

    xs = np.concatenate([f["x_prompt"].reshape(SEQ, D), f["x_sample"].reshape(ND, D)])
    o["x"] = xs.T.reshape(KT, P, TOK).transpose(1, 0, 2)
    w = f["w_in"]
    at = np.cumsum([0, 256, 256, 128, ROPE, 128, 128, GW, 16, GW])
    u, cq, ckv, kpe, gq, gk, gv, ga, go = (w[:, :, a:b] for a, b in zip(at[:-1], at[1:]))
    z = np.zeros((L, D, 48), w.dtype)
    mixed = np.concatenate([ga, z, kpe, z[:, :, :32]], 2)
    w_a = np.concatenate([u, cq, ckv, mixed, gq, gk], 2)
    xo = tiles(f["w_xo"]).reshape(L, 4, 2, P, 4, P).transpose(0, 1, 3, 2, 4, 5).reshape(L, 4, P, KT, P)
    o["ring"] = np.concatenate([tiles(w_a), tiles(f["w_out"]), tiles(f["w_xk"]), tiles(f["w_xq"]), xo], 1)
    o["wvg"] = tiles(np.concatenate([gv, go], 2), 512)[:, 0]
    wp = np.zeros((L, P, 2, P), w.dtype)
    for g in range(4):
        r = slice(64 * (g % 2), 64 * (g % 2) + 64)
        wp[:, r, g // 2, r] = f["w_pool"][:, g]
    o["wpool"] = wp
    o["wgk"] = f["w_gk2"]
    o["wuv"] = f["w_uv"].reshape(L, P, H * VD)
    wh = np.zeros((L, H + 2, P, 384), w.dtype)
    uq = f["w_uq"].reshape(L, 2, P, H, QK).transpose(0, 3, 2, 1, 4)
    wh[:, :H, :, 0:192] = uq.reshape(L, H, P, 192)
    wh[:, :H, :, 192:256] = f["w_uk"].transpose(0, 2, 1, 3)
    wh[:, :H, 0:NOPE, 256:384] = f["w_uk"].transpose(0, 2, 3, 1)
    wh[:, H:] = wh[:, 0:2]
    o["w_h"] = wh
    v = np.zeros((L, P, NVEC), w.dtype)

    def put(name, a):
        at, n = _v[name]
        a = np.broadcast_to(a.reshape(-1, a.shape[-1]), (L, a.shape[-1]))
        v[:, :, at:at + n] = a.reshape(L, n, P).transpose(0, 2, 1)

    for n in ("g_mix", "g_x", "g_ffn", "g_mem", "g_qn", "g_kvn", "b_gk", "pool_scale", "g_final"):
        put(n, f[n])
    put("g_gla", np.concatenate([f["g_gla"], f["g_gla"]], 1))
    put("b_r", np.concatenate([f["b_rg"], f["b_re"], np.zeros((L, P - NG - NE), w.dtype)], 1))
    o["vec"] = v
    o["consts"], o["rope"], o["lmask"] = constants()
    o["pool_prev"] = f["state_pool"].reshape(L, DB, POOL_BUF, 2, P).transpose(0, 4, 3, 1, 2)
    o["pool_old"] = f["state_pool"]
    o["state_gla"] = f["state_gla"]
    o["pages"] = np.repeat(f["page_table"].T, P // PAGES, axis=0)
    o["cache_ckv"], o["cache_kpe"] = f["cache_ckv"], f["cache_kpe"]
    o["mem"] = f["mem_prompt"][0].T.reshape(KT, P, NMEM).transpose(1, 0, 2)
    o["wxv"] = tiles(f["w_xv"], 512)[:, 0]
    o["mem_k"] = f["cache_mem_k"].transpose(0, 1, 4, 3, 2)
    o["mem_v"] = f["cache_mem_v"]
    o["w_r"] = np.concatenate([f["w_rg"], f["w_re"]], 2).reshape(L, KT, P, NR).transpose(0, 2, 1, 3)
    gu = np.concatenate([f["w_eg"], f["w_eu"]], 3).reshape(L, NE, KT, P, 2 * DE).transpose(0, 1, 3, 2, 4).reshape(L, NE, P, -1)
    o["w_e"] = np.concatenate([gu, f["w_ed"].reshape(L, NE, 2, P, D).transpose(0, 1, 3, 2, 4).reshape(L, NE, P, -1)], 3)
    return {n: np.ascontiguousarray(a) for n, a in o.items()}


def kernel(**inputs):
    import concourse.bacc as bacc
    from concourse.bass_utils import run_bass_kernel_spmd

    nc = bacc.Bacc("TRN2", target_bir_lowering=False, num_devices=1)
    arrays, ins, outs = {}, {}, {}
    for name, a in layout(inputs).items():
        arrays["in_" + name] = a
        ins[name] = nc.dram_tensor("in_" + name, a.shape, mybir.dt.from_np(a.dtype), kind="ExternalInput").ap()
    for name, shape in _OUTS:
        outs[name] = nc.dram_tensor("out_" + name, shape, F32, kind="ExternalOutput").ap()
    build(nc, ins, outs)
    r = run_bass_kernel_spmd(nc, [arrays], core_ids=[0]).results[0]
    o = {name: np.asarray(r["out_" + name]) for name, _ in _OUTS}
    y = o["y"].transpose(2, 1, 0).reshape(TOK, D)
    ckv, kpe = o["ckv"].transpose(0, 2, 1), o["kpe"].transpose(0, 2, 1)
    mk = o["mk"].transpose(0, 3, 2, 1).reshape(DEPTH, 1, NMEM, XH, XHD)
    mv = o["mv"].transpose(0, 2, 1, 3).reshape(DEPTH, 1, NMEM, XH, XHD)
    got = (y[:SEQ].reshape(1, SEQ, D), y[SEQ:].reshape(DB, DT, D),
           ckv[:, :SEQ].reshape(DEPTH, 1, SEQ, P), kpe[:, :SEQ].reshape(DEPTH, 1, SEQ, ROPE),
           o["pool_p"].reshape(DEPTH, 1, POOL_BUF, GW), o["gla_p"].reshape(DEPTH, 1, GH, GK, GV), mk, mv,
           ckv[:, SEQ:].reshape(DEPTH, DB, DT, P), kpe[:, SEQ:].reshape(DEPTH, DB, DT, ROPE), o["pool_s"], o["gla_s"])
    return tuple(np.ascontiguousarray(a) for a in got)
```
